# Optimizing a Trainium2 kernel written in Bass

```python
import math
import jax
import jax.numpy as jnp
from jax import lax
import numpy as np

D_MODEL = 1024
BATCH = 1
SEQ = 512
DEPTH = 1
DEC_BATCH = 8
DEC_SEQ = 1
PAST_LEN = 256
PAGE_SIZE = 128

SSD_EXPAND = 2
D_INNER = SSD_EXPAND * D_MODEL
SSD_HEAD_DIM = 64
SSD_HEADS = D_INNER // SSD_HEAD_DIM
SSD_GROUPS = 4
SSD_HPG = SSD_HEADS // SSD_GROUPS
SSD_STATE = 128
SSD_CONV = 4
SSD_CONV_DIM = D_INNER + 2 * SSD_GROUPS * SSD_STATE
SSD_CHUNK = 128
NSA_HEADS = 16
NSA_KV_HEADS = 4
NSA_GQ = NSA_HEADS // NSA_KV_HEADS
NSA_HEAD_DIM = 64
CMP_LEN = 32
CMP_STRIDE = 16
CMP_RATIO = CMP_LEN // CMP_STRIDE
CMP_HIDDEN = 2 * NSA_HEAD_DIM
SEL_BLOCK = 64
SEL_TOPN = 16
SEL_FORCE = 1.0e4
WINDOW = 512
QUERY_BLOCK = 128
MEM_TOKENS = 256
MEM_HEADS = 4
MEM_HEAD_DIM = 256
D_FF = 2816
FFN_CONV = 3
ROPE_THETA = 10000.0
EPS = 1e-6
N_BRANCH = 3
IN_SIZES = (D_INNER, SSD_CONV_DIM, SSD_HEADS, NSA_HEADS * NSA_HEAD_DIM,
            6 * NSA_KV_HEADS * NSA_HEAD_DIM, 3 * NSA_HEADS, MEM_HEADS * MEM_HEAD_DIM,
            N_BRANCH * D_MODEL)
D_IN_PROJ = sum(IN_SIZES)

kernel_name = 'hybrid_ssd_nsa_memory_convffn_step'

def rmsnorm(x, g):
    xf = x.astype(jnp.float32)
    y = xf * lax.rsqrt(jnp.mean(xf * xf, axis=-1, keepdims=True) + EPS)
    return (y * g.astype(jnp.float32)).astype(x.dtype)

def rope(x, pos):
    half = x.shape[-1] // 2
    inv = ROPE_THETA ** (-jnp.arange(half, dtype=jnp.float32) / half)
    ang = pos.astype(jnp.float32)[:, None] * inv[None, :]
    cos = jnp.cos(ang)[None, :, None, :]
    sin = jnp.sin(ang)[None, :, None, :]
    xf = x.astype(jnp.float32)
    x1, x2 = xf[..., :half], xf[..., half:]
    return jnp.concatenate([x1 * cos - x2 * sin, x2 * cos + x1 * sin], axis=-1).astype(x.dtype)

def masked_softmax(s, mask):
    s = jnp.where(mask, s.astype(jnp.float32), -jnp.inf)
    m = jnp.max(s, axis=-1, keepdims=True)
    m = jnp.where(jnp.isfinite(m), m, 0.0)
    p = jnp.exp(s - m)
    den = jnp.sum(p, axis=-1, keepdims=True)
    return p / jnp.where(den > 0, den, 1.0)

def causal_dwconv(u, prev, w, bias):
    width, length = w.shape[0], u.shape[1]
    up = jnp.concatenate([prev.astype(u.dtype), u], axis=1)
    out = bias + w[0] * up[:, :length]
    for k in range(1, width):
        out = out + w[k] * up[:, k:k + length]
    return out, up[:, length:]

def ssd_scan(xh, dt, a, bm, cm, h0):
    b, length = xh.shape[:2]
    q = min(SSD_CHUNK, length)
    pad = (-length) % q
    if pad:
        padf = lambda t: jnp.pad(t, [(0, 0), (0, pad)] + [(0, 0)] * (t.ndim - 2))
        xh, dt, bm, cm = padf(xh), padf(dt), padf(bm), padf(cm)
    nc = (length + pad) // q
    chunk = lambda t: t.reshape((b, nc, q) + t.shape[2:])
    xh, dt, bm, cm = chunk(xh), chunk(dt), chunk(bm), chunk(cm)
    cum = jnp.cumsum(dt * a, axis=2)
    cum_t = jnp.moveaxis(cum, 2, -1)
    seg = cum_t[..., :, None] - cum_t[..., None, :]
    causal = jnp.tril(jnp.ones((q, q), dtype=bool))
    decay = jnp.exp(jnp.where(causal, seg, -jnp.inf))
    cb = jnp.einsum('bcign,bcjgn->bcgij', cm, bm)
    xdt = xh * dt[..., None]
    y_diag = jnp.einsum('bcgeij,bcjgep->bcigep', cb[:, :, :, None] * decay, xdt)
    decay_end = jnp.exp(cum[:, :, -1:] - cum)
    states = jnp.einsum('bcjgn,bcjgep->bcgepn', bm, xdt * decay_end[..., None])
    chunk_decay = jnp.exp(cum[:, :, -1])

    def step(h, inp):
        dec, st = inp
        return dec[..., None, None] * h + st, h

    h_last, h_prev = lax.scan(step, h0, (jnp.moveaxis(chunk_decay, 1, 0), jnp.moveaxis(states, 1, 0)))
    h_prev = jnp.moveaxis(h_prev, 0, 1)
    y_off = jnp.einsum('bcign,bcgepn->bcigep', cm, h_prev) * jnp.exp(cum)[..., None]
    y = (y_diag + y_off).reshape((b, nc * q) + xh.shape[3:])[:, :length]
    return y, h_last

def compress(rows, pe, w1, w2):
    b, t = rows.shape[:2]
    n_chunk = t // CMP_STRIDE
    n_cmp = n_chunk - CMP_RATIO + 1
    chunks = rows[:, :n_chunk * CMP_STRIDE].reshape(b, n_chunk, CMP_STRIDE, NSA_KV_HEADS, NSA_HEAD_DIM)
    w1r = w1.reshape(CMP_LEN, NSA_HEAD_DIM, CMP_HIDDEN)
    hid = jnp.einsum('ld,ldm->m', pe, w1r)
    for r in range(CMP_RATIO):
        hid = hid + jnp.einsum('bcskd,sdm->bckm', chunks[:, r:r + n_cmp],
                               w1r[r * CMP_STRIDE:(r + 1) * CMP_STRIDE])
    return jax.nn.silu(hid) @ w2

def nsa_attend(q, gates, q_pos0, kc, vc, ks, vs, kw, vw, kw_pos0):
    b, lq = q.shape[:2]
    qb_len = min(QUERY_BLOCK, lq)
    nb = lq // qb_len
    scale = NSA_HEAD_DIM ** -0.5
    nc = kc.shape[1]
    kc_end = jnp.arange(nc, dtype=jnp.int32) * CMP_STRIDE + (CMP_LEN - 1)
    t_s = ks.shape[1]
    ns = -(-t_s // SEL_BLOCK)
    padn = ns * SEL_BLOCK - t_s
    to_blocks = lambda t: jnp.pad(t, ((0, 0), (0, padn), (0, 0), (0, 0))).reshape(
        b, ns, SEL_BLOCK, NSA_KV_HEADS, NSA_HEAD_DIM).transpose(0, 3, 1, 2, 4)
    ks_b, vs_b = to_blocks(ks), to_blocks(vs)
    k_top = min(SEL_TOPN, ns)
    ci = np.arange(nc)[:, None] * CMP_STRIDE
    sj = np.arange(ns)[None, :] * SEL_BLOCK
    overlap = jnp.asarray(((ci <= sj + SEL_BLOCK - 1) & (ci + CMP_LEN - 1 >= sj)).astype(np.float32))
    span = WINDOW + qb_len
    padw = lambda t: jnp.pad(t, ((0, 0), (WINDOW, 0), (0, 0), (0, 0)))
    kw_p, vw_p = padw(kw), padw(vw)
    gather = jax.vmap(jax.vmap(lambda tab, ix: tab[ix]))
    jb = jnp.arange(ns, dtype=jnp.int32)

    def block(args):
        qb, gb, qs = args
        t = q_pos0 + qs + jnp.arange(qb_len, dtype=jnp.int32)
        s_c = jnp.einsum('bqkgd,bnkd->bkgqn', qb, kc) * scale
        p_c = masked_softmax(s_c, kc_end[None, :] <= t[:, None])
        o_c = jnp.einsum('bkgqn,bnkd->bqkgd', p_c.astype(vc.dtype), vc)
        imp = jnp.einsum('bkgqn,nj->bqkj', p_c, overlap)
        cur = (t // SEL_BLOCK)[:, None]
        forced = ((jb == 0) | (jb == cur) | (jb == cur - 1))[:, None, :]
        valid = (jb * SEL_BLOCK <= t[:, None])[:, None, :]
        score = jnp.where(valid, imp + SEL_FORCE * forced.astype(jnp.float32), -jnp.inf)
        _, idx = lax.top_k(score, k_top)
        idx = idx.transpose(0, 2, 1, 3)
        k_sel = gather(ks_b, idx).reshape(b, NSA_KV_HEADS, qb_len, k_top * SEL_BLOCK, NSA_HEAD_DIM)
        v_sel = gather(vs_b, idx).reshape(b, NSA_KV_HEADS, qb_len, k_top * SEL_BLOCK, NSA_HEAD_DIM)
        pos_s = (idx[..., None] * SEL_BLOCK + jnp.arange(SEL_BLOCK, dtype=jnp.int32)).reshape(
            b, NSA_KV_HEADS, qb_len, k_top * SEL_BLOCK)
        s_s = jnp.einsum('bqkgd,bkqmd->bkgqm', qb, k_sel) * scale
        p_s = masked_softmax(s_s, (pos_s <= t[:, None])[:, :, None])
        o_s = jnp.einsum('bkgqm,bkqmd->bqkgd', p_s.astype(v_sel.dtype), v_sel)
        start = q_pos0 + qs - kw_pos0
        k_win = lax.dynamic_slice_in_dim(kw_p, start, span, axis=1)
        v_win = lax.dynamic_slice_in_dim(vw_p, start, span, axis=1)
        pos_w = q_pos0 + qs - WINDOW + jnp.arange(span, dtype=jnp.int32)
        mask_w = (pos_w[None, :] <= t[:, None]) & (pos_w[None, :] >= t[:, None] - WINDOW) & (pos_w[None, :] >= 0)
        s_w = jnp.einsum('bqkgd,bskd->bkgqs', qb, k_win) * scale
        p_w = masked_softmax(s_w, mask_w)
        o_w = jnp.einsum('bkgqs,bskd->bqkgd', p_w.astype(v_win.dtype), v_win)
        return gb[..., 0:1] * o_c + gb[..., 1:2] * o_s + gb[..., 2:3] * o_w

    q_blocks = jnp.moveaxis(q.reshape((b, nb, qb_len) + q.shape[2:]), 1, 0)
    g_blocks = jnp.moveaxis(gates.reshape((b, nb, qb_len) + gates.shape[2:]), 1, 0)
    starts = jnp.arange(nb, dtype=jnp.int32) * qb_len
    out = lax.map(block, (q_blocks, g_blocks, starts))
    return jnp.moveaxis(out, 0, 1).reshape(b, lq, NSA_HEADS * NSA_HEAD_DIM)

def memory_kv(mem, norm, w_kv, k_norm):
    b, m, _ = mem.shape
    kv = rmsnorm(mem, norm) @ w_kv
    mk, mv = jnp.split(kv, 2, axis=-1)
    mk = rmsnorm(mk.reshape(b, m, MEM_HEADS, MEM_HEAD_DIM), k_norm)
    return mk, mv.reshape(b, m, MEM_HEADS, MEM_HEAD_DIM)

def hybrid_layer(x, pos0, past, mem_k, mem_v, w):
    (cmp_k_past, cmp_v_past, sel_k_past, sel_v_past, win_k_buf, win_v_buf,
     ssd_conv_prev, ssd_h0, ffn_conv_prev) = past
    b, length, _ = x.shape
    pos = pos0 + jnp.arange(length, dtype=jnp.int32)
    h = rmsnorm(x, w['norm_mix'])
    proj = h @ w['w_in']
    splits = np.cumsum(IN_SIZES)[:-1].tolist()
    z, xbc, dt_raw, q, kv, g_nsa, q_mem, g_merge = jnp.split(proj, splits, axis=-1)

    xbc, ssd_conv_new = causal_dwconv(xbc, ssd_conv_prev, w['ssd_conv_w'], w['ssd_conv_b'])
    xbc = jax.nn.silu(xbc).astype(jnp.float32)
    xs, bm, cm = jnp.split(xbc, [D_INNER, D_INNER + SSD_GROUPS * SSD_STATE], axis=-1)
    xh = xs.reshape(b, length, SSD_GROUPS, SSD_HPG, SSD_HEAD_DIM)
    bm = bm.reshape(b, length, SSD_GROUPS, SSD_STATE)
    cm = cm.reshape(b, length, SSD_GROUPS, SSD_STATE)
    dt = jax.nn.softplus(dt_raw.astype(jnp.float32) + w['ssd_dt_bias'].astype(jnp.float32))
    dt = dt.reshape(b, length, SSD_GROUPS, SSD_HPG)
    a = -jnp.exp(w['ssd_a_log'].astype(jnp.float32)).reshape(SSD_GROUPS, SSD_HPG)
    h0 = ssd_h0.astype(jnp.float32).reshape(b, SSD_GROUPS, SSD_HPG, SSD_HEAD_DIM, SSD_STATE)
    y, h_last = ssd_scan(xh, dt, a, bm, cm, h0)
    y = y + w['ssd_d'].astype(jnp.float32).reshape(SSD_GROUPS, SSD_HPG)[..., None] * xh
    y = y.reshape(b, length, D_INNER).astype(x.dtype)
    o_ssd = rmsnorm(y * jax.nn.silu(z), w['ssd_norm']) @ w['w_ssd_o']
    ssd_state_new = h_last.reshape(b, SSD_HEADS, SSD_HEAD_DIM, SSD_STATE)

    q = rope(rmsnorm(q.reshape(b, length, NSA_HEADS, NSA_HEAD_DIM), w['nsa_q_norm']), pos)
    q = q.reshape(b, length, NSA_KV_HEADS, NSA_GQ, NSA_HEAD_DIM)
    ck, cv, sk, sv, wk, wv = [t.reshape(b, length, NSA_KV_HEADS, NSA_HEAD_DIM) for t in jnp.split(kv, 6, axis=-1)]
    sk = rope(rmsnorm(sk, w['nsa_k_norm'][1]), pos)
    wk = rope(rmsnorm(wk, w['nsa_k_norm'][2]), pos)
    ck_all = jnp.concatenate([cmp_k_past.astype(ck.dtype), ck], axis=1)
    cv_all = jnp.concatenate([cmp_v_past.astype(cv.dtype), cv], axis=1)
    sk_all = jnp.concatenate([sel_k_past.astype(sk.dtype), sk], axis=1)
    sv_all = jnp.concatenate([sel_v_past.astype(sv.dtype), sv], axis=1)
    kc = compress(ck_all, w['cmp_k_pe'], w['cmp_k_w1'], w['cmp_k_w2'])
    kc_pos = jnp.arange(kc.shape[1], dtype=jnp.int32) * CMP_STRIDE + (CMP_LEN - 1)
    kc = rope(rmsnorm(kc, w['nsa_k_norm'][0]), kc_pos)
    vc = compress(cv_all, w['cmp_v_pe'], w['cmp_v_w1'], w['cmp_v_w2'])
    kw_all = jnp.concatenate([win_k_buf.astype(wk.dtype), wk], axis=1)
    vw_all = jnp.concatenate([win_v_buf.astype(wv.dtype), wv], axis=1)
    kw_pos0 = pos0 - win_k_buf.shape[1]
    gates = jax.nn.sigmoid(g_nsa).reshape(b, length, NSA_KV_HEADS, NSA_GQ, 3)
    o_nsa = nsa_attend(q, gates, pos0, kc, vc, sk_all, sv_all, kw_all, vw_all, kw_pos0) @ w['w_nsa_o']
    keep = min(WINDOW, kw_all.shape[1])
    win_k_new, win_v_new = kw_all[:, -keep:], vw_all[:, -keep:]

    qm = rmsnorm(q_mem.reshape(b, length, MEM_HEADS, MEM_HEAD_DIM), w['mem_q_norm'])
    s_m = jnp.einsum('bqhd,bmhd->bhqm', qm, mem_k.astype(qm.dtype)) * (MEM_HEAD_DIM ** -0.5)
    p_m = jax.nn.softmax(s_m.astype(jnp.float32), axis=-1)
    o_mem = jnp.einsum('bhqm,bmhd->bqhd', p_m.astype(x.dtype), mem_v.astype(x.dtype))
    o_mem = o_mem.reshape(b, length, MEM_HEADS * MEM_HEAD_DIM) @ w['w_mem_o']

    gm = jax.nn.sigmoid(g_merge.reshape(b, length, N_BRANCH, D_MODEL) + w['b_merge'])
    mixed = gm[:, :, 0] * o_ssd + gm[:, :, 1] * o_nsa + gm[:, :, 2] * o_mem
    x = x + mixed @ w['w_out']

    u = rmsnorm(x, w['norm_ffn']) @ w['w_up']
    u, ffn_conv_new = causal_dwconv(u, ffn_conv_prev, w['ffn_conv_w'], w['ffn_conv_b'])
    x = x + (jax.nn.silu(u[..., :D_FF]) * u[..., D_FF:]) @ w['w_down']
    return x, (ck, cv, sk, sv, win_k_new, win_v_new, ssd_conv_new, ssd_state_new, ffn_conv_new)

def setup_inputs(seed: int = 0) -> dict:
    key = jax.random.key(seed)
    keys = iter(jax.random.split(key, 64))
    f32 = jnp.float32

    def nrm(shape, scale=1.0):
        return jax.random.normal(next(keys), shape, f32) * scale

    def gain(shape):
        return 1.0 + 0.05 * nrm(shape)

    L = (DEPTH,)
    n_pages = PAST_LEN // PAGE_SIZE
    n_pool = -(-(DEC_BATCH * n_pages * 5) // 4)
    kvr = (NSA_KV_HEADS, NSA_HEAD_DIM)
    wbuf = min(WINDOW, PAST_LEN)
    perm = jax.random.permutation(next(keys), n_pool)[:DEC_BATCH * n_pages]
    page_table = perm.reshape(DEC_BATCH, n_pages).astype(jnp.int32)
    dt0 = jnp.exp(jax.random.uniform(next(keys), L + (SSD_HEADS,), f32, math.log(1e-3), math.log(1e-1)))
    dt_bias = dt0 + jnp.log(-jnp.expm1(-dt0))
    a_log = jnp.log(jax.random.uniform(next(keys), L + (SSD_HEADS,), f32, 1.0, 16.0))
    return {
        'x_prompt': nrm((BATCH, SEQ, D_MODEL)),
        'x_sample': nrm((DEC_BATCH, DEC_SEQ, D_MODEL)),
        'cache_nsa_cmp_k': nrm(L + (n_pool, PAGE_SIZE) + kvr),
        'cache_nsa_cmp_v': nrm(L + (n_pool, PAGE_SIZE) + kvr),
        'cache_nsa_sel_k': nrm(L + (n_pool, PAGE_SIZE) + kvr),
        'cache_nsa_sel_v': nrm(L + (n_pool, PAGE_SIZE) + kvr),
        'state_nsa_win_k': nrm(L + (DEC_BATCH, wbuf) + kvr),
        'state_nsa_win_v': nrm(L + (DEC_BATCH, wbuf) + kvr),
        'state_ssd_conv': nrm(L + (DEC_BATCH, SSD_CONV - 1, SSD_CONV_DIM)),
        'state_ssd': nrm(L + (DEC_BATCH, SSD_HEADS, SSD_HEAD_DIM, SSD_STATE), 0.1),
        'cache_mem_k': nrm(L + (DEC_BATCH, MEM_TOKENS, MEM_HEADS, MEM_HEAD_DIM)),
        'cache_mem_v': nrm(L + (DEC_BATCH, MEM_TOKENS, MEM_HEADS, MEM_HEAD_DIM)),
        'state_ffn_conv': nrm(L + (DEC_BATCH, FFN_CONV - 1, 2 * D_FF)),
        'page_table': page_table,
        'mem_prompt': nrm((BATCH, MEM_TOKENS, D_MODEL)),
        'norm_mix': gain(L + (D_MODEL,)),
        'w_in': nrm(L + (D_MODEL, D_IN_PROJ), D_MODEL ** -0.5),
        'b_merge': nrm(L + (N_BRANCH, D_MODEL), 0.1),
        'ssd_conv_w': nrm(L + (SSD_CONV, SSD_CONV_DIM), SSD_CONV ** -0.5),
        'ssd_conv_b': nrm(L + (SSD_CONV_DIM,), 0.02),
        'ssd_dt_bias': dt_bias,
        'ssd_a_log': a_log,
        'ssd_d': 1.0 + 0.1 * nrm(L + (SSD_HEADS,)),
        'ssd_norm': gain(L + (D_INNER,)),
        'w_ssd_o': nrm(L + (D_INNER, D_MODEL), D_INNER ** -0.5),
        'nsa_q_norm': gain(L + (NSA_HEAD_DIM,)),
        'nsa_k_norm': gain(L + (3, NSA_HEAD_DIM)),
        'cmp_k_pe': nrm(L + (CMP_LEN, NSA_HEAD_DIM), 0.02),
        'cmp_k_w1': nrm(L + (CMP_LEN * NSA_HEAD_DIM, CMP_HIDDEN), (CMP_LEN * NSA_HEAD_DIM) ** -0.5),
        'cmp_k_w2': nrm(L + (CMP_HIDDEN, NSA_HEAD_DIM), CMP_HIDDEN ** -0.5),
        'cmp_v_pe': nrm(L + (CMP_LEN, NSA_HEAD_DIM), 0.02),
        'cmp_v_w1': nrm(L + (CMP_LEN * NSA_HEAD_DIM, CMP_HIDDEN), (CMP_LEN * NSA_HEAD_DIM) ** -0.5),
        'cmp_v_w2': nrm(L + (CMP_HIDDEN, NSA_HEAD_DIM), CMP_HIDDEN ** -0.5),
        'w_nsa_o': nrm(L + (NSA_HEADS * NSA_HEAD_DIM, D_MODEL), (NSA_HEADS * NSA_HEAD_DIM) ** -0.5),
        'mem_norm': gain(L + (D_MODEL,)),
        'w_mem_kv': nrm(L + (D_MODEL, 2 * MEM_HEADS * MEM_HEAD_DIM), D_MODEL ** -0.5),
        'mem_q_norm': gain(L + (MEM_HEAD_DIM,)),
        'mem_k_norm': gain(L + (MEM_HEAD_DIM,)),
        'w_mem_o': nrm(L + (MEM_HEADS * MEM_HEAD_DIM, D_MODEL), (MEM_HEADS * MEM_HEAD_DIM) ** -0.5),
        'w_out': nrm(L + (D_MODEL, D_MODEL), D_MODEL ** -0.5),
        'norm_ffn': gain(L + (D_MODEL,)),
        'w_up': nrm(L + (D_MODEL, 2 * D_FF), D_MODEL ** -0.5),
        'ffn_conv_w': nrm(L + (FFN_CONV, 2 * D_FF), FFN_CONV ** -0.5),
        'ffn_conv_b': nrm(L + (2 * D_FF,), 0.02),
        'w_down': nrm(L + (D_FF, D_MODEL), D_FF ** -0.5),
    }

def reference(x_prompt, x_sample, cache_nsa_cmp_k, cache_nsa_cmp_v, cache_nsa_sel_k, cache_nsa_sel_v,
              state_nsa_win_k, state_nsa_win_v, state_ssd_conv, state_ssd, cache_mem_k, cache_mem_v,
              state_ffn_conv, page_table, mem_prompt, norm_mix, w_in, b_merge, ssd_conv_w, ssd_conv_b,
              ssd_dt_bias, ssd_a_log, ssd_d, ssd_norm, w_ssd_o, nsa_q_norm, nsa_k_norm, cmp_k_pe,
              cmp_k_w1, cmp_k_w2, cmp_v_pe, cmp_v_w1, cmp_v_w2, w_nsa_o, mem_norm, w_mem_kv,
              mem_q_norm, mem_k_norm, w_mem_o, w_out, norm_ffn, w_up, ffn_conv_w, ffn_conv_b, w_down):
    weights = dict(norm_mix=norm_mix, w_in=w_in, b_merge=b_merge, ssd_conv_w=ssd_conv_w,
                   ssd_conv_b=ssd_conv_b, ssd_dt_bias=ssd_dt_bias, ssd_a_log=ssd_a_log, ssd_d=ssd_d,
                   ssd_norm=ssd_norm, w_ssd_o=w_ssd_o, nsa_q_norm=nsa_q_norm, nsa_k_norm=nsa_k_norm,
                   cmp_k_pe=cmp_k_pe, cmp_k_w1=cmp_k_w1, cmp_k_w2=cmp_k_w2, cmp_v_pe=cmp_v_pe,
                   cmp_v_w1=cmp_v_w1, cmp_v_w2=cmp_v_w2, w_nsa_o=w_nsa_o, mem_norm=mem_norm,
                   w_mem_kv=w_mem_kv, mem_q_norm=mem_q_norm, mem_k_norm=mem_k_norm, w_mem_o=w_mem_o,
                   w_out=w_out, norm_ffn=norm_ffn, w_up=w_up, ffn_conv_w=ffn_conv_w,
                   ffn_conv_b=ffn_conv_b, w_down=w_down)
    bp, bs = x_prompt.shape[0], x_sample.shape[0]
    past_len = page_table.shape[1] * cache_nsa_cmp_k.shape[2]

    def pages(pool):
        return pool[page_table].reshape((bs, past_len) + pool.shape[2:])

    kv_empty = jnp.zeros((bp, 0, NSA_KV_HEADS, NSA_HEAD_DIM), x_prompt.dtype)
    y_p, y_s = x_prompt, x_sample
    out_p, out_s = [], []
    for layer in range(DEPTH):
        w = {name: arr[layer] for name, arr in weights.items()}
        mem_k, mem_v = memory_kv(mem_prompt, w['mem_norm'], w['w_mem_kv'], w['mem_k_norm'])
        past_p = (kv_empty, kv_empty, kv_empty, kv_empty, kv_empty, kv_empty,
                  jnp.zeros((bp, SSD_CONV - 1, SSD_CONV_DIM), x_prompt.dtype),
                  jnp.zeros((bp, SSD_HEADS, SSD_HEAD_DIM, SSD_STATE), jnp.float32),
                  jnp.zeros((bp, FFN_CONV - 1, 2 * D_FF), x_prompt.dtype))
        y_p, st_p = hybrid_layer(y_p, 0, past_p, mem_k, mem_v, w)
        out_p.append(st_p + (mem_k, mem_v))
        past_s = (pages(cache_nsa_cmp_k[layer]), pages(cache_nsa_cmp_v[layer]),
                  pages(cache_nsa_sel_k[layer]), pages(cache_nsa_sel_v[layer]),
                  state_nsa_win_k[layer], state_nsa_win_v[layer], state_ssd_conv[layer],
                  state_ssd[layer], state_ffn_conv[layer])
        y_s, st_s = hybrid_layer(y_s, past_len, past_s, cache_mem_k[layer], cache_mem_v[layer], w)
        out_s.append(st_s)
    (p_cmp_k, p_cmp_v, p_sel_k, p_sel_v, p_win_k, p_win_v, p_ssd_conv, p_ssd, p_ffn_conv,
     p_mem_k, p_mem_v) = [jnp.stack(s) for s in zip(*out_p)]
    (s_cmp_k, s_cmp_v, s_sel_k, s_sel_v, s_win_k, s_win_v, s_ssd_conv, s_ssd,
     s_ffn_conv) = [jnp.stack(s) for s in zip(*out_s)]
    return (y_p, y_s, p_cmp_k, p_cmp_v, p_sel_k, p_sel_v, p_win_k, p_win_v, p_ssd_conv, p_ssd,
            p_ffn_conv, p_mem_k, p_mem_v, s_cmp_k, s_cmp_v, s_sel_k, s_sel_v, s_win_k, s_win_v,
            s_ssd_conv, s_ssd, s_ffn_conv)


_drawn_inputs = setup_inputs


def setup_inputs(seed=0):
    import zlib

    import numpy as np

    out = dict(_drawn_inputs(seed))
    spreads = {}
    factors = {'cache_nsa_sel_k': 2.916,
     'b_merge': 2.723,
     'nsa_q_norm': 8.0,
     'cmp_k_pe': 8.0,
     'cmp_v_pe': 8.0,
     'mem_q_norm': 8.0,
     'ffn_conv_b': 4.301}
    for name, (base, spread) in spreads.items():
        noise = np.random.default_rng([zlib.crc32(name.encode()), seed]).standard_normal(out[name].shape)
        drawn = base * np.exp(spread * noise) if base else spread * noise
        out[name] = jnp.asarray(drawn.astype(out[name].dtype))
    for name, factor in factors.items():
        out[name] = (out[name] * factor).astype(out[name].dtype)
    return out
```

```python
from contextlib import ExitStack

import numpy as np

import concourse.bass as bass
from concourse import mybir

F32 = mybir.dt.float32
I32 = mybir.dt.int32
ACT = mybir.ActivationFunctionType
ALU = mybir.AluOpType
AX_X = mybir.AxisListType.X

P = 128
D_MODEL = 1024
SEQ = 512
DEC = 8
COLS = SEQ + DEC
PAST = 256
PAGE = 128
PAGES = PAST // PAGE
KC = D_MODEL // P
TT = SEQ // P
D_INNER = 2048
DI = D_INNER // P
SSD_HEADS = 32
GROUPS = 4
HPG = SSD_HEADS // GROUPS
HEAD_P = 64
STATE = 128
CONV = 4
XBC = (D_INNER + 2 * GROUPS * STATE) // P
HEADS = 16
KV = 4
GQ = HEADS // KV
HD = 64
CMP_LEN = 32
CMP_STRIDE = 16
NCP = SEQ // CMP_STRIDE - 1
NCS = PAST // CMP_STRIDE - 1
MEM = 256
MEM_HEADS = 4
D_FF = 2816
FC = D_FF // P
FCONV = 3
EPS = 1e-6
NEG = -1.0e30
FLOOR = -1.0e20
ROWS = DEC * HEADS
DIAG = P + HEADS

PROMPT = slice(0, SEQ)
SAMPLE = slice(SEQ, COLS)


class Order:

    def __init__(self, eng, sem):
        self.eng, self.sem, self.base, self.n = eng, sem, 0, 0

    def __call__(self, instruction):
        instruction.then_inc(self.sem, 1)
        self.n += 1

    def settle(self):
        self.eng.wait_ge(self.sem, self.base + self.n)

    def enter(self, i, per):
        self.start, self.per = self.base + self.n, per
        self.base, self.n = self.start + i * per, 0

    def leave(self, turns):
        assert self.n == self.per, (self.n, self.per)
        self.base, self.n = self.start + turns * self.per, 0


class Stage:

    taken = []

    def __init__(self, nc, ctx):
        self.nc, self.ctx = nc, ctx

    def sb(self, name, shape, dt=F32):
        return self.ctx.enter_context(self.nc.sbuf_tensor(name, shape, dt))

    def ps(self, name, shape):
        return self.ctx.enter_context(self.nc.psum_tensor(name, shape, F32))

    def sem(self, name):
        sem = self.nc.alloc_semaphore(name)
        Stage.taken.append(sem)
        return sem

    @staticmethod
    def retire_semaphores(nc):
        nc.clear_and_free_semaphores(Stage.taken)
        Stage.taken.clear()
        nc.all_engine_barrier()


def at(t, k):
    if len(t.shape) == 2:
        return t[:, bass.ds(k, 1)]
    if len(t.shape) == 3:
        return t[:, bass.ds(k, 1), :].rearrange("p a n -> p (a n)")
    return t[:, bass.ds(k, 1), :, :].rearrange("p a m n -> p (a m) n")


def stream_weights(sp, w_dram, ring, landed, used, tiles, slots):
    for u in range(slots):
        sp.dma_start(ring[:, u], w_dram[u]).then_inc(landed[u], 16)
    if tiles > slots:
        with sp.Fori(0, tiles // slots - 1) as i:
            for u in range(slots):
                sp.wait_ge(used, i * slots + u + 1)
                sp.dma_start(ring[:, u], w_dram[bass.ds(i * slots + (slots + u), 1)].rearrange(
                    "a p k m -> (a p) k m")).then_inc(landed[u], 16)


def multiply_tiles(pe, ring, landed, evacuated, done, tiles, slots, sums):
    with pe.Fori(0, tiles // slots) as i:
        for u in range(slots):
            pe.wait_ge(landed[u], 16 * (i + 1))
            pe.wait_ge(evacuated, i * slots + (u + 1))
            for out, chunks, rhs in sums:
                for n, kk in enumerate(chunks):
                    last = pe.matmul(out(u % 2), ring[:, u, kk], rhs(n), start=n == 0, stop=n == len(chunks) - 1)
            last.then_inc(done, 1)


def load_constants(nc, d, c):
    with ExitStack() as ctx:
        s = Stage(nc, ctx)
        loaded = s.sem("consts_loaded")
        block = ctx.enter_context(nc.Block())
        names = [n for n in c if n in d]

        @block.sync
        def _(sp):
            for n in names:
                sp.dma_start(c[n][:], d[n]).then_inc(loaded, 16)
            sp.wait_ge(loaded, 16 * len(names))


def norm_columns(nc, name, src, dst, gain, ones, eps, chunks, parts, width):
    with ExitStack() as ctx:
        s = Stage(nc, ctx)
        sq = s.sb(name + "_sq", [P, 2, width])
        r = s.sb(name + "_r", [P, width])
        total = s.ps(name + "_total", [P, 2, 512])
        squared, summed, scaled = s.sem(name + "_squared"), s.sem(name + "_summed"), s.sem(name + "_scaled")
        act_order = s.sem(name + "_act")
        block = ctx.enter_context(nc.Block())

        @block.scalar
        def _(act):
            act.preload_act_table_set("natural_log_exp_and_others")
            for k in range(chunks):
                if k >= 2:
                    act.wait_ge(summed, k - 1)
                act.activation(sq[:, k % 2, :], src[:, k, :], ACT.Square).then_inc(squared, 1)
            act.wait_ge(summed, chunks)
            o = Order(act, act_order)
            for n, part in enumerate(parts):
                w = part.stop - part.start
                o(act.activation(r[:, part], total[:, n, 0:w], ACT.Ln, scale=1.0 / (chunks * P), bias=eps[:, 0:1]))
            o.settle()
            act.activation(r[:, :], r[:, :], ACT.Exp, scale=-0.5).then_inc(scaled, 1)

        @block.tensor
        def _(pe):
            for k in range(chunks):
                pe.wait_ge(squared, k + 1)
                for n, part in enumerate(parts):
                    w = part.stop - part.start
                    mm = pe.matmul(total[:, n, 0:w], ones[:, :], sq[:, k % 2, part], start=k == 0,
                                   stop=k == chunks - 1)
                mm.then_inc(summed, 1)

        @block.vector
        def _(dve):
            dve.wait_ge(scaled, 1)
            for k in range(chunks):
                dve.scalar_tensor_tensor(out=dst[:, k, :], in0=src[:, k, :], scalar=gain[:, k:k + 1], in1=r[:, :],
                                         op0=ALU.mult, op1=ALU.mult)


def project_ssd(nc, d, c, h, zt, xbct, dt_raw):
    slots, nz = 4, DI
    tiles = nz + XBC
    with ExitStack() as ctx:
        s = Stage(nc, ctx)
        ring = s.sb("ssd_ring", [P, slots, KC, P])
        wdt = s.sb("ssd_wdt", [P, KC, SSD_HEADS])
        pad = s.sb("ssd_pad", [P, 2, CONV - 1 + SEQ])
        acc = s.sb("ssd_acc", [P, 2, SEQ])
        prod = s.sb("ssd_prod", [P, 2, DEC, CONV])
        acc_s = s.sb("ssd_acc_s", [P, 2, DEC])
        tails = s.sb("ssd_tails", [P, XBC, CONV - 1])
        conv_s = s.sb("ssd_conv_s", [P, XBC, DEC, CONV])
        pp = s.ps("ssd_pp", [P, 2, 512])
        psm = s.ps("ssd_ps", [P, 2, 512])
        pdt = s.ps("ssd_pdt", [P, 2, 512])
        landed = [s.sem(f"ssd_w_landed{u}") for u in range(slots)]
        dt_landed, state_landed = s.sem("ssd_dt_landed"), s.sem("ssd_state_landed")
        done, evacuated, convolved = s.sem("ssd_tile_done"), s.sem("ssd_evacuated"), s.sem("ssd_convolved")
        dt_done, dve_order, stored, silu_done = (s.sem("ssd_dt_done"), s.sem("ssd_dve"), s.sem("ssd_stored"),
                                                 s.sem("ssd_silu_done"))
        block = ctx.enter_context(nc.Block())

        @block.sync
        def _(sp):
            sp.dma_start(wdt[:], d["w_dt"]).then_inc(dt_landed, 16)
            sp.dma_start(conv_s[:], d["ssd_state_conv"]).then_inc(state_landed, 16)
            stream_weights(sp, d["w_zxbc"], ring, landed, done, tiles, slots)
            sp.wait_ge(silu_done, XBC)
            sp.dma_start(d["out_p_conv"], tails[:]).then_inc(stored, 16)
            sp.dma_start(d["out_s_conv"], conv_s[:]).then_inc(stored, 16)
            sp.wait_ge(stored, 32)

        @block.tensor
        def _(pe):
            pe.wait_ge(dt_landed, 16)
            for n, part in enumerate((PROMPT, SAMPLE)):
                for k in range(KC):
                    mm = pe.matmul(pdt[0:SSD_HEADS, n, 0:part.stop - part.start], wdt[:, k], h[:, k, part],
                                   start=k == 0, stop=k == KC - 1)
            mm.then_inc(dt_done, 1)
            multiply_tiles(pe, ring, landed, evacuated, done, tiles, slots, [
                (lambda b: pp[:, b, :], range(KC), lambda k: h[:, k, PROMPT]),
                (lambda b: psm[:, b, 0:DEC], range(KC), lambda k: h[:, k, SAMPLE])])

        @block.scalar
        def _(act):
            act.preload_act_table(ACT.Silu)
            with act.Fori(0, nz // 2) as i:
                for u in range(2):
                    t = i * 2 + u
                    act.wait_ge(done, t + 1)
                    act.activation(at(zt, t)[:, PROMPT], pp[:, u, :], ACT.Silu)
                    act.activation(at(zt, t)[:, SAMPLE], psm[:, u, 0:DEC], ACT.Silu).then_inc(evacuated, 1)
            act.wait_ge(state_landed, 16)
            with act.Fori(0, XBC // 2) as i:
                for u in range(2):
                    t = i * 2 + u
                    act.wait_ge(done, t + (nz + 1))
                    act.wait_ge(convolved, t + 1)
                    act.copy(pad[:, u, CONV - 1:], pp[:, u, :])
                    act.copy(conv_s[:, bass.ds(t, 1), :, CONV - 1:CONV].rearrange("p a s k -> p (a s k)"),
                             psm[:, u, 0:DEC]).then_inc(evacuated, 1)
                    act.wait_ge(convolved, t + 3)
                    act.activation(at(xbct, t)[:, PROMPT], acc[:, u, :], ACT.Silu)
                    act.activation(at(xbct, t)[:, SAMPLE], acc_s[:, u, :], ACT.Silu).then_inc(silu_done, 1)

        @block.vector
        def _(dve):
            o = Order(dve, dve_order)
            dve.memset(pad[:, :, 0:CONV - 1], 0.0).then_inc(evacuated, 2)
            dve.memset(acc_s[:], 0.0).then_inc(convolved, 2)
            w, b = c["ssd_conv_w"], c["ssd_conv_b"]
            with dve.Fori(0, XBC // 2) as i:
                o.enter(i, 2 * (CONV + 3))
                for u in range(2):
                    t = i * 2 + u
                    wt = at(w, t)
                    dve.wait_ge(evacuated, t + (nz + 3))
                    o(dve.tensor_scalar(acc[:, u, :], pad[:, u, 0:SEQ], wt[:, 0:1], at(b, t), ALU.mult, ALU.add))
                    o(dve.tensor_tensor(prod[:, u], at(conv_s, t), wt.unsqueeze(1).broadcast_to([P, DEC, CONV]),
                                        ALU.mult))
                    for k in range(1, CONV):
                        o.settle()
                        o(dve.scalar_tensor_tensor(out=acc[:, u, :], in0=pad[:, u, k:k + SEQ], scalar=wt[:, k:k + 1],
                                                   in1=acc[:, u, :], op0=ALU.mult, op1=ALU.add))
                    o(dve.tensor_reduce(acc_s[:, u, :], prod[:, u], AX_X, ALU.add))
                    o.settle()
                    o(dve.tensor_scalar(acc_s[:, u, :], acc_s[:, u, :], at(b, t), None, ALU.add))
                    o.settle()
                    dve.tensor_copy(at(tails, t), pad[:, u, SEQ:SEQ + CONV - 1]).then_inc(convolved, 1)
                o.leave(XBC // 2)
            dve.wait_ge(dt_done, 1)
            dve.tensor_copy(dt_raw[:, PROMPT], pdt[0:SSD_HEADS, 0, :])
            dve.tensor_copy(dt_raw[:, SAMPLE], pdt[0:SSD_HEADS, 1, 0:DEC])


LOG1P_TERMS = 7


def step_sizes(nc, d, c, dt_raw, dts, ec, wend, cdec, negcum, dtr, cumt, dxs):
    H = SSD_HEADS
    with ExitStack() as ctx:
        s = Stage(nc, ctx)
        t, ab, e, sq, p, dta = (s.sb("dt_" + n, [H, COLS]) for n in ("t", "ab", "e", "sq", "p", "dta"))
        a = s.sb("dt_a", [H, 2])
        both = s.sb("dt_both", [H, 2, DEC])
        dtar = s.sb("dt_dtar", [P, TT, H])
        cum = s.sb("dt_cum", [P, TT, H])
        dend = s.sb("dt_dend", [P, TT, H])
        ptr = s.ps("dt_ptr", [P, 2, TT, P])
        psum = s.ps("dt_psum", [P, 2, 512])
        pct = s.ps("dt_pct", [H, 512])
        pex = s.ps("dt_pex", [P, 512])
        dve_order, act_order, pe_order = s.sem("dt_dve"), s.sem("dt_act"), s.sem("dt_pe")
        ready, exped = s.sem("dt_ready"), s.sem("dt_exped")
        block = ctx.enter_context(nc.Block())

        @block.vector
        def _(dve):
            o = Order(dve, dve_order)

            def do(ins):
                o(ins)
                o.settle()

            do(dve.tensor_scalar(t[:], dt_raw[:], c["ssd_dt_bias"][:, 0:1], None, ALU.add))
            o(dve.scalar_tensor_tensor(out=ab[:], in0=t[:], scalar=-1.0, in1=t[:], op0=ALU.mult, op1=ALU.max))
            dve.wait_ge(act_order, 1)
            o(dve.tensor_scalar(a[:, 1:2], a[:, 0:1], -1.0, None, ALU.mult))
            dve.wait_ge(act_order, 2)
            do(dve.tensor_scalar(p[:], e[:], 2.0, None, ALU.add))
            do(dve.reciprocal(p[:], p[:]))
            do(dve.tensor_tensor(e[:], e[:], p[:], ALU.mult))
            do(dve.tensor_tensor(sq[:], e[:], e[:], ALU.mult))
            do(dve.tensor_scalar(p[:], sq[:], 1.0 / (2 * LOG1P_TERMS + 1), None, ALU.mult))
            for k in range(LOG1P_TERMS - 1, 0, -1):
                do(dve.scalar_tensor_tensor(out=p[:], in0=p[:], scalar=1.0 / (2 * k + 1), in1=sq[:], op0=ALU.add,
                                            op1=ALU.mult))
            do(dve.scalar_tensor_tensor(out=p[:], in0=p[:], scalar=1.0, in1=e[:], op0=ALU.add, op1=ALU.mult))
            do(dve.tensor_scalar(t[:], t[:], 0.0, None, ALU.max))
            do(dve.scalar_tensor_tensor(out=dts[:], in0=p[:], scalar=2.0, in1=t[:], op0=ALU.mult, op1=ALU.add))
            do(dve.tensor_scalar(dta[:], dts[:], a[:, 1:2], None, ALU.mult))
            dve.tensor_copy(both[:, 0, :], dts[:, SAMPLE]).then_inc(ready, 1)
            dve.wait_ge(pe_order, 1)
            do(dve.tensor_copy(dtr[:], ptr[:, 0, :, 0:H]))
            dve.tensor_copy(dtar[:], ptr[:, 1, :, 0:H]).then_inc(ready, 1)
            dve.wait_ge(pe_order, 2)
            do(dve.tensor_copy(cum[:].rearrange("p a b -> p (a b)"), psum[:, 0, 0:TT * H]))
            do(dve.tensor_tensor(dend[:].rearrange("p a b -> p (a b)"), psum[:, 1, 0:TT * H],
                                 cum[:].rearrange("p a b -> p (a b)"), ALU.subtract))
            do(dve.tensor_scalar(negcum[:], cum[:], -1.0, None, ALU.mult))
            dve.tensor_copy(cumt[:], pct[:, :]).then_inc(ready, 1)
            dve.wait_ge(exped, 1)
            do(dve.tensor_tensor(wend[:], dend[:], dtr[:], ALU.mult))
            dve.wait_ge(pe_order, 3)
            dve.tensor_copy(dxs[:].rearrange("p a b c -> p (a b c)"), pex[:, 0:DI * 2 * DEC])

        @block.scalar
        def _(act):
            act.preload_act_table(ACT.Exp)
            act.activation(a[:, 0:1], c["ssd_a_log"][:, 0:1], ACT.Exp).then_inc(act_order, 1)
            act.wait_ge(dve_order, 2)
            act.activation(e[:], ab[:], ACT.Exp, scale=-1.0).then_inc(act_order, 1)
            act.wait_ge(ready, 1)
            act.activation(both[:, 1, :], dta[:, SAMPLE], ACT.Exp).then_inc(act_order, 1)
            act.wait_ge(ready, 3)
            act.activation(ec[:], cum[:], ACT.Exp)
            act.activation(cdec[:].rearrange("p a b -> p (a b)"), psum[:, 1, 0:TT * H], ACT.Exp)
            act.activation(dend[:], dend[:], ACT.Exp).then_inc(exped, 1)

        @block.tensor
        def _(pe):
            ident, tri, ones = c["ident"], c["tri"], c["ones"]
            pe.wait_ge(ready, 1)
            for n, src in enumerate((dts, dta)):
                for k in range(TT):
                    mm = pe.transpose(ptr[:, n, k, 0:H], src[:, k * P:(k + 1) * P], ident[0:H, 0:H])
            mm.then_inc(pe_order, 1)
            pe.wait_ge(ready, 2)
            rows = dtar[:].rearrange("p a b -> p (a b)")
            pe.matmul(psum[:, 0, 0:TT * H], tri[:], rows, start=True, stop=True)
            pe.matmul(psum[:, 1, 0:TT * H], ones[:], rows, start=True, stop=True)
            for k in range(TT):
                mm = pe.matmul(pct[:, k * P:(k + 1) * P], dtar[:, k, :], tri[:], start=True, stop=True)
            mm.then_inc(pe_order, 1)
            pe.wait_ge(act_order, 3)
            for k in range(DI):
                mm = pe.matmul(pex[:, k * 2 * DEC:(k + 1) * 2 * DEC], c["expand"][:, k * P:(k + 1) * P],
                               both[:].rearrange("p a b -> p (a b)"), start=True, stop=True)
            mm.then_inc(pe_order, 1)


def scan_prompt(nc, d, c, xbct, zt, dtr, ec, wend, cdec, negcum, cumt, m):
    H = SSD_HEADS
    W = HPG * HEAD_P
    XC = W // P
    with ExitStack() as ctx:
        s = Stage(nc, ctx)
        bs = s.sb("sc_bs", [P, SEQ])
        cs = s.sb("sc_cs", [P, SEQ])
        xs = s.sb("sc_xs", [P, XC, SEQ])
        cbt = s.sb("sc_cbt", [P, TT, P])
        br = s.sb("sc_br", [P, TT, P])
        dg = s.sb("sc_dg", [H, 2, SEQ])
        seg = s.sb("sc_seg", [P, 2, TT, P])
        xdt = s.sb("sc_xdt", [P, HPG, HEAD_P])
        xend = s.sb("sc_xend", [P, HPG, HEAD_P])
        y = s.sb("sc_y", [P, HPG, HEAD_P])
        yx = s.sb("sc_yx", [P, XC, P])
        state = s.sb("sc_state", [P, GROUPS, W])
        pcb = s.ps("sc_pcb", [P, TT, P])
        pbc = s.ps("sc_pbc", [P, 2, 512])
        px = s.ps("sc_px", [P, HPG, HEAD_P])
        pyd = s.ps("sc_pyd", [P, HPG, HEAD_P])
        pyo = s.ps("sc_pyo", [P, HPG, HEAD_P])
        pst = s.ps("sc_pst", [P, HPG, HEAD_P])
        pt = s.ps("sc_pt", [P, XC, P])
        copied, pe_order, act_order, dve_order = s.sem("sc_copied"), s.sem("sc_pe"), s.sem("sc_act"), s.sem("sc_dve")
        masked_row, stored = s.sem("sc_masked_row"), s.sem("sc_stored")
        PE_TURN = 2 + HPG + 3 * TT
        DVE_HEAD = TT + 1

        def dve_chunk(k):
            return 2 + HPG * DVE_HEAD + (6 + 8 * (k - 1) if k else 0)

        DVE_TURN = dve_chunk(TT)
        block = ctx.enter_context(nc.Block())

        @block.gpsimd
        def _(pool):
            with pool.Fori(0, GROUPS) as g:
                pool.wait_ge(dve_order, g * DVE_TURN + 1)
                pool.tensor_copy(bs[:], at(xbct, g + DI)[:, PROMPT])
                pool.tensor_copy(cs[:], at(xbct, g + (DI + GROUPS))[:, PROMPT])
                for k in range(XC):
                    last = pool.tensor_copy(xs[:, k, :], at(xbct, g * XC + k)[:, PROMPT])
                last.then_inc(copied, 1)


        @block.scalar
        def _(act):
            act.preload_act_table(ACT.Exp)
            with act.Fori(0, GROUPS) as g:
                act.wait_ge(copied, g + 1)

                def spread(e):
                    if e >= 2:
                        act.wait_ge(pe_order, g * PE_TURN + (2 + e - 1))
                    act.activation(dg[:, e % 2, :], cumt[:], ACT.Copy,
                                   scale=c["ident"][0:H, bass.ds(g * HPG + e, 1)]).then_inc(masked_row, 1)

                spread(0)
                spread(1)
                for e in range(HPG):
                    act.wait_ge(dve_order, g * DVE_TURN + (1 + 2 + e * DVE_HEAD + TT))
                    act.activation(seg[:, e % 2], seg[:, e % 2], ACT.Exp).then_inc(act_order, 1)
                    if e + 2 < HPG:
                        spread(e + 2)

        @block.tensor
        def _(pe):
            ident, ones = c["ident"], c["ones"]
            o = Order(pe, pe_order)
            with pe.Fori(0, GROUPS) as g:
                o.enter(g, PE_TURN)
                base = g * DVE_TURN + 1
                pe.wait_ge(copied, g + 1)
                for k in range(TT):
                    mm = pe.matmul(pcb[:, k, :], bs[:, k * P:(k + 1) * P], cs[:, k * P:(k + 1) * P],
                                   start=True, stop=True)
                o(mm)
                pe.wait_ge(dve_order, base + 1)
                for k in range(TT):
                    mm = pe.transpose(pcb[:, k, :], bs[:, k * P:(k + 1) * P], ident[:])
                o(mm)
                for e in range(HPG):
                    pe.wait_ge(masked_row, g * HPG + (e + 1))
                    if e >= 2:
                        pe.wait_ge(dve_order, base + 2 + (e - 2) * DVE_HEAD + TT)
                    o(pe.matmul(pbc[:, e % 2, :], ones[0:H, :], dg[:, e % 2, :], start=True, stop=True))
                for k in range(TT):
                    pos = slice(k * P, (k + 1) * P)
                    for j in range(XC):
                        mm = pe.transpose(px[:, 2 * j:2 * j + 2, :].rearrange("p a b -> p (a b)"), xs[:, j, pos],
                                          ident[:])
                    o(mm)
                    pe.wait_ge(dve_order, base + (dve_chunk(k) + 2))
                    for e in range(HPG):
                        pe.matmul(pyd[:, e, :], m[:, e, pos], xdt[:, e, :], start=True, stop=True)
                    if k:
                        pe.matmul(pyo[:].rearrange("p a b -> p (a b)"), cs[:, pos], at(state, g), start=True,
                                  stop=True)
                    o(pe.matmul(pst[:].rearrange("p a b -> p (a b)"), br[:, k, :],
                                xend[:].rearrange("p a b -> p (a b)"), start=True, stop=True))
                    pe.wait_ge(dve_order, base + (dve_chunk(k) + (6 if k else 4)))
                    for j in range(XC):
                        mm = pe.transpose(pt[:, j, :], y[:, 2 * j:2 * j + 2, :].rearrange("p a b -> p (a b)"),
                                          ident[:])
                    o(mm)
                o.leave(GROUPS)

        @block.vector
        def _(dve):
            o = Order(dve, dve_order)
            o(dve.memset(y[:], 0.0))
            with dve.Fori(0, GROUPS) as g:
                o.enter(g, DVE_TURN)
                pbase = g * PE_TURN
                heads = [P, HPG, HEAD_P]

                def of_heads(t, k):
                    return t[:, k, bass.ds(g * HPG, HPG)].unsqueeze(2).broadcast_to(heads)

                dve.wait_ge(pe_order, pbase + 1)
                o(dve.tensor_copy(cbt[:], pcb[:]))
                dve.wait_ge(pe_order, pbase + 2)
                o(dve.tensor_copy(br[:], pcb[:]))

                def segments(e):
                    dve.wait_ge(pe_order, pbase + (2 + e + 1))
                    for k in range(TT):
                        o(dve.scalar_tensor_tensor(out=seg[:, e % 2, k], in0=pbc[:, e % 2, k * P:(k + 1) * P],
                                                   scalar=negcum[:, k, bass.ds(g * HPG + e, 1)],
                                                   in1=c["ssd_mask"][:], op0=ALU.add, op1=ALU.add))

                def decayed(e):
                    dve.wait_ge(act_order, g * HPG + (e + 1))
                    o(dve.tensor_tensor(m[:, e, PROMPT], seg[:, e % 2].rearrange("p a b -> p (a b)"),
                                        cbt[:].rearrange("p a b -> p (a b)"), ALU.mult))

                for e in range(HPG):
                    segments(e)
                    decayed(e)
                for k in range(TT):
                    dve.wait_ge(pe_order, pbase + (2 + HPG + 3 * k + 1))
                    o(dve.tensor_tensor(xdt[:], px[:], of_heads(dtr, k), ALU.mult))
                    o(dve.tensor_tensor(xend[:], px[:], of_heads(wend, k), ALU.mult))
                    dve.wait_ge(pe_order, pbase + (2 + HPG + 3 * k + 2))
                    st = at(state, g).rearrange("p (a b) -> p a b", a=HPG)
                    if k:
                        o(dve.tensor_tensor(y[:], pyo[:], of_heads(ec, k), ALU.mult))
                        o(dve.tensor_tensor(st, st, of_heads(cdec, k), ALU.mult))
                        o.settle()
                        o(dve.tensor_tensor(st, st, pst[:], ALU.add))
                        o(dve.tensor_tensor(y[:], y[:], pyd[:], ALU.add))
                    else:
                        o(dve.tensor_copy(st, pst[:]))
                        o(dve.tensor_copy(y[:], pyd[:]))
                    dve.wait_ge(pe_order, pbase + (2 + HPG + 3 * k + 3))
                    for j in range(XC):
                        ins = dve.scalar_tensor_tensor(out=yx[:, j, :], in0=xs[:, j, k * P:(k + 1) * P],
                                                       scalar=at(c["ssd_d"], g * XC + j), in1=pt[:, j, :],
                                                       op0=ALU.mult, op1=ALU.add)
                    o(ins)
                    o.settle()
                    zk = zt[:, bass.ds(g * XC, XC), k * P:(k + 1) * P]
                    o(dve.tensor_tensor(zk, zk, yx[:], ALU.mult))
                o.leave(GROUPS)

        @block.sync
        def _(sp):
            sp.wait_ge(dve_order, 1 + GROUPS * DVE_TURN)
            sp.dma_start(d["out_p_ssd"], state[:]).then_inc(stored, 16)
            sp.wait_ge(stored, 16)


def scan_sample(nc, d, c, xbct, zt, dxs):
    slots = 2
    with ExitStack() as ctx:
        s = Stage(nc, ctx)
        ring = s.sb("st_ring", [P, slots, DI, STATE])
        diag = s.sb("st_diag", [P, 2, GROUPS, STATE])
        xb = s.sb("st_xb", [P, DI, STATE])
        hc = s.sb("st_hc", [P, DI, STATE])
        xdt = s.sb("st_xdt", [P, DI, DEC])
        y = s.sb("st_y", [P, DEC, DI])
        pb = s.ps("st_pb", [P, 2, 2, GROUPS, STATE])
        landed = [s.sem(f"st_landed{u}") for u in range(slots)]
        stored = [s.sem(f"st_stored{u}") for u in range(slots)]
        spread, outer, dve_order = s.sem("st_spread"), s.sem("st_outer"), s.sem("st_dve")
        ready = s.sem("st_ready")
        TURN = 4
        block = ctx.enter_context(nc.Block())

        @block.sync
        def _(sp):
            for u in range(slots):
                sp.dma_start(ring[:, u], d["ssd_state"][u]).then_inc(landed[u], 16)

            def store(u, q):
                sp.wait_ge(dve_order, q * TURN + 3)
                sp.dma_start(d["out_s_ssd"][bass.ds(q, 1)].rearrange("a p k n -> (a p) k n"),
                             ring[:, u]).then_inc(stored[u], 16)

            with sp.Fori(0, DEC // slots - 1) as i:
                for u in range(slots):
                    store(u, i * slots + u)
                    sp.wait_ge(stored[u], 16 * (i + 1))
                    sp.dma_start(ring[:, u], d["ssd_state"][bass.ds(i * slots + (u + slots), 1)].rearrange(
                        "a p k n -> (a p) k n")).then_inc(landed[u], 16)
            for u in range(slots):
                store(u, DEC - slots + u)
            for u in range(slots):
                sp.wait_ge(stored[u], 16 * (DEC // slots))

        @block.vector
        def _(dve):
            o = Order(dve, dve_order)
            dve.tensor_tensor(xdt[:], xbct[:, 0:DI, SAMPLE], dxs[:, :, 0, :], ALU.mult).then_inc(ready, 1)
            eye = c["ident"][:].unsqueeze(1).broadcast_to([P, GROUPS, P])
            dve.wait_ge(ready, 1)
            with dve.Fori(0, DEC // 2) as i:
                o.enter(i, 2 * TURN)
                for u in range(2):
                    q = i * 2 + u
                    col = bass.ds(q + SEQ, 1)
                    for n in range(2):
                        rows = slice(DI + n * GROUPS, DI + (n + 1) * GROUPS)
                        ins = dve.tensor_tensor(diag[:, n], eye,
                                                xbct[:, rows, col].broadcast_to([P, GROUPS, P]), ALU.mult)
                    o(ins)
                    dve.wait_ge(outer, q + 1)
                    dve.wait_ge(landed[u], 16 * (i + 1))
                    for k in range(DI):
                        ins = dve.scalar_tensor_tensor(out=ring[:, u, k, :], in0=ring[:, u, k, :],
                                                       scalar=dxs[:, k, 1, bass.ds(q, 1)], in1=xb[:, k, :],
                                                       op0=ALU.mult, op1=ALU.add)
                    o(ins)
                    o.settle()
                    for g in range(GROUPS):
                        per = DI // GROUPS
                        ins = dve.tensor_tensor(hc[:, g * per:(g + 1) * per], ring[:, u, g * per:(g + 1) * per],
                                                pb[:, u, 1, g].unsqueeze(1).broadcast_to([P, per, STATE]), ALU.mult)
                    o(ins)
                    o.settle()
                    o(dve.tensor_reduce(at(y, q), hc[:], AX_X, ALU.add))
                o.leave(DEC // 2)
            o.settle()
            dve.tensor_tensor(xdt[:], xbct[:, 0:DI, SAMPLE],
                              c["ssd_d"][:].unsqueeze(2).broadcast_to([P, DI, DEC]), ALU.mult).then_inc(ready, 1)
            dve.wait_ge(ready, 2)
            dve.tensor_tensor(xdt[:], xdt[:], y[:].rearrange("p s k -> p k s"), ALU.add).then_inc(ready, 1)
            dve.wait_ge(ready, 3)
            dve.tensor_tensor(zt[:, :, SAMPLE], zt[:, :, SAMPLE], xdt[:], ALU.mult)

        @block.tensor
        def _(pe):
            with pe.Fori(0, DEC // 2) as i:
                for u in range(2):
                    q = i * 2 + u
                    pe.wait_ge(dve_order, q * TURN + 1)
                    for n in range(2):
                        mm = pe.matmul(pb[:, u, n].rearrange("p a b -> p (a b)"), c["ones"][:],
                                       diag[:, n].rearrange("p a b -> p (a b)"), start=True, stop=True)
                    mm.then_inc(spread, 1)

        @block.scalar
        def _(act):
            act.wait_ge(ready, 1)
            with act.Fori(0, DEC // 2) as i:
                for u in range(2):
                    q = i * 2 + u
                    act.wait_ge(spread, q + 1)
                    for k in range(DI):
                        ins = act.activation(xb[:, k, :], pb[:, u, 0, k // (DI // GROUPS)], ACT.Copy,
                                             scale=xdt[:, k, bass.ds(q, 1)])
                    ins.then_inc(outer, 1)


def gain_and_square(nc, c, zt, r):
    with ExitStack() as ctx:
        s = Stage(nc, ctx)
        sq = s.sb("gn_sq", [P, 2, COLS])
        total = s.ps("gn_total", [P, 2, 512])
        squared, summed, act_order = s.sem("gn_squared"), s.sem("gn_summed"), s.sem("gn_act")
        block = ctx.enter_context(nc.Block())

        @block.scalar
        def _(act):
            act.preload_act_table_set("natural_log_exp_and_others")
            for k in range(DI):
                if k >= 2:
                    act.wait_ge(summed, k - 1)
                act.activation(sq[:, k % 2, :], zt[:, k, :], ACT.Square).then_inc(squared, 1)
            act.wait_ge(summed, DI)
            act.activation(r[:, PROMPT], total[:, 0, :], ACT.Ln, scale=1.0 / D_INNER, bias=c["eps"][:, 0:1])
            act.activation(r[:, SAMPLE], total[:, 1, 0:DEC], ACT.Ln, scale=1.0 / D_INNER,
                           bias=c["eps"][:, 0:1]).then_inc(act_order, 1)
            act.wait_ge(act_order, 1)
            act.activation(r[:, :], r[:, :], ACT.Exp, scale=-0.5)

        @block.tensor
        def _(pe):
            for k in range(DI):
                pe.wait_ge(squared, k + 1)
                pe.matmul(total[:, 0, :], c["ones"][:], sq[:, k % 2, PROMPT], start=k == 0, stop=k == DI - 1)
                pe.matmul(total[:, 1, 0:DEC], c["ones"][:], sq[:, k % 2, SAMPLE], start=k == 0,
                          stop=k == DI - 1).then_inc(summed, 1)

        @block.vector
        def _(dve):
            for k in range(DI):
                dve.wait_ge(squared, k + 1)
                dve.tensor_scalar(zt[:, k, :], zt[:, k, :], c["ssd_norm"][:, k:k + 1], None, ALU.mult)


def merge_branch(nc, d, c, name, n, w_dram, src, kin, h, mixed, r):
    slots = 2
    with ExitStack() as ctx:
        s = Stage(nc, ctx)
        ring = s.sb(name + "_ring", [P, slots, kin + KC, P])
        gate = s.sb(name + "_gate", [P, 2, COLS])
        po = s.ps(name + "_po", [P, 2, 512])
        pg = s.ps(name + "_pg", [P, 2, 512])
        pso = s.ps(name + "_pso", [P, 2, 512])
        psg = s.ps(name + "_psg", [P, 2, 512])
        landed = [s.sem(f"{name}_landed{u}") for u in range(slots)]
        done, gated, evacuated, dve_order = (s.sem(name + x) for x in ("_done", "_gated", "_evacuated", "_dve"))
        block = ctx.enter_context(nc.Block())

        @block.sync
        def _(sp):
            stream_weights(sp, w_dram, ring, landed, done, KC, slots)

        @block.tensor
        def _(pe):
            branch, merge = range(kin), range(kin, kin + KC)
            multiply_tiles(pe, ring, landed, evacuated, done, KC, slots, [
                (lambda b: pg[:, b, :], merge, lambda k: h[:, k, PROMPT]),
                (lambda b: psg[:, b, 0:DEC], merge, lambda k: h[:, k, SAMPLE]),
                (lambda b: po[:, b, :], branch, lambda k: src[:, k, PROMPT]),
                (lambda b: pso[:, b, 0:DEC], branch, lambda k: src[:, k, SAMPLE])])

        @block.scalar
        def _(act):
            act.preload_act_table(ACT.Sigmoid)
            bias = c["b_merge"][:, n * KC:(n + 1) * KC]
            with act.Fori(0, KC // 2) as i:
                for u in range(2):
                    t = i * 2 + u
                    act.wait_ge(done, t + 1)
                    b = bias[:, bass.ds(t, 1)]
                    act.activation(gate[:, u, PROMPT], pg[:, u, :], ACT.Sigmoid, bias=b)
                    act.activation(gate[:, u, SAMPLE], psg[:, u, 0:DEC], ACT.Sigmoid, bias=b).then_inc(gated, 1)

        @block.vector
        def _(dve):
            o = Order(dve, dve_order)
            dve.memset(gate[0:1, 0, 0:1], 0.0).then_inc(evacuated, 2)
            with dve.Fori(0, KC // 2) as i:
                o.enter(i, 4)
                for u in range(2):
                    t = i * 2 + u
                    dve.wait_ge(gated, t + 1)
                    o(dve.tensor_tensor(gate[:, u, PROMPT], po[:, u, :], gate[:, u, PROMPT], ALU.mult))
                    o(dve.tensor_tensor(gate[:, u, SAMPLE], pso[:, u, 0:DEC], gate[:, u, SAMPLE], ALU.mult))
                    o.settle()
                    if r is not None:
                        ins = dve.tensor_tensor(at(mixed, t), gate[:, u, :], r[:], ALU.mult)
                    else:
                        ins = dve.tensor_tensor(at(mixed, t), at(mixed, t), gate[:, u, :], ALU.add)
                    ins.then_inc(evacuated, 1)
                o.leave(KC // 2)


NQ = HEADS // 2
NR = NQ + KV
CK, CV = NR, NR + 2
CMP_P = KV * NCP
CMP_S = KV * DEC * NCS
QK_SCALE = HD ** -0.5


def project_nsa(nc, d, c, h, qk, vr, gates, gates_s):
    slots, tiles = 4, NR + 4
    W = 2 * KV * HD
    G = 3 * HEADS
    with ExitStack() as ctx:
        s = Stage(nc, ctx)
        ring = s.sb("nq_ring", [P, slots, KC, P])
        wv = s.sb("nq_wv", [P, KC, W])
        wg = s.sb("nq_wg", [P, KC, G])
        gs = s.sb("nq_gs", [DEC, G])
        pp = s.ps("nq_pp", [P, 2, 512])
        psm = s.ps("nq_ps", [P, 2, 512])
        pv = s.ps("nq_pv", [P, 2, 512])
        pg = s.ps("nq_pg", [P, 2, 512])
        landed = [s.sem(f"nq_landed{u}") for u in range(slots)]
        v_landed = s.sem("nq_v_landed")
        done, evacuated, rows_done, rows_out = (s.sem("nq_" + x) for x in ("done", "evac", "rows_done", "rows_out"))
        gates_out, stored = s.sem("nq_gates_out"), s.sem("nq_stored")
        block = ctx.enter_context(nc.Block())

        @block.sync
        def _(sp):
            sp.dma_start(wv[:], d["w_v"]).then_inc(v_landed, 16)
            sp.dma_start(wg[:], d["w_gates"]).then_inc(v_landed, 16)
            stream_weights(sp, d["w_qk"], ring, landed, done, tiles, slots)
            sp.wait_ge(evacuated, 2 + tiles)
            sp.dma_start(d["out_cmp"], qk[:, CK:CK + 4, :]).then_inc(stored, 16)
            sp.wait_ge(rows_out, 2 * (TT + 1))
            sp.dma_start(d["out_v"], vr[:, 0:TT, :]).then_inc(stored, 16)
            sp.dma_start(d["out_v_s"], vr[0:DEC, TT, :]).then_inc(stored, 16)
            sp.wait_ge(gates_out, TT + 1)
            sp.dma_start(d["gates_turn"], gs[:]).then_inc(stored, 16)
            sp.wait_ge(stored, 64)
            sp.dma_start(gates_s[:], d["gates_turn"].rearrange("s (h b) -> (s h) b", b=3)).then_inc(stored, 16)
            sp.wait_ge(stored, 80)

        @block.tensor
        def _(pe):
            pe.wait_ge(v_landed, 32)
            for i in range(TT + 1):
                part, m = (slice(i * P, (i + 1) * P), P) if i < TT else (SAMPLE, DEC)
                if i >= 2:
                    pe.wait_ge(rows_out, 2 * (i - 1))
                    pe.wait_ge(gates_out, i - 1)
                for w, out, n in ((wv, pv, W), (wg, pg, G)):
                    for k in range(KC):
                        mm = pe.matmul(out[0:m, i % 2, 0:n], h[:, k, part], w[:, k, :], start=k == 0,
                                       stop=k == KC - 1)
                mm.then_inc(rows_done, 1)
            multiply_tiles(pe, ring, landed, evacuated, done, tiles, slots, [
                (lambda b: pp[:, b, :], range(KC), lambda k: h[:, k, PROMPT]),
                (lambda b: psm[:, b, 0:DEC], range(KC), lambda k: h[:, k, SAMPLE])])

        @block.vector
        def _(dve):
            dve.memset(vr[:, TT, :], 0.0).then_inc(evacuated, 2)
            for i in range(TT + 1):
                m = P if i < TT else DEC
                dve.wait_ge(rows_done, i + 1)
                if i == TT:
                    dve.wait_ge(rows_out, 2 * TT)
                    dve.wait_ge(evacuated, 2)
                dve.tensor_copy(vr[0:m, i, :], pv[0:m, i % 2, :]).then_inc(rows_out, 2)

        @block.scalar
        def _(act):
            act.preload_act_table(ACT.Sigmoid)
            for i in range(TT + 1):
                m = P if i < TT else DEC
                act.wait_ge(rows_done, i + 1)
                dst = gates[0:m, i, :] if i < TT else gs[:]
                act.activation(dst, pg[0:m, i % 2, 0:G], ACT.Sigmoid).then_inc(gates_out, 1)
            with act.Fori(0, tiles // 2) as i:
                for u in range(2):
                    t = i * 2 + u
                    act.wait_ge(done, t + 1)
                    act.activation(at(qk, t)[:, PROMPT], pp[:, u, :], ACT.Copy)
                    act.activation(at(qk, t)[:, SAMPLE], psm[:, u, 0:DEC], ACT.Copy).then_inc(evacuated, 1)


def rotate_tiles(nc, d, c, qk):
    with ExitStack() as ctx:
        s = Stage(nc, ctx)
        sq = s.sb("ro_sq", [P, 2, COLS])
        r = s.sb("ro_r", [P, 2, COLS])
        n = s.sb("ro_n", [P, 2, COLS])
        t2 = s.sb("ro_t2", [P, 2, COLS])
        pss = s.ps("ro_pss", [P, 2, 2, 512])
        prt = s.ps("ro_prt", [P, 2, 2, 512])
        squared, summed, scaled, normed, turned = (s.sem("ro_" + x) for x in (
            "squared", "summed", "scaled", "normed", "turned"))
        dve_order, act_order, stored = s.sem("ro_dve"), s.sem("ro_act"), s.sem("ro_stored")
        block = ctx.enter_context(nc.Block())

        @block.scalar
        def _(act):
            act.preload_act_table_set("natural_log_exp_and_others")
            o = Order(act, act_order)
            with act.Fori(0, NR // 2) as i:
                o.enter(i, 4)
                for u in range(2):
                    j = i * 2 + u
                    act.activation(sq[:, u, :], at(qk, j), ACT.Square).then_inc(squared, 1)
                    act.wait_ge(summed, j + 1)
                    o(act.activation(r[:, u, PROMPT], pss[:, u, 0, :], ACT.Ln, scale=1.0 / HD, bias=c["eps"][:, 0:1]))
                    o(act.activation(r[:, u, SAMPLE], pss[:, u, 1, 0:DEC], ACT.Ln, scale=1.0 / HD,
                                     bias=c["eps"][:, 0:1]))
                    o.settle()
                    act.activation(r[:, u, :], r[:, u, :], ACT.Exp, scale=-0.5).then_inc(scaled, 1)
                o.leave(NR // 2)

        @block.tensor
        def _(pe):
            with pe.Fori(0, NR // 2) as i:
                for u in range(2):
                    j = i * 2 + u
                    pe.wait_ge(squared, j + 1)
                    pe.matmul(pss[:, u, 0, :], c["head_ones"][:], sq[:, u, PROMPT], start=True, stop=True)
                    pe.matmul(pss[:, u, 1, 0:DEC], c["head_ones"][:], sq[:, u, SAMPLE], start=True,
                              stop=True).then_inc(summed, 1)
                    pe.wait_ge(normed, j + 1)
                    pe.matmul(prt[:, u, 0, :], c["rotate"][:], n[:, u, PROMPT], start=True, stop=True)
                    pe.matmul(prt[:, u, 1, 0:DEC], c["rotate"][:], n[:, u, SAMPLE], start=True,
                              stop=True).then_inc(turned, 1)

        @block.vector
        def _(dve):
            o = Order(dve, dve_order)
            with dve.Fori(0, NR // 2) as i:
                o.enter(i, 8)
                for u in range(2):
                    j = i * 2 + u
                    dve.wait_ge(scaled, j + 1)
                    dve.scalar_tensor_tensor(out=n[:, u, :], in0=at(qk, j), scalar=at(c["head_gain"], j),
                                             in1=r[:, u, :], op0=ALU.mult, op1=ALU.mult).then_inc(normed, 1)
                    dve.wait_ge(normed, j + 1)
                    o(dve.tensor_tensor(r[:, u, :], n[:, u, :], c["cos"][:], ALU.mult))
                    dve.wait_ge(turned, j + 1)
                    o(dve.tensor_tensor(t2[:, u, PROMPT], prt[:, u, 0, :], c["sin"][:, PROMPT], ALU.mult))
                    o(dve.tensor_tensor(t2[:, u, SAMPLE], prt[:, u, 1, 0:DEC], c["sin"][:, SAMPLE], ALU.mult))
                    o.settle()
                    o(dve.tensor_tensor(at(qk, j), r[:, u, :], t2[:, u, :], ALU.add))
                o.leave(NR // 2)

        @block.sync
        def _(sp):
            sp.wait_ge(dve_order, 4 * NR)
            sp.dma_start(d["out_k"], qk[:, NQ:NR, :]).then_inc(stored, 16)
            sp.wait_ge(stored, 16)


def compress_rows(nc, d, c, qk, kct, vcp, vcs):
    PAIRS = CMP_LEN // 2
    NP_ALL = CMP_P + CMP_S
    with ExitStack() as ctx:
        s = Stage(nc, ctx)
        tp = s.sb("cm_tp", [P, KV, SEQ])
        ts = s.sb("cm_ts", [P, KV, DEC, PAST])
        w1 = s.sb("cm_w1", [P, 2, PAIRS, P])
        w2 = s.sb("cm_w2", [P, 2, 2 * HD])
        pos = s.sb("cm_pos", [P, 2, PAIRS])
        pb = s.sb("cm_pb", [P, 2])
        hid = s.sb("cm_hid", [P, NP_ALL])
        r = s.sb("cm_r", [P, NP_ALL])
        n = s.sb("cm_n", [P, NP_ALL])
        t2 = s.sb("cm_t2", [P, NP_ALL])
        table = s.sb("cm_table", [1, DEC * PAGES], I32)
        php = s.ps("cm_php", [P, 512])
        phs = s.ps("cm_phs", [P, 512])
        ppe = s.ps("cm_ppe", [P, 2])
        pa = s.ps("cm_pa", [P, 2, 512])
        pv = s.ps("cm_pv", [P, 2, KV, HD])
        w_landed, table_landed, pages_landed = s.sem("cm_w_landed"), s.sem("cm_table"), s.sem("cm_pages")
        turned, products, act_order, dve_order = s.sem("cm_turned"), s.sem("cm_products"), s.sem("cm_act"), s.sem("cm_dve")
        shifted = s.sem("cm_shifted")
        block = ctx.enter_context(nc.Block())
        parts = ((0, CMP_P), (CMP_P, NP_ALL))

        @block.sync
        def _(sp):
            sp.dma_start(table[:], d["page_table"]).then_inc(table_landed, 16)
            sp.dma_start(w1[:], d["cmp_w1"]).then_inc(w_landed, 16)
            sp.dma_start(w2[:], d["cmp_w2"]).then_inc(w_landed, 16)
            sp.dma_start(pos[:], d["cmp_pe"]).then_inc(w_landed, 16)
            sp.wait_ge(table_landed, 16)
            for kind, name in enumerate(("pool_cmp_k", "pool_cmp_v")):
                if kind:
                    sp.wait_ge(products, 2)
                for q in range(DEC):
                    for g in range(PAGES):
                        page = sp.value_load(table[0:1, q * PAGES + g:q * PAGES + g + 1], min_val=0,
                                             max_val=d[name].shape[0] - 1)
                        src = d[name][bass.ds(page, 1)].rearrange("a p k n -> (a p) k n")
                        lo = g * PAGE
                        sp.dma_start(ts[0:HD, :, q, lo:lo + PAGE], src).then_inc(pages_landed, 16)
                        skip = 1 if g == 0 else 0
                        sp.dma_start(ts[HD:P, :, q, lo - 1 + skip:lo - 1 + PAGE],
                                     src[:, :, skip:PAGE]).then_inc(pages_landed, 16)

        @block.gpsimd
        def _(pool):
            for kind in range(2):
                if kind:
                    pool.wait_ge(products, 2)
                for half in range(2):
                    for kv in range(KV):
                        rows = slice((kv % 2) * HD, (kv % 2 + 1) * HD)
                        last = pool.tensor_copy(tp[half * HD:(half + 1) * HD, kv, 0:SEQ - half],
                                                qk[rows, CK + 2 * kind + kv // 2, half:SEQ])
                last.then_inc(turned, 1)

        @block.tensor
        def _(pe):
            pe.wait_ge(w_landed, 48)
            for kind in range(2):
                for l in range(PAIRS):
                    mm = pe.matmul(ppe[:, kind:kind + 1], w1[:, kind, l, :], pos[:, kind, l:l + 1], start=l == 0,
                                   stop=l == PAIRS - 1)
                mm.then_inc(products, 1)
                pe.wait_ge(turned, kind + 1)
                for l in range(PAIRS):
                    pe.matmul(php[:, 0:CMP_P], w1[:, kind, l, :],
                              tp[:, :, 2 * l:2 * l + CMP_STRIDE * (NCP - 1) + 1:CMP_STRIDE],
                              start=l == 0, stop=l == PAIRS - 1)
                pe.wait_ge(pages_landed, 16 * 2 * DEC * PAGES * (kind + 1))
                for l in range(PAIRS):
                    mm = pe.matmul(phs[:, 0:CMP_S], w1[:, kind, l, :],
                                   ts[:, :, :, 2 * l:2 * l + CMP_STRIDE * (NCS - 1) + 1:CMP_STRIDE].rearrange(
                                       "p k s n -> p (k s) n"),
                                   start=l == 0, stop=l == PAIRS - 1)
                mm.then_inc(products, 1)
                pe.wait_ge(act_order, 3 * (kind + 1) if kind == 0 else 3 + 3 + 3)
                if kind == 0:
                    for m, (a, b) in enumerate(parts):
                        mm = pe.matmul(pa[:, m, 0:b - a], w2[:, 0, :], hid[:, a:b], start=True, stop=True)
                    mm.then_inc(products, 1)
                    pe.wait_ge(act_order, 4)
                    pe.wait_ge(dve_order, 1)
                    for m, (a, b) in enumerate(parts):
                        mm = pe.matmul(pa[:, m, 0:b - a], c["head_ones"][:], r[:, a:b], start=True, stop=True)
                    mm.then_inc(products, 1)
                    pe.wait_ge(dve_order, 2)
                    for m, (a, b) in enumerate(parts):
                        mm = pe.matmul(pa[:, m, 0:b - a], c["rotate"][:], n[:, a:b], start=True, stop=True)
                    mm.then_inc(products, 1)
                else:
                    for kv in range(KV):
                        pe.matmul(pv[0:NCP, 0, kv, :], hid[:, kv * NCP:(kv + 1) * NCP], w2[:, 1, 0:HD], start=True,
                                  stop=True)
                    for kv in range(KV):
                        a = CMP_P + kv * DEC * NCS
                        mm = pe.matmul(pv[0:DEC * NCS, 1, kv, :], hid[:, a:a + DEC * NCS], w2[:, 1, 0:HD],
                                       start=True, stop=True)
                    mm.then_inc(products, 1)

        @block.scalar
        def _(act):
            o = Order(act, act_order)
            act.preload_act_table(ACT.Silu)
            for kind in range(2):
                act.wait_ge(products, 2 if kind == 0 else 7)
                o(act.activation(pb[:, kind:kind + 1], ppe[:, kind:kind + 1], ACT.Copy))
                o.settle()
                o(act.activation(hid[:, 0:CMP_P], php[:, 0:CMP_P], ACT.Silu, bias=pb[:, kind:kind + 1]))
                o(act.activation(hid[:, CMP_P:], phs[:, 0:CMP_S], ACT.Silu, bias=pb[:, kind:kind + 1]))
                if kind == 0:
                    act.wait_ge(products, 3)
                    act.activation(r[:, 0:CMP_P], pa[:, 0, 0:CMP_P], ACT.Square)
                    o(act.activation(r[:, CMP_P:], pa[:, 1, 0:CMP_S], ACT.Square))
                    act.wait_ge(products, 4)
                    act.activation(r[:, 0:CMP_P], pa[:, 0, 0:CMP_P], ACT.Ln, scale=1.0 / HD, bias=c["eps"][:, 0:1])
                    o(act.activation(r[:, CMP_P:], pa[:, 1, 0:CMP_S], ACT.Ln, scale=1.0 / HD, bias=c["eps"][:, 0:1]))
                    o.settle()
                    o(act.activation(r[:], r[:], ACT.Exp, scale=-0.5))

        @block.vector
        def _(dve):
            o = Order(dve, dve_order)
            gain = c["cmp_gain"][:, 0:1]
            dve.wait_ge(products, 3)
            dve.wait_ge(act_order, 4)
            dve.tensor_copy(n[:, 0:CMP_P], pa[:, 0, 0:CMP_P])
            o(dve.tensor_copy(n[:, CMP_P:], pa[:, 1, 0:CMP_S]))
            dve.wait_ge(act_order, 6)
            dve.wait_ge(dve_order, 1)
            o(dve.scalar_tensor_tensor(out=n[:], in0=n[:], scalar=gain, in1=r[:], op0=ALU.mult, op1=ALU.mult))
            o.settle()
            dve.wait_ge(products, 5)
            o(dve.tensor_tensor(t2[:, 0:CMP_P], pa[:, 0, 0:CMP_P], c["cmp_sin"][:, 0:CMP_P], ALU.mult))
            o(dve.tensor_tensor(t2[:, CMP_P:], pa[:, 1, 0:CMP_S], c["cmp_sin"][:, CMP_P:], ALU.mult))
            o(dve.tensor_tensor(n[:], n[:], c["cmp_cos"][:], ALU.mult))
            o.settle()
            dve.tensor_tensor(kct[:], n[:], t2[:], ALU.add)
            dve.wait_ge(products, 8)
            dve.tensor_copy(vcp[0:NCP], pv[0:NCP, 0])
            dve.tensor_copy(vcs[0:DEC * NCS], pv[0:DEC * NCS, 1])


def attend_prompt(nc, d, c, qk, vr, gates, kct, vcp, ot):
    UNITS = KV
    BLOCKS = [(kb, i) for kb in range(TT) for i in range(kb, TT)]
    GROUPS_T = [[0], [1], [2, 3]]
    EV = 1 + 2 * len(GROUPS_T)
    with ExitStack() as ctx:
        s = Stage(nc, ctx)
        qs = s.sb("ap_qs", [P, 2, SEQ])
        pr = s.sb("ap_pr", [P, 2, TT, 2, SEQ])
        pc = s.sb("ap_pc", [P, 2, TT, NCP])
        pt = s.sb("ap_pt", [P, EV, SEQ])
        mx = s.sb("ap_mx", [P, TT, 2])
        mc = s.sb("ap_mc", [P, TT])
        nb = s.sb("ap_nb", [P, 2, TT, 2])
        den = s.sb("ap_den", [P, 2, TT, 3])
        pss = s.ps("ap_pss", [P, 2, 2, 512])
        psc = s.ps("ap_psc", [P, TT, 32])
        pst = s.ps("ap_pst", [P, 2, 512])
        pso = s.ps("ap_pso", [P, 512])
        copied, scored, shifted, exped = (s.sem("ap_" + x) for x in ("copied", "scored", "shifted", "exped"))
        scaled, scaled_w, turned, evacuated = (s.sem("ap_" + x) for x in ("scaled", "scaled_w", "turned", "evac"))
        summed, written, dve_order, pool_ready = (s.sem("ap_" + x) for x in ("summed", "written", "dve", "pool_ready"))
        block = ctx.enter_context(nc.Block())

        @block.gpsimd
        def _(pool):
            with pool.Fori(0, GQ) as g:
                pool.wait_ge(written, g * UNITS + 1)
                pool.tensor_copy(qs[:, 0, :], at(qk, g)[:, PROMPT])
                pool.tensor_copy(qs[:, 1, :], at(qk, g + GQ)[:, PROMPT]).then_inc(copied, 1)
                for u in range(UNITS):
                    pool.wait_ge(pool_ready, g * UNITS + (u + 1))
                    for i in range(TT):
                        w = (i + 1) * P
                        ins = pool.tensor_tensor(pr[:, u % 2, i, 1, 0:w], pr[:, u % 2, i, 1, 0:w],
                                                 den[:, u % 2, i, 2:3].broadcast_to([P, w]), ALU.mult)
                    ins.then_inc(scaled_w, 1)

        @block.tensor
        def _(pe):
            ident = c["ident"]
            with pe.Fori(0, GQ) as g:

                def scores(u):
                    ch, half = u // 2, slice((u % 2) * HD, (u % 2 + 1) * HD)
                    if u:
                        pe.wait_ge(shifted, g * 5 * UNITS + (5 * (u - 1) + 1))
                    for i in range(TT):
                        mm = pe.matmul(psc[:, i, 0:NCP], qs[half, ch, i * P:(i + 1) * P],
                                       kct[half, u * NCP:(u + 1) * NCP], start=True, stop=True)
                    mm.then_inc(scored, 1)
                    for i in range(TT):
                        if i >= 2 or u:
                            pe.wait_ge(exped, g * 5 * UNITS + (5 * u + 1 + (i - 2) + 1 if i >= 2
                                                               else 5 * (u - 1) + 1 + (i + 2) + 1))
                        for b in range(2):
                            mm = pe.matmul(pss[:, i % 2, b, 0:(i + 1) * P], qs[half, ch, i * P:(i + 1) * P],
                                           qk[half, NQ + 2 * b + ch, 0:(i + 1) * P], start=True, stop=True)
                        mm.then_inc(scored, 1)

                def products(u):
                    ch, half = u // 2, slice((u % 2) * HD, (u % 2 + 1) * HD)
                    pe.wait_ge(scaled, g * UNITS + (u + 1))
                    first_v = [True]

                    def turn(k):
                        if k >= 2:
                            pe.wait_ge(evacuated, g * EV * UNITS + (EV * u + k - 1))
                        if k == 1 + len(GROUPS_T):
                            pe.wait_ge(scaled_w, g * UNITS + (u + 1))
                        if k == 0:
                            for i in range(TT):
                                mm = pe.transpose(pst[0:NCP, k % 2, i * P:(i + 1) * P], pc[:, u % 2, i, :], ident[:])
                        else:
                            b, gr = (k - 1) // len(GROUPS_T), GROUPS_T[(k - 1) % len(GROUPS_T)]
                            for n, (kb, i) in enumerate([x for x in BLOCKS if x[0] in gr]):
                                mm = pe.transpose(pst[:, k % 2, n * P:(n + 1) * P],
                                                  pr[:, u % 2, i, b, kb * P:(kb + 1) * P], ident[:])
                        mm.then_inc(turned, 1)

                    def values(k):
                        pe.wait_ge(evacuated, g * EV * UNITS + (EV * u + k + 1))
                        if k == 0:
                            return pe.matmul(pso[half, :], vcp[0:NCP, u, :], pt[0:NCP, 0, :], start=True, stop=False,
                                             skip_group_check=True)
                        b, gr = (k - 1) // len(GROUPS_T), GROUPS_T[(k - 1) % len(GROUPS_T)]
                        n = 0
                        for kb in gr:
                            w = (TT - kb) * P
                            mm = pe.matmul(pso[half, kb * P:SEQ], vr[:, kb, (b * KV + u) * HD:(b * KV + u + 1) * HD],
                                           pt[:, k, n * P:n * P + w], start=False, stop=k == EV - 1 and kb == gr[-1],
                                           skip_group_check=True)
                            n += TT - kb
                        return mm

                    turn(0)
                    if u >= 2:
                        pe.wait_ge(written, g * UNITS + (u - 2 + 2))
                    for k in range(EV):
                        if k + 1 < EV:
                            turn(k + 1)
                        mm = values(k)
                    mm.then_inc(summed, 1)

                pe.wait_ge(copied, g + 1)
                scores(0)
                for u in range(UNITS):
                    if u + 1 < UNITS:
                        scores(u + 1)
                    products(u)

        @block.vector
        def _(dve):
            o = Order(dve, dve_order)
            dve.memset(mx[:], 0.0).then_inc(written, 1)
            TURN = UNITS * (3 + 2 * TT + 4)
            with dve.Fori(0, GQ) as g:
                o.enter(g, TURN)
                for u in range(UNITS):
                    head = (u // 2) * 2 * GQ + (u % 2) * GQ
                    pcu = pc[:, u % 2]
                    if u >= 2:
                        dve.wait_ge(turned, g * EV * UNITS + EV * (u - 1))
                    dve.wait_ge(scored, g * 5 * UNITS + (5 * u + 1))
                    o(dve.tensor_tensor(pcu, psc[:, :, 0:NCP], c["cmp_mask"][:], ALU.add))
                    o.settle()
                    o(dve.tensor_reduce(mc[:], pcu, AX_X, ALU.max))
                    o.settle()
                    o(dve.tensor_scalar(mc[:], mc[:], FLOOR, None, ALU.max))
                    o.settle()
                    dve.tensor_tensor(pcu, pcu, mc[:].unsqueeze(2).broadcast_to([P, TT, NCP]),
                                      ALU.subtract).then_inc(shifted, 1)
                    for i in range(TT):
                        dve.wait_ge(scored, g * 5 * UNITS + (5 * u + 2 + i))
                        blk = pss[:, i % 2, :, i * P:(i + 1) * P]
                        o(dve.tensor_tensor(blk, blk, c["causal"][:].unsqueeze(1).broadcast_to([P, 2, P]), ALU.add))
                        o.settle()
                        o(dve.tensor_reduce(mx[:, i, :], pss[:, i % 2, :, 0:(i + 1) * P], AX_X, ALU.max))
                        o.settle()
                        dve.tensor_scalar(nb[:, u % 2, i, :], mx[:, i, :], -QK_SCALE, None,
                                          ALU.mult).then_inc(shifted, 1)
                    dn = den[:, u % 2]
                    dve.wait_ge(exped, g * 5 * UNITS + 5 * (u + 1))
                    o(dve.tensor_reduce(dn[:, :, 0], pcu, AX_X, ALU.add))
                    o.settle()
                    o(dve.tensor_scalar(dn, dn, 1e-30, None, ALU.max))
                    o.settle()
                    o(dve.reciprocal(dn, dn))
                    o.settle()
                    dve.tensor_tensor(dn, dn, gates[:, :, bass.ds(g * 3 + head * 3, 3)], ALU.mult).then_inc(pool_ready, 1)
                    dve.wait_ge(pool_ready, g * UNITS + (u + 1))
                    o(dve.tensor_tensor(pcu, pcu, dn[:, :, 0:1].broadcast_to([P, TT, NCP]), ALU.mult))
                    for i in range(TT):
                        w = (i + 1) * P
                        ins = dve.tensor_scalar(pr[:, u % 2, i, 0, 0:w], pr[:, u % 2, i, 0, 0:w], dn[:, i, 1:2], None,
                                                ALU.mult)
                    ins.then_inc(scaled, 1)
                    o.settle()
                o.leave(GQ)

        @block.scalar
        def _(act):
            act.preload_act_table(ACT.Exp)
            with act.Fori(0, GQ) as g:

                def weights(u):
                    if u >= 2:
                        act.wait_ge(turned, g * EV * UNITS + EV * (u - 1))
                    act.wait_ge(shifted, g * 5 * UNITS + (5 * u + 1))
                    act.activation(pc[:, u % 2], pc[:, u % 2], ACT.Exp, scale=QK_SCALE).then_inc(exped, 1)
                    for i in range(TT):
                        act.wait_ge(shifted, g * 5 * UNITS + (5 * u + 2 + i))
                        w = (i + 1) * P
                        for b in range(2):
                            ins = act.activation(pr[:, u % 2, i, b, 0:w], pss[:, i % 2, b, 0:w], ACT.Exp,
                                                 scale=QK_SCALE, bias=nb[:, u % 2, i, b:b + 1],
                                                 accum_out=den[:, u % 2, i, 1 + b:2 + b])
                        ins.then_inc(exped, 1)

                def evacuate(u):
                    for k in range(EV):
                        act.wait_ge(turned, g * EV * UNITS + (EV * u + k + 1))
                        if k == 0 and u:
                            act.wait_ge(summed, g * UNITS + u)
                        w = {0: SEQ, 1: SEQ, 2: SEQ - P, 3: 3 * P}[(k - 1) % 3 + 1 if k else 0]
                        rows = slice(0, P) if k else slice(0, NCP)
                        act.copy(pt[rows, k, 0:w], pst[rows, k % 2, 0:w]).then_inc(evacuated, 1)
                    half = slice((u % 2) * HD, (u % 2 + 1) * HD)
                    act.wait_ge(summed, g * UNITS + (u + 1))
                    act.copy(at(ot, g + (u // 2) * GQ)[half, PROMPT], pso[half, :]).then_inc(written, 1)

                weights(0)
                for u in range(UNITS):
                    if u + 1 < UNITS:
                        weights(u + 1)
                    evacuate(u)


def attend_sample_nsa(nc, d, c, qk, vr, gates_s, kct, vcs, ot):
    with ExitStack() as ctx:
        s = Stage(nc, ctx)
        qd = s.sb("as_qd", [P, 2, DEC * DIAG])
        q64 = s.sb("as_q64", [HD, ROWS])
        kt = s.sb("as_kt", [P, 2, 2, DEC, PAST + 1])
        vt = s.sb("as_vt", [P, DEC, PAGES, KV * HD])
        pd = s.sb("as_pd", [P, PAGES, DEC * DIAG])
        w = s.sb("as_w", [P, PAST + 1])
        wc = s.sb("as_wc", [P, KV, DEC * NCS])
        wct = s.sb("as_wct", [P, KV, P])
        wn = s.sb("as_wn", [P, DEC])
        wnt = s.sb("as_wnt", [DEC, P])
        st = s.sb("as_st", [P, 4])
        osum = s.sb("as_o", [P, HD])
        table = s.sb("as_table", [1, DEC * PAGES], I32)
        psc = s.ps("as_psc", [P, 512])
        ptr = s.ps("as_ptr", [P, PAGES, P])
        pn = s.ps("as_pn", [DEC, P])
        pcs = s.ps("as_pcs", [P, 512])
        pct = s.ps("as_pct", [P, KV, P])
        po = s.ps("as_po", [P, KV * HD])
        poc = s.ps("as_poc", [P, HD])
        pot = s.ps("as_pot", [HD, P])
        table_landed, k_landed = s.sem("as_table_landed"), s.sem("as_k_landed")
        v_landed, vw_landed = s.sem("as_v_landed"), s.sem("as_vw_landed")
        pe_order, act_order, dve_order, pool_order = (s.sem("as_" + x) for x in ("pe", "act", "dve", "pool"))
        dve_steps, shift_ready = s.sem("as_dve_steps"), s.sem("as_shift_ready")
        PE_SEL_VALUES = 6
        block = ctx.enter_context(nc.Block())

        @block.sync
        def _(sp):
            sp.dma_start(table[:], d["page_table"]).then_inc(table_landed, 16)
            sp.dma_start(kt[:, 1, :, :, 0:PAST], d["win_k"]).then_inc(k_landed, 16)
            sp.wait_ge(table_landed, 16)
            for q in range(DEC):
                for g in range(PAGES):
                    page = sp.value_load(table[0:1, q * PAGES + g:q * PAGES + g + 1], min_val=0,
                                         max_val=d["pool_sel_k"].shape[0] - 1)
                    sp.dma_start(kt[:, 0, :, q, g * PAGE:(g + 1) * PAGE],
                                 d["pool_sel_k"][bass.ds(page, 1)].rearrange("a p k n -> (a p) k n")
                                 ).then_inc(k_landed, 16)
                    sp.dma_start(vt[:, q, g, :], d["pool_sel_v"][bass.ds(page, 1)].rearrange("a p n -> (a p) n")
                                 ).then_inc(v_landed, 16)
            sp.wait_ge(pe_order, PE_SEL_VALUES)
            sp.dma_start(vt[:], d["win_v"]).then_inc(vw_landed, 16)

        @block.gpsimd
        def _(pool):
            pool.memset(qd[:], 0.0).then_inc(pool_order, 1)
            pool.memset(pd[:], 0.0).then_inc(pool_order, 1)

        @block.tensor
        def _(pe):
            ident = c["ident"]
            o = Order(pe, pe_order)
            pe.wait_ge(dve_order, 1)
            o(pe.matmul(pcs[:, 0:CMP_S], q64[:], kct[0:HD, CMP_P:], start=True, stop=True))
            pe.wait_ge(dve_order, 2)
            for kv in range(KV):
                mm = pe.transpose(pct[0:DEC * NCS, kv, :], wc[:, kv, :], ident[:])
            o(mm)
            pe.wait_ge(k_landed, 16 * (1 + DEC * PAGES))
            pe.wait_ge(pool_order, 3)
            for b in range(2):
                n = 0
                if b:
                    pe.wait_ge(act_order, 2)
                for q in range(DEC):
                    for ch in range(2):
                        mm = pe.matmul(psc[:, 0:PAST + 1], qd[:, ch, 0:DEC * P].rearrange("p (s r) -> p s r", s=DEC)[
                            :, q, :], kt[:, b, ch, q, :], start=n == 0, stop=n == 2 * DEC - 1)
                        n += 1
                o(mm)
                pe.wait_ge(dve_order, 3 + 2 * b)
                for g in range(PAGES):
                    mm = pe.transpose(ptr[:, g, :], w[:, g * PAGE:(g + 1) * PAGE], ident[:])
                o(mm)
                o(pe.transpose(pn[:], wn[:], ident[:]))
                pe.wait_ge(dve_order, 4 + 2 * b)
                if b:
                    pe.wait_ge(vw_landed, 16)
                else:
                    pe.wait_ge(v_landed, 16 * DEC * PAGES)
                for q in range(DEC):
                    for g in range(PAGES):
                        pe.matmul(po[:], pd[:, g, 0:DEC * P].rearrange("p (s r) -> p s r", s=DEC)[:, q, :],
                                  vt[:, q, g, :], start=b == 0 and q == 0 and g == 0, stop=False,
                                  skip_group_check=True)
                o(pe.matmul(po[:], wnt[:], vr[0:DEC, TT, b * KV * HD:(b + 1) * KV * HD], start=False, stop=b == 1,
                            skip_group_check=True))
            for kv in range(KV):
                mm = pe.matmul(poc[:], wct[0:DEC * NCS, kv, :], vcs[0:DEC * NCS, kv, :], start=kv == 0,
                               stop=kv == KV - 1)
            o(mm)
            pe.wait_ge(dve_order, 7)
            o(pe.transpose(pot[:], osum[:], ident[:]))

        @block.scalar
        def _(act):
            act.preload_act_table(ACT.Exp)
            o = Order(act, act_order)
            act.wait_ge(pool_order, 2)
            for ch in range(2):
                for par in range(2):
                    half = slice(par * HD, (par + 1) * HD)
                    first = ch * 2 * GQ + par * GQ
                    dst = qd[half, ch, :].rearrange("p (s x) -> p s x", x=DIAG)[:, :, first:first + GQ]
                    act.copy(dst, qk[half, ch * GQ:(ch + 1) * GQ, SAMPLE].rearrange("p g s -> p s g"))
            for b in range(2):
                for ch in range(2):
                    ins = act.copy(kt[:, b, ch, :, PAST], qk[:, NQ + 2 * b + ch, SAMPLE])
            ins.then_inc(pool_order, 1)
            act.wait_ge(shift_ready, 1)
            o(act.activation(wc[:], wc[:], ACT.Exp, scale=QK_SCALE, accum_out=st[:, 2:3]))
            for b in range(2):
                act.wait_ge(shift_ready, 2 + b)
                o(act.activation(w[:], psc[:, 0:PAST + 1], ACT.Exp, scale=QK_SCALE, bias=st[:, 1:2],
                                 accum_out=st[:, 2:3]))

        @block.vector
        def _(dve):
            sh, o = Order(dve, dve_steps), Order(dve, dve_order)

            def do(ins):
                sh(ins)
                sh.settle()

            for ch in range(2):
                for par in range(2):
                    half = slice(par * HD, (par + 1) * HD)
                    first = ch * 2 * GQ + par * GQ
                    ins = dve.tensor_copy(q64[:].rearrange("p (s h) -> p s h", s=DEC)[:, :, first:first + GQ],
                                          qk[half, ch * GQ:(ch + 1) * GQ, SAMPLE].rearrange("p g s -> p s g"))
            o(ins)
            dve.wait_ge(pe_order, 1)
            wcf = wc[:].rearrange("p a b -> p (a b)")
            do(dve.tensor_tensor(wcf, pcs[:, 0:CMP_S], c["own_mask"][:], ALU.add))
            do(dve.tensor_reduce(st[:, 0:1], wcf, AX_X, ALU.max))
            dve.tensor_scalar(wcf, wcf, st[:, 0:1], None, ALU.subtract).then_inc(shift_ready, 1)
            dve.wait_ge(act_order, 1)
            do(dve.reciprocal(st[:, 3:4], st[:, 2:3]))
            do(dve.tensor_tensor(st[:, 3:4], st[:, 3:4], gates_s[:, 0:1], ALU.mult))
            o(dve.tensor_scalar(wcf, wcf, st[:, 3:4], None, ALU.mult))
            dve.wait_ge(pe_order, 2)
            do(dve.tensor_copy(wct[0:DEC * NCS], pct[0:DEC * NCS]))
            for b in range(2):
                dve.wait_ge(pe_order, 3 + 4 * b)
                do(dve.tensor_reduce(st[:, 0:1], psc[:, 0:PAST + 1], AX_X, ALU.max))
                dve.tensor_scalar(st[:, 1:2], st[:, 0:1], -QK_SCALE, None, ALU.mult).then_inc(shift_ready, 1)
                dve.wait_ge(act_order, 2 + b)
                do(dve.reciprocal(st[:, 3:4], st[:, 2:3]))
                do(dve.tensor_tensor(st[:, 3:4], st[:, 3:4], gates_s[:, 1 + b:2 + b], ALU.mult))
                do(dve.tensor_scalar(w[:], w[:], st[:, 3:4], None, ALU.mult))
                o(dve.tensor_scalar(wn[:], c["own_seq"][:], w[:, PAST:PAST + 1], None, ALU.mult))
                dve.wait_ge(pe_order, 3 + 4 * b + 2)
                for g in range(PAGES):
                    dve.tensor_copy(pd[:, g, :].rearrange("p (s x) -> p s x", x=DIAG)[:, :, 0:HEADS],
                                    ptr[:, g, :].rearrange("p (s h) -> p s h", s=DEC))
                o(dve.tensor_copy(wnt[:], pn[:]))
            dve.wait_ge(pe_order, 11)
            do(dve.tensor_copy(osum[:], poc[:]))
            for kv in range(KV):
                ins = dve.scalar_tensor_tensor(out=osum[:], in0=po[:, kv * HD:(kv + 1) * HD],
                                               scalar=c["own_kv"][:, kv:kv + 1], in1=osum[:], op0=ALU.mult,
                                               op1=ALU.add)
                if kv < KV - 1:
                    do(ins)
            o(ins)
            dve.wait_ge(pe_order, 12)
            for ch in range(2):
                for par in range(2):
                    half = slice(par * HD, (par + 1) * HD)
                    first = ch * 2 * GQ + par * GQ
                    dve.tensor_copy(ot[half, ch * GQ:(ch + 1) * GQ, SAMPLE],
                                    pot[:].rearrange("p (s h) -> p h s", s=DEC)[:, first:first + GQ, :])


MC = D_MODEL // P
MD = D_MODEL // MEM_HEADS
HALVES = MD // P
MEM_SCALE = MD ** -0.5
MROWS = DEC * MEM_HEADS
MDIAG = MROWS + 1


def project_mem(nc, d, c, h, mem, mk, mv, qm):
    slots, tiles = 4, 2 * MC
    with ExitStack() as ctx:
        s = Stage(nc, ctx)
        ring = s.sb("mp_ring", [P, slots, KC, P])
        wv = s.sb("mp_wv", [P, KC, D_MODEL])
        pp = s.ps("mp_pp", [P, 2, 512])
        psm = s.ps("mp_ps", [P, 2, 512])
        pv = s.ps("mp_pv", [P, 2, 512])
        landed = [s.sem(f"mp_landed{u}") for u in range(slots)]
        v_landed, stored = s.sem("mp_v_landed"), s.sem("mp_stored")
        done, evacuated, rows_done, rows_out = (s.sem("mp_" + x) for x in ("done", "evac", "rows_done", "rows_out"))
        block = ctx.enter_context(nc.Block())

        @block.sync
        def _(sp):
            stream_weights(sp, d["w_mk_qm"], ring, landed, done, tiles, slots)
            sp.dma_start(wv[:], d["w_mv"]).then_inc(v_landed, 16)
            sp.wait_ge(rows_out, 2 * (MEM // P))
            sp.dma_start(d["out_mem_v"], mv[:]).then_inc(stored, 16)
            sp.wait_ge(stored, 16)

        @block.tensor
        def _(pe):
            def chunk_tiles(first, turns, sums):
                with pe.Fori(0, turns) as i:
                    for u in range(slots):
                        pe.wait_ge(landed[u], 16 * (i + (first // slots + 1)))
                        pe.wait_ge(evacuated, i * slots + (first + u + 1))
                        for out, rhs in sums:
                            for k in range(KC):
                                mm = pe.matmul(out(u % 2), ring[:, u, k], rhs(k), start=k == 0, stop=k == KC - 1)
                        mm.then_inc(done, 1)

            chunk_tiles(0, MC // slots, [(lambda b: pp[:, b, 0:MEM], lambda k: mem[:, k, :])])
            chunk_tiles(MC, MC // slots, [(lambda b: pp[:, b, :], lambda k: h[:, k, PROMPT]),
                                          (lambda b: psm[:, b, 0:DEC], lambda k: h[:, k, SAMPLE])])
            pe.wait_ge(v_landed, 16)
            for n in range(2 * (MEM // P)):
                i, half = n // 2, n % 2
                if n >= 2:
                    pe.wait_ge(rows_out, n - 1)
                for k in range(KC):
                    mm = pe.matmul(pv[:, n % 2, :], mem[:, k, i * P:(i + 1) * P], wv[:, k, half * 512:(half + 1) * 512],
                                   start=k == 0, stop=k == KC - 1)
                mm.then_inc(rows_done, 1)

        @block.scalar
        def _(act):
            with act.Fori(0, MC // 2) as i:
                for u in range(2):
                    t = i * 2 + u
                    act.wait_ge(done, t + 1)
                    act.activation(at(mk, t), pp[:, u, 0:MEM], ACT.Copy).then_inc(evacuated, 1)
            with act.Fori(0, MC // 2) as i:
                for u in range(2):
                    t = i * 2 + u
                    act.wait_ge(done, t + (MC + 1))
                    act.activation(at(qm, t)[:, PROMPT], pp[:, u, :], ACT.Copy)
                    act.activation(at(qm, t)[:, SAMPLE], psm[:, u, 0:DEC], ACT.Copy).then_inc(evacuated, 1)

        @block.vector
        def _(dve):
            dve.memset(mv[0:1, 0, 0:1], 0.0).then_inc(evacuated, 2)
            dve.wait_ge(evacuated, 2)
            for n in range(2 * (MEM // P)):
                i, half = n // 2, n % 2
                dve.wait_ge(rows_done, n + 1)
                dve.tensor_copy(mv[:, i, half * 512:(half + 1) * 512], pv[:, n % 2, :]).then_inc(rows_out, 1)


def norm_heads(nc, d, c, mk, qm):
    with ExitStack() as ctx:
        s = Stage(nc, ctx)
        sq = s.sb("mn_sq", [P, HALVES, COLS])
        r = s.sb("mn_r", [P, COLS])
        pss = s.ps("mn_pss", [P, 2, 512])
        squared, summed, scaled, normed = (s.sem("mn_" + x) for x in ("squared", "summed", "scaled", "normed"))
        act_order, stored = s.sem("mn_act"), s.sem("mn_stored")
        block = ctx.enter_context(nc.Block())
        jobs = [(t, w, parts, hd * HALVES, gain) for t, w, parts, gain in (
            (mk, MEM, (slice(0, MEM),), c["mem_k_gain"]), (qm, COLS, (PROMPT, SAMPLE), c["mem_q_gain"]))
            for hd in range(MEM_HEADS)]

        @block.scalar
        def _(act):
            act.preload_act_table_set("natural_log_exp_and_others")
            o = Order(act, act_order)
            for j, (t, w, parts, ch, gain) in enumerate(jobs):
                act.activation(sq[:, :, 0:w], t[:, ch:ch + HALVES, :], ACT.Square).then_inc(squared, 1)
                act.wait_ge(summed, j + 1)
                if j:
                    act.wait_ge(normed, j)
                for n, part in enumerate(parts):
                    o(act.activation(r[:, part], pss[:, n, 0:part.stop - part.start], ACT.Ln, scale=1.0 / MD,
                                     bias=c["eps"][:, 0:1]))
                o.settle()
                act.activation(r[:, 0:w], r[:, 0:w], ACT.Exp, scale=-0.5).then_inc(scaled, 1)

        @block.tensor
        def _(pe):
            for j, (t, w, parts, ch, gain) in enumerate(jobs):
                pe.wait_ge(squared, j + 1)
                for n, part in enumerate(parts):
                    for k in range(HALVES):
                        mm = pe.matmul(pss[:, n, 0:part.stop - part.start], c["ones"][:], sq[:, k, part], start=k == 0,
                                       stop=k == HALVES - 1)
                mm.then_inc(summed, 1)

        @block.vector
        def _(dve):
            for j, (t, w, parts, ch, gain) in enumerate(jobs):
                dve.wait_ge(scaled, j + 1)
                for k in range(HALVES):
                    ins = dve.scalar_tensor_tensor(out=t[:, ch + k, :], in0=t[:, ch + k, :], scalar=gain[:, k:k + 1],
                                                   in1=r[:, 0:w], op0=ALU.mult, op1=ALU.mult)
                ins.then_inc(normed, 1)

        @block.sync
        def _(sp):
            sp.wait_ge(normed, MEM_HEADS)
            sp.dma_start(d["out_mem_k"], mk[:]).then_inc(stored, 16)
            sp.wait_ge(stored, 16)


def attend_prompt_mem(nc, d, c, qm, mk, mv, om):
    KB = MEM // P
    with ExitStack() as ctx:
        s = Stage(nc, ctx)
        w = s.sb("am_w", [P, TT, MEM])
        wt = s.sb("am_wt", [P, KB, SEQ])
        mx, nb, den = (s.sb("am_" + x, [P, TT]) for x in ("mx", "nb", "den"))
        psc = s.ps("am_psc", [P, TT, MEM])
        pt = s.ps("am_pt", [P, KB, SEQ])
        po = s.ps("am_po", [P, HALVES, SEQ])
        pe_order, act_order, dve_order = s.sem("am_pe"), s.sem("am_act"), s.sem("am_dve")
        block = ctx.enter_context(nc.Block())

        @block.tensor
        def _(pe):
            for hd in range(MEM_HEADS):
                ch = hd * HALVES
                if hd:
                    pe.wait_ge(act_order, 3 * hd - 2)
                for i in range(TT):
                    for k in range(HALVES):
                        mm = pe.matmul(psc[:, i, :], qm[:, ch + k, i * P:(i + 1) * P], mk[:, ch + k, :],
                                       start=k == 0, stop=k == HALVES - 1)
                mm.then_inc(pe_order, 1)
                pe.wait_ge(dve_order, 4 * hd + 4)
                for kb in range(KB):
                    for i in range(TT):
                        mm = pe.transpose(pt[:, kb, i * P:(i + 1) * P], w[:, i, kb * P:(kb + 1) * P], c["ident"][:])
                mm.then_inc(pe_order, 1)
                pe.wait_ge(act_order, 3 * hd + 2)
                for k in range(HALVES):
                    for kb in range(KB):
                        mm = pe.matmul(po[:, k, :], mv[:, kb, hd * MD + k * P:hd * MD + (k + 1) * P], wt[:, kb, :],
                                       start=kb == 0, stop=kb == KB - 1)
                mm.then_inc(pe_order, 1)

        @block.vector
        def _(dve):
            o = Order(dve, dve_order)
            for hd in range(MEM_HEADS):
                dve.wait_ge(pe_order, 3 * hd + 1)
                o(dve.tensor_reduce(mx[:], psc[:], AX_X, ALU.max))
                o.settle()
                o(dve.tensor_scalar(nb[:], mx[:], -MEM_SCALE, None, ALU.mult))
                dve.wait_ge(act_order, 3 * hd + 1)
                o(dve.reciprocal(den[:], den[:]))
                o.settle()
                o(dve.tensor_tensor(w[:], w[:], den[:].unsqueeze(2).broadcast_to([P, TT, MEM]), ALU.mult))

        @block.scalar
        def _(act):
            act.preload_act_table(ACT.Exp)
            for hd in range(MEM_HEADS):
                act.wait_ge(dve_order, 4 * hd + 2)
                if hd:
                    act.wait_ge(pe_order, 3 * hd - 1)
                for i in range(TT):
                    ins = act.activation(w[:, i, :], psc[:, i, :], ACT.Exp, scale=MEM_SCALE, bias=nb[:, i:i + 1],
                                         accum_out=den[:, i:i + 1])
                ins.then_inc(act_order, 1)
                act.wait_ge(pe_order, 3 * hd + 2)
                for kb in range(KB):
                    ins = act.copy(wt[:, kb, :], pt[:, kb, :])
                ins.then_inc(act_order, 1)
                act.wait_ge(pe_order, 3 * hd + 3)
                for k in range(HALVES):
                    ins = act.copy(om[:, hd * HALVES + k, PROMPT], po[:, k, :])
                ins.then_inc(act_order, 1)


def attend_sample_mem(nc, d, c, qm, om):
    slots = 2
    with ExitStack() as ctx:
        s = Stage(nc, ctx)
        qd = s.sb("sm_qd", [P, HALVES, MROWS * MDIAG])
        wd = s.sb("sm_wd", [P, MEM // P, MROWS * MDIAG])
        ring = s.sb("sm_ring", [P, slots, MC, MEM])
        w = s.sb("sm_w", [MROWS, MEM])
        st = s.sb("sm_st", [MROWS, 4])
        orow = s.sb("sm_orow", [MROWS, MD])
        psc = s.ps("sm_psc", [MROWS, MEM])
        pt = s.ps("sm_pt", [P, MEM // P, MROWS])
        po = s.ps("sm_po", [MROWS, MD])
        pot = s.ps("sm_pot", [P, HALVES, MROWS])
        landed = [s.sem(f"sm_landed{u}") for u in range(slots)]
        used, pe_order, act_order, dve_order, zeroed = (s.sem("sm_" + x) for x in ("used", "pe", "act", "dve", "zeroed"))
        dve_steps, shift_ready = s.sem("sm_dve_steps"), s.sem("sm_shift_ready")
        block = ctx.enter_context(nc.Block())

        @block.gpsimd
        def _(pool):
            pool.memset(qd[:], 0.0).then_inc(zeroed, 1)
            pool.memset(wd[:], 0.0).then_inc(zeroed, 1)

        @block.sync
        def _(sp):
            for u in range(slots):
                sp.dma_start(ring[:, u], d["mem_kv"][u]).then_inc(landed[u], 16)
            with sp.Fori(0, 2 * DEC // slots - 1) as i:
                for u in range(slots):
                    sp.wait_ge(used, i * slots + (u + 1))
                    sp.dma_start(ring[:, u], d["mem_kv"][bass.ds(i * slots + (u + slots), 1)].rearrange(
                        "a p k n -> (a p) k n")).then_inc(landed[u], 16)

        @block.tensor
        def _(pe):
            ident = c["ident"]

            def rows(t, n, r):
                return t[:, n, 0:MROWS * MROWS].rearrange("p (a b) -> p a b", a=MROWS)[:, r, :]

            pe.wait_ge(act_order, 1)
            for q in range(DEC):
                pe.wait_ge(landed[q % slots], 16 * (q // slots + 1))
                for hd in range(MEM_HEADS):
                    for k in range(HALVES):
                        mm = pe.matmul(psc[:], rows(qd, k, q * MEM_HEADS + hd), ring[:, q % slots, hd * HALVES + k, :],
                                       start=q == 0 and hd == 0 and k == 0,
                                       stop=q == DEC - 1 and hd == MEM_HEADS - 1 and k == HALVES - 1)
                mm.then_inc(used, 1)
            pe.wait_ge(dve_order, 1)
            for g in range(MEM // P):
                mm = pe.transpose(pt[:, g, :], w[:, g * P:(g + 1) * P], ident[0:MROWS, 0:MROWS])
            mm.then_inc(pe_order, 1)
            pe.wait_ge(act_order, 3)
            for q in range(DEC):
                pe.wait_ge(landed[q % slots], 16 * (DEC // slots + q // slots + 1))
                vq = ring[:, q % slots].rearrange("p (g h) n -> p g h n", g=MEM // P)
                for hd in range(MEM_HEADS):
                    for g in range(MEM // P):
                        mm = pe.matmul(po[:], rows(wd, g, q * MEM_HEADS + hd), vq[:, g, hd, :],
                                       start=q == 0 and hd == 0 and g == 0,
                                       stop=q == DEC - 1 and hd == MEM_HEADS - 1 and g == MEM // P - 1)
                mm.then_inc(used, 1)
            pe.wait_ge(dve_order, 2)
            for k in range(HALVES):
                mm = pe.transpose(pot[:, k, :], orow[:, k * P:(k + 1) * P], ident[0:MROWS, 0:MROWS])
            mm.then_inc(pe_order, 1)

        @block.scalar
        def _(act):
            act.preload_act_table(ACT.Exp)
            act.wait_ge(zeroed, 2)
            for k in range(HALVES):
                dst = qd[:, k, :].rearrange("p (s h x) -> p s h x", s=DEC, h=MEM_HEADS)[:, :, :, 0]
                src = qm[:].rearrange("p (h k) n -> p k h n", k=HALVES)[:, k, :, SAMPLE].rearrange("p h s -> p s h")
                ins = act.copy(dst, src)
            ins.then_inc(act_order, 1)
            act.wait_ge(shift_ready, 1)
            act.activation(w[:], psc[:], ACT.Exp, scale=MEM_SCALE, bias=st[:, 1:2],
                           accum_out=st[:, 2:3]).then_inc(act_order, 1)
            act.wait_ge(pe_order, 1)
            for g in range(MEM // P):
                ins = act.copy(wd[:, g, :].rearrange("p (r x) -> p r x", x=MDIAG)[:, :, 0], pt[:, g, :])
            ins.then_inc(act_order, 1)

        @block.vector
        def _(dve):
            o = Order(dve, dve_steps)

            def do(ins):
                o(ins)
                o.settle()

            dve.wait_ge(used, DEC)
            do(dve.tensor_reduce(st[:, 0:1], psc[:], AX_X, ALU.max))
            dve.tensor_scalar(st[:, 1:2], st[:, 0:1], -MEM_SCALE, None, ALU.mult).then_inc(shift_ready, 1)
            dve.wait_ge(act_order, 2)
            do(dve.reciprocal(st[:, 3:4], st[:, 2:3]))
            dve.tensor_scalar(w[:], w[:], st[:, 3:4], None, ALU.mult).then_inc(dve_order, 1)
            dve.wait_ge(used, 2 * DEC)
            dve.tensor_copy(orow[:], po[:]).then_inc(dve_order, 1)
            dve.wait_ge(pe_order, 2)
            for k in range(HALVES):
                dve.tensor_copy(om[:].rearrange("p (h k) n -> p k h n", k=HALVES)[:, k, :, SAMPLE],
                                pot[:, k, :].rearrange("p (s h) -> p h s", s=DEC))


def project_add(nc, d, c, name, w_dram, kin, slots, src, res, dst, out):
    with ExitStack() as ctx:
        s = Stage(nc, ctx)
        ring = s.sb(name + "_ring", [P, slots, kin, P])
        pp = s.ps(name + "_pp", [P, 2, 512])
        psm = s.ps(name + "_ps", [P, 2, 512])
        landed = [s.sem(f"{name}_landed{u}") for u in range(slots)]
        done, evacuated, stored = (s.sem(name + x) for x in ("_done", "_evacuated", "_stored"))
        block = ctx.enter_context(nc.Block())

        @block.sync
        def _(sp):
            stream_weights(sp, w_dram, ring, landed, done, KC, slots)
            if out is not None:
                sp.wait_ge(evacuated, 2 + KC)
                sp.dma_start(out, dst[:]).then_inc(stored, 16)
                sp.wait_ge(stored, 16)

        @block.tensor
        def _(pe):
            multiply_tiles(pe, ring, landed, evacuated, done, KC, slots, [
                (lambda b: pp[:, b, :], range(kin), lambda k: src[:, k, PROMPT]),
                (lambda b: psm[:, b, 0:DEC], range(kin), lambda k: src[:, k, SAMPLE])])

        @block.vector
        def _(dve):
            dve.memset(dst[0:1, 0, 0:1], 0.0).then_inc(evacuated, 2)
            dve.wait_ge(evacuated, 2)
            with dve.Fori(0, KC // 2) as i:
                for u in range(2):
                    t = i * 2 + u
                    dve.wait_ge(done, t + 1)
                    dve.tensor_tensor(at(dst, t)[:, PROMPT], pp[:, u, :], at(res, t)[:, PROMPT], ALU.add)
                    dve.tensor_tensor(at(dst, t)[:, SAMPLE], psm[:, u, 0:DEC], at(res, t)[:, SAMPLE],
                                      ALU.add).then_inc(evacuated, 1)


def expand_ffn(nc, d, c, h, act_t):
    slots = 2
    with ExitStack() as ctx:
        s = Stage(nc, ctx)
        ring = s.sb("up_ring", [P, slots, 2 * KC, P])
        pad = s.sb("up_pad", [P, 2, 2, FCONV - 1 + SEQ])
        acc = s.sb("up_acc", [P, 2, 2, COLS])
        prod = s.sb("up_prod", [P, 2, 2, DEC, FCONV])
        sil = s.sb("up_sil", [P, 2, COLS])
        tails = s.sb("up_tails", [P, FC, 2, FCONV - 1])
        conv_s = s.sb("up_conv_s", [P, FC, 2, DEC * FCONV])
        pp = s.ps("up_pp", [P, 2, 2, 512])
        psm = s.ps("up_ps", [P, 2, 512])
        landed = [s.sem(f"up_landed{u}") for u in range(slots)]
        done, evacuated, convolved, silued, dve_order, state_landed, stored = (
            s.sem("up_" + x) for x in ("done", "evacuated", "convolved", "silued", "dve", "state_landed", "stored"))
        PER_HALF = 1 + 1 + (FCONV - 1) + 1 + 1 + 1
        TURN = 2 * (2 * PER_HALF - 1 + 1)
        block = ctx.enter_context(nc.Block())

        @block.sync
        def _(sp):
            sp.dma_start(conv_s[:], d["ffn_state"]).then_inc(state_landed, 16)
            stream_weights(sp, d["w_up"], ring, landed, done, FC, slots)
            sp.wait_ge(dve_order, TURN * FC // 2)
            sp.dma_start(d["out_p_ffn"], tails[:]).then_inc(stored, 16)
            sp.dma_start(d["out_s_ffn"], conv_s[:]).then_inc(stored, 16)
            sp.wait_ge(stored, 32)

        @block.tensor
        def _(pe):
            multiply_tiles(pe, ring, landed, evacuated, done, FC, slots, [
                (lambda b: pp[:, b, 0, :], range(KC), lambda k: h[:, k, PROMPT]),
                (lambda b: pp[:, b, 1, :], range(KC, 2 * KC), lambda k: h[:, k, PROMPT]),
                (lambda b: psm[:, b, 0:DEC], range(KC), lambda k: h[:, k, SAMPLE]),
                (lambda b: psm[:, b, DEC:2 * DEC], range(KC, 2 * KC), lambda k: h[:, k, SAMPLE])])

        @block.scalar
        def _(act):
            act.preload_act_table(ACT.Silu)
            act.wait_ge(state_landed, 16)
            with act.Fori(0, FC // 2) as i:
                for u in range(2):
                    t = i * 2 + u
                    act.wait_ge(done, t + 1)
                    act.wait_ge(convolved, t + 1)
                    act.copy(pad[:, u, :, FCONV - 1:], pp[:, u])
                    act.copy(conv_s[:, bass.ds(t, 1), :, :].rearrange("p a m (s k) -> p (a m) s k", k=FCONV)[
                        :, :, :, FCONV - 1], psm[:, u, 0:2 * DEC].rearrange("p (m s) -> p m s", m=2)).then_inc(evacuated, 1)
                    act.wait_ge(convolved, t + 3)
                    act.activation(sil[:, u, :], acc[:, u, 0, :], ACT.Silu).then_inc(silued, 1)

        @block.vector
        def _(dve):
            o = Order(dve, dve_order)
            dve.memset(pad[:, :, :, 0:FCONV - 1], 0.0).then_inc(evacuated, 2)
            dve.memset(acc[:], 0.0).then_inc(convolved, 2)
            dve.wait_ge(convolved, 2)
            with dve.Fori(0, FC // 2) as i:
                o.enter(i, TURN)
                for u in range(2):
                    t = i * 2 + u
                    dve.wait_ge(evacuated, t + 3)
                    wt = at(c["ffn_conv_w"], t)
                    cs = conv_s[:, bass.ds(t, 1), :, :].rearrange("p a m (s k) -> p (a m) s k", k=FCONV)
                    for m in range(2):
                        tap = lambda k: wt[:, m * (FCONV + 1) + k:m * (FCONV + 1) + k + 1]
                        taps = wt[:, m * (FCONV + 1):m * (FCONV + 1) + FCONV]
                        o(dve.tensor_scalar(acc[:, u, m, PROMPT], pad[:, u, m, 0:SEQ], tap(0), tap(FCONV), ALU.mult,
                                            ALU.add))
                        o(dve.tensor_tensor(prod[:, u, m], cs[:, m], taps.unsqueeze(1).broadcast_to([P, DEC, FCONV]),
                                            ALU.mult))
                        for k in range(1, FCONV):
                            o.settle()
                            o(dve.scalar_tensor_tensor(out=acc[:, u, m, PROMPT], in0=pad[:, u, m, k:k + SEQ],
                                                       scalar=tap(k), in1=acc[:, u, m, PROMPT], op0=ALU.mult,
                                                       op1=ALU.add))
                        o(dve.tensor_reduce(acc[:, u, m, SAMPLE], prod[:, u, m], AX_X, ALU.add))
                        o(dve.tensor_copy(tails[:, bass.ds(t, 1), m, :].rearrange("p a k -> p (a k)"),
                                          pad[:, u, m, SEQ:]))
                        o.settle()
                        ins = dve.tensor_scalar(acc[:, u, m, SAMPLE], acc[:, u, m, SAMPLE], tap(FCONV), None, ALU.add)
                        if m == 0:
                            o(ins)
                        else:
                            ins.then_inc(convolved, 1)
                    dve.wait_ge(silued, t + 1)
                    o(dve.tensor_tensor(at(act_t, t), sil[:, u, :], acc[:, u, 1, :], ALU.mult))
                o.leave(FC // 2)


def copy_windows(nc, d):
    with ExitStack() as ctx:
        s = Stage(nc, ctx)
        stored = s.sem("cw_stored")
        block = ctx.enter_context(nc.Block())

        @block.sync
        def _(sp):
            sp.dma_start(d["out_win_k"], d["win_k_rows"]).then_inc(stored, 16)
            sp.dma_start(d["out_win_v"], d["win_v_rows"]).then_inc(stored, 16)
            sp.wait_ge(stored, 32)


CONSTANTS = {
    "ident": [P, P], "ones": [P, P], "head_ones": [P, P], "rotate": [P, P], "tri": [P, P], "ssd_mask": [P, P],
    "causal": [P, P], "cmp_mask": [P, TT, NCP], "cos": [P, COLS], "sin": [P, COLS], "expand": [SSD_HEADS, D_INNER],
    "own_mask": [P, CMP_S], "own_seq": [P, DEC], "own_kv": [P, KV], "eps": [P, 1],
    "cmp_cos": [P, CMP_P + CMP_S], "cmp_sin": [P, CMP_P + CMP_S],
    "norm_mix": [P, KC], "norm_ffn": [P, KC], "mem_norm": [P, KC], "b_merge": [P, 3 * KC],
    "ssd_conv_w": [P, XBC, CONV], "ssd_conv_b": [P, XBC], "ssd_dt_bias": [SSD_HEADS, 1], "ssd_a_log": [SSD_HEADS, 1],
    "ssd_d": [P, DI], "ssd_norm": [P, DI], "head_gain": [P, NR], "cmp_gain": [P, 1],
    "mem_k_gain": [P, HALVES], "mem_q_gain": [P, HALVES], "ffn_conv_w": [P, FC, 2 * (FCONV + 1)],
}

OUTPUTS = {
    "out_y": [P, KC, COLS], "out_cmp": [P, 4, COLS], "out_v": [P, TT, 2 * KV * HD], "out_v_s": [DEC, 2 * KV * HD],
    "out_k": [P, KV, COLS], "out_p_conv": [P, XBC, CONV - 1], "out_s_conv": [P, XBC, DEC, CONV],
    "out_p_ssd": [P, GROUPS, HPG * HEAD_P], "out_s_ssd": [DEC, P, DI, STATE],
    "out_p_ffn": [P, FC, 2, FCONV - 1], "out_s_ffn": [P, FC, 2, DEC * FCONV],
    "out_mem_k": [P, MC, MEM], "out_mem_v": [P, MEM // P, D_MODEL],
    "out_win_k": [DEC, PAST * KV * HD], "out_win_v": [DEC, PAST * KV * HD],
}


def load_columns(nc, name, pairs):
    with ExitStack() as ctx:
        s = Stage(nc, ctx)
        landed = s.sem(name + "_landed")
        block = ctx.enter_context(nc.Block())

        @block.sync
        def _(sp):
            for dst, src in pairs:
                sp.dma_start(dst[:], src).then_inc(landed, 16)
            sp.wait_ge(landed, 16 * len(pairs))


def build_layer(nc, d):
    both = (PROMPT, SAMPLE)
    Stage.taken.clear()
    with ExitStack() as whole:
        top = Stage(nc, whole)
        c = {n: top.sb("c_" + n, shape) for n, shape in CONSTANTS.items()}
        h, mixed = top.sb("h", [P, KC, COLS]), top.sb("mixed", [P, KC, COLS])
        load_constants(nc, d, c)
        with ExitStack() as ctx:
            x = Stage(nc, ctx).sb("x", [P, KC, COLS])
            load_columns(nc, "x", [(x, d["x"])])
            norm_columns(nc, "nx", x, h, c["norm_mix"], c["ones"], c["eps"], KC, both, COLS)

        with ExitStack() as ctx:
            s = Stage(nc, ctx)
            zt, r = s.sb("zt", [P, DI, COLS]), s.sb("zr", [P, COLS])
            with ExitStack() as inner:
                s = Stage(nc, inner)
                xbct = s.sb("xbct", [P, XBC, COLS])
                dts, dt_raw = s.sb("dts", [SSD_HEADS, COLS]), s.sb("dt_raw", [SSD_HEADS, COLS])
                ec, wend, cdec, negcum, dtr = (s.sb("t_" + n, [P, TT, SSD_HEADS]) for n in (
                    "ec", "wend", "cdec", "negcum", "dtr"))
                cumt = s.sb("cumt", [SSD_HEADS, SEQ])
                dxs = s.sb("dxs", [P, DI, 2, DEC])
                project_ssd(nc, d, c, h, zt, xbct, dt_raw)
                step_sizes(nc, d, c, dt_raw, dts, ec, wend, cdec, negcum, dtr, cumt, dxs)
                scan_prompt(nc, d, c, xbct, zt, dtr, ec, wend, cdec, negcum, cumt, mixed)
                scan_sample(nc, d, c, xbct, zt, dxs)
            gain_and_square(nc, c, zt, r)
            merge_branch(nc, d, c, "ms", 0, d["w_ssd_merge"], zt, DI, h, mixed, r)

        with ExitStack() as ctx:
            s = Stage(nc, ctx)
            ot = s.sb("ot", [P, KC, COLS])
            with ExitStack() as inner:
                s = Stage(nc, inner)
                qk = s.sb("qk", [P, NR + 4, COLS])
                vr = s.sb("vr", [P, TT + 1, 2 * KV * HD])
                gates, gates_s = s.sb("gates", [P, TT, 3 * HEADS]), s.sb("gates_s", [ROWS, 3])
                kct, vcp, vcs = s.sb("kct", [P, CMP_P + CMP_S]), s.sb("vcp", [P, KV, HD]), s.sb("vcs", [P, KV, HD])
                project_nsa(nc, d, c, h, qk, vr, gates, gates_s)
                rotate_tiles(nc, d, c, qk)
                compress_rows(nc, d, c, qk, kct, vcp, vcs)
                attend_prompt(nc, d, c, qk, vr, gates, kct, vcp, ot)
                attend_sample_nsa(nc, d, c, qk, vr, gates_s, kct, vcs, ot)
            merge_branch(nc, d, c, "mn", 1, d["w_nsa_merge"], ot, KC, h, mixed, None)
        Stage.retire_semaphores(nc)

        with ExitStack() as ctx:
            s = Stage(nc, ctx)
            om = s.sb("om", [P, KC, COLS])
            with ExitStack() as inner:
                s = Stage(nc, inner)
                mem, mk, mv = s.sb("mem", [P, KC, MEM]), s.sb("mk", [P, MC, MEM]), s.sb("mv", [P, MEM // P, D_MODEL])
                qm = s.sb("qm", [P, MC, COLS])
                load_columns(nc, "mem", [(mem, d["mem"])])
                norm_columns(nc, "nm", mem, mem, c["mem_norm"], c["ones"], c["eps"], KC, (slice(0, MEM),), MEM)
                project_mem(nc, d, c, h, mem, mk, mv, qm)
                norm_heads(nc, d, c, mk, qm)
                attend_prompt_mem(nc, d, c, qm, mk, mv, om)
                attend_sample_mem(nc, d, c, qm, om)
            merge_branch(nc, d, c, "mm", 2, d["w_mem_merge"], om, KC, h, mixed, None)

        with ExitStack() as ctx:
            s = Stage(nc, ctx)
            x = s.sb("x_again", [P, KC, COLS])
            act_t = s.sb("act_t", [P, FC, COLS])
            load_columns(nc, "x_again", [(x, d["x"])])
            project_add(nc, d, c, "po", d["w_out"], KC, 4, mixed, x, h, None)
            norm_columns(nc, "nf", h, mixed, c["norm_ffn"], c["ones"], c["eps"], KC, both, COLS)
            expand_ffn(nc, d, c, mixed, act_t)
            project_add(nc, d, c, "pd", d["w_down"], FC, 2, act_t, h, x, d["out_y"])
        copy_windows(nc, d)


def tiles(w):
    k, m = w.shape
    return w.reshape(k // P, P, m // P, P).transpose(2, 1, 0, 3)


def columns(v):
    return v.reshape(-1, P).T


def rows_of(w):
    return w.reshape(-1, P, w.shape[1]).transpose(1, 0, 2)


def constants():
    f = np.float32
    i = np.arange(P)
    pos = np.concatenate([np.arange(SEQ), np.full(DEC, PAST)]).astype(f)
    inv = (f(10000.0) ** (-np.arange(HD // 2, dtype=f) / f(HD // 2))).astype(f)
    of_row = inv[i % (HD // 2)][:, None]
    cmp_pos = np.concatenate([np.tile(np.arange(NCP), KV), np.tile(np.arange(NCS), KV * DEC)]) * CMP_STRIDE + CMP_LEN - 1
    ang, cang = of_row * pos[None, :], of_row * cmp_pos.astype(f)[None, :]
    rotate = np.zeros((P, P), f)
    for m in range(P):
        if m % HD < HD // 2:
            rotate[m + HD // 2, m] = -1
        else:
            rotate[m - HD // 2, m] = 1
    t = np.arange(SEQ).reshape(TT, P).T[:, :, None]
    end = np.arange(NCP) * CMP_STRIDE + CMP_LEN - 1
    sq, hd = np.divmod(np.arange(ROWS), HEADS)
    own = (sq[:, None, None] == np.arange(DEC)[None, None, :]) & (hd[:, None, None] // GQ == np.arange(KV)[None, :, None])
    return {
        "ident": np.eye(P, dtype=f), "ones": np.ones((P, P), f),
        "head_ones": (i[:, None] // HD == i[None, :] // HD).astype(f), "rotate": rotate,
        "tri": (i[:, None] <= i[None, :]).astype(f),
        "ssd_mask": np.where(i[:, None] <= i[None, :], 0, NEG).astype(f),
        "causal": np.where(i[None, :] <= i[:, None], 0, NEG).astype(f),
        "cmp_mask": np.where(end[None, None, :] <= t, 0, NEG).astype(f),
        "cos": np.cos(ang).astype(f), "sin": np.sin(ang).astype(f),
        "cmp_cos": np.cos(cang).astype(f), "cmp_sin": np.sin(cang).astype(f),
        "expand": (np.arange(SSD_HEADS)[:, None] == np.arange(D_INNER)[None, :] // HEAD_P).astype(f),
        "own_mask": np.repeat(np.where(own, 0, NEG).astype(f).reshape(ROWS, -1), NCS, axis=1),
        "own_seq": (sq[:, None] == np.arange(DEC)[None, :]).astype(f),
        "own_kv": (hd[:, None] // GQ == np.arange(KV)[None, :]).astype(f),
        "eps": np.full((P, 1), EPS, f),
    }


def by_pair(pool):
    lead = pool.shape[:-3]
    n = len(lead)
    a = pool.reshape(lead + (pool.shape[-3], KV // 2, 2, HD))
    a = a.transpose(tuple(range(n)) + (n + 2, n + 3, n + 1, n))
    return a.reshape(lead + (P, KV // 2, pool.shape[-3]))


def lay_out(v):
    f = {n: np.asarray(a)[0] if np.asarray(a).ndim and n not in (
        "x_prompt", "x_sample", "page_table", "mem_prompt") else np.asarray(a) for n, a in v.items()}
    cut = np.cumsum([D_INNER, XBC * P, SSD_HEADS, HEADS * HD, 6 * KV * HD, 3 * HEADS, D_MODEL])
    wz, wxbc, wdt, wq, wkv, wg, wqm, wm = np.split(f["w_in"], cut, axis=1)
    order = [2 * GQ * ch + GQ * par + g for ch in range(2) for g in range(GQ) for par in range(2)]
    wq = wq.reshape(D_MODEL, HEADS, HD)[:, order].reshape(D_MODEL, HEADS * HD)
    w_nsa_o = f["w_nsa_o"].reshape(HEADS, HD, D_MODEL)[order].reshape(HEADS * HD, D_MODEL)
    ck, cv, sk, sv, wk, wv = np.split(wkv, 6, axis=1)
    merge = [wm[:, n * D_MODEL:(n + 1) * D_MODEL] for n in range(3)]
    mem_k = f["cache_mem_k"].reshape(DEC, MEM, MC, P).transpose(0, 3, 2, 1)
    mem_v = f["cache_mem_v"].reshape(DEC, MEM // P, P, MEM_HEADS, MD).transpose(0, 2, 1, 3, 4).reshape(DEC, P, MC, MEM)
    state = f["state_ssd"].reshape(DEC, DI, 2, HEAD_P, STATE).transpose(0, 2, 3, 1, 4).reshape(DEC, P, DI, STATE)
    conv = np.zeros((P, XBC, DEC, CONV), np.float32)
    conv[..., :CONV - 1] = f["state_ssd_conv"].reshape(DEC, CONV - 1, XBC, P).transpose(3, 2, 0, 1)
    ffn = np.zeros((P, FC, 2, DEC, FCONV), np.float32)
    ffn[..., :FCONV - 1] = f["state_ffn_conv"].reshape(DEC, FCONV - 1, 2, FC, P).transpose(4, 3, 2, 0, 1)
    taps = np.concatenate([f["ffn_conv_w"], f["ffn_conv_b"][None]]).reshape(FCONV + 1, 2, FC, P).transpose(3, 2, 1, 0)
    q_gain, k_gain = f["nsa_q_norm"], f["nsa_k_norm"]
    win_k, win_v = f["state_nsa_win_k"], f["state_nsa_win_v"]
    pe = [f["cmp_k_pe"], f["cmp_v_pe"]]
    a = {
        "x": np.concatenate([f["x_prompt"][0], f["x_sample"][:, 0]]).T.reshape(KC, P, COLS).transpose(1, 0, 2),
        "mem": f["mem_prompt"][0].T.reshape(KC, P, MEM).transpose(1, 0, 2),
        "w_zxbc": tiles(np.concatenate([wz, wxbc], axis=1)), "w_dt": rows_of(wdt),
        "w_ssd_merge": np.concatenate([tiles(f["w_ssd_o"]), tiles(merge[0])], axis=2),
        "w_qk": tiles(np.concatenate([wq, sk, wk, ck, cv], axis=1)),
        "w_v": rows_of(np.concatenate([sv, wv], axis=1)), "w_gates": rows_of(wg),
        "w_nsa_merge": np.concatenate([tiles(w_nsa_o), tiles(merge[1])], axis=2),
        "w_mk_qm": tiles(np.concatenate([f["w_mem_kv"][:, :D_MODEL], wqm], axis=1)),
        "w_mv": rows_of(f["w_mem_kv"][:, D_MODEL:]),
        "w_mem_merge": np.concatenate([tiles(f["w_mem_o"]), tiles(merge[2])], axis=2),
        "w_out": tiles(f["w_out"]),
        "w_up": np.concatenate([tiles(f["w_up"][:, :D_FF]), tiles(f["w_up"][:, D_FF:])], axis=2),
        "w_down": tiles(f["w_down"]),
        "ssd_state": state, "ssd_state_conv": conv, "ffn_state": ffn.reshape(P, FC, 2, DEC * FCONV),
        "pool_cmp_k": f["cache_nsa_cmp_k"].transpose(0, 3, 2, 1), "pool_cmp_v": f["cache_nsa_cmp_v"].transpose(0, 3, 2, 1),
        "pool_sel_k": by_pair(f["cache_nsa_sel_k"]),
        "pool_sel_v": f["cache_nsa_sel_v"].reshape(-1, PAGE, KV * HD),
        "win_k": by_pair(win_k).transpose(1, 2, 0, 3),
        "win_v": win_v.reshape(DEC, PAGES, P, KV * HD).transpose(2, 0, 1, 3),
        "win_k_rows": win_k.reshape(DEC, -1), "win_v_rows": win_v.reshape(DEC, -1),
        "cmp_w1": np.stack([f[n].reshape(CMP_LEN // 2, P, P).transpose(1, 0, 2) for n in ("cmp_k_w1", "cmp_v_w1")], 1),
        "cmp_w2": np.stack([np.tile(f[n], (1, 2)) for n in ("cmp_k_w2", "cmp_v_w2")], 1),
        "cmp_pe": np.stack([p.reshape(CMP_LEN // 2, P).T for p in pe], 1),
        "page_table": f["page_table"].reshape(1, -1).astype(np.int32),
        "mem_kv": np.concatenate([mem_k, mem_v]),
        "norm_mix": columns(f["norm_mix"]), "norm_ffn": columns(f["norm_ffn"]), "mem_norm": columns(f["mem_norm"]),
        "b_merge": columns(f["b_merge"].reshape(-1)),
        "ssd_conv_w": f["ssd_conv_w"].reshape(CONV, XBC, P).transpose(2, 1, 0), "ssd_conv_b": columns(f["ssd_conv_b"]),
        "ssd_dt_bias": f["ssd_dt_bias"][:, None], "ssd_a_log": f["ssd_a_log"][:, None],
        "ssd_d": columns(np.repeat(f["ssd_d"], HEAD_P)), "ssd_norm": columns(f["ssd_norm"]),
        "head_gain": np.stack([np.tile(g, 2) for g in [q_gain] * NQ + [k_gain[1]] * 2 + [k_gain[2]] * 2], 1),
        "cmp_gain": np.tile(k_gain[0], 2)[:, None],
        "mem_k_gain": columns(f["mem_k_norm"]), "mem_q_gain": columns(f["mem_q_norm"]),
        "ffn_conv_w": taps.reshape(P, FC, 2 * (FCONV + 1)),
    }
    a.update(constants())
    return {n: np.ascontiguousarray(x) for n, x in a.items()}


def channels(a):
    return a.transpose(2, 1, 0).reshape(a.shape[2], -1)


def rows_by_kv(a):
    return a.reshape(2, HD, KV // 2, -1).transpose(3, 2, 0, 1).reshape(-1, KV, HD)


def take_apart(o):
    y = channels(o["out_y"])
    cmp_k, cmp_v = rows_by_kv(o["out_cmp"][:, 0:2]), rows_by_kv(o["out_cmp"][:, 2:4])
    sel_k, win_k = rows_by_kv(o["out_k"][:, 0:2]), rows_by_kv(o["out_k"][:, 2:4])
    v = o["out_v"].transpose(1, 0, 2).reshape(SEQ, 2, KV, HD)
    v_s = o["out_v_s"].reshape(DEC, 2, KV, HD)
    p_conv = channels(o["out_p_conv"])
    s_conv = o["out_s_conv"][..., 1:].transpose(2, 3, 1, 0).reshape(DEC, CONV - 1, XBC * P)
    p_ssd = o["out_p_ssd"].reshape(STATE, GROUPS * HPG, HEAD_P).transpose(1, 2, 0)
    s_ssd = o["out_s_ssd"].reshape(DEC, 2, HEAD_P, DI, STATE).transpose(0, 3, 1, 2, 4).reshape(
        DEC, SSD_HEADS, HEAD_P, STATE)
    p_ffn = o["out_p_ffn"].transpose(3, 2, 1, 0).reshape(FCONV - 1, 2 * D_FF)
    s_ffn = o["out_s_ffn"].reshape(P, FC, 2, DEC, FCONV)[..., 1:].transpose(3, 4, 2, 1, 0).reshape(
        DEC, FCONV - 1, 2 * D_FF)
    mem_k = channels(o["out_mem_k"]).reshape(MEM, MEM_HEADS, MD)
    mem_v = o["out_mem_v"].transpose(1, 0, 2).reshape(MEM, MEM_HEADS, MD)
    s_win = [np.concatenate([o[n].reshape(DEC, PAST, KV, HD), new[:, None]], axis=1)
             for n, new in (("out_win_k", win_k[SEQ:]), ("out_win_v", v_s[:, 1]))]
    p = [cmp_k[:SEQ], cmp_v[:SEQ], sel_k[:SEQ], v[:, 0], win_k[:SEQ], v[:, 1], p_conv, p_ssd, p_ffn, mem_k, mem_v]
    s = [cmp_k[SEQ:][:, None], cmp_v[SEQ:][:, None], sel_k[SEQ:][:, None], v_s[:, 0][:, None], s_win[0], s_win[1],
         s_conv, s_ssd, s_ffn]
    return tuple([y[None, :SEQ], y[SEQ:, None]] + [a[None, None] for a in p] + [a[None] for a in s])


def build_program(nc, arrays):
    d = {n: nc.dram_tensor("in_" + n, a.shape, mybir.dt.from_np(a.dtype), kind="ExternalInput").ap()
         for n, a in arrays.items()}
    for n, shape in OUTPUTS.items():
        d[n] = nc.dram_tensor(n, shape, F32, kind="ExternalOutput").ap()
    d["gates_turn"] = nc.dram_tensor("gates_turn", [DEC, 3 * HEADS], F32, kind="Internal").ap()
    build_layer(nc, d)


def kernel(**inputs):
    import concourse.bacc as bacc
    from concourse.bass_utils import run_bass_kernel_spmd

    nc = bacc.Bacc("TRN2", target_bir_lowering=False, num_devices=1)
    arrays = lay_out(inputs)
    build_program(nc, arrays)
    r = run_bass_kernel_spmd(nc, [{"in_" + n: a for n, a in arrays.items()}], core_ids=[0])
    return take_apart({n: r.results[0][n] for n in OUTPUTS})
```

```python
from contextlib import ExitStack

import numpy as np

import concourse.bass as bass
from concourse import mybir

F32 = mybir.dt.float32
F32R = mybir.dt.float32r
I32 = mybir.dt.int32
ACT = mybir.ActivationFunctionType
ALU = mybir.AluOpType
AX_X = mybir.AxisListType.X

P = 128
D_MODEL = 1024
SEQ = 512
DEC = 8
COLS = SEQ + DEC
PAST = 256
PAGE = 128
PAGES = PAST // PAGE
KC = D_MODEL // P
TT = SEQ // P
D_INNER = 2048
DI = D_INNER // P
SSD_HEADS = 32
GROUPS = 4
HPG = SSD_HEADS // GROUPS
HEAD_P = 64
STATE = 128
CONV = 4
XBC = (D_INNER + 2 * GROUPS * STATE) // P
HEADS = 16
KV = 4
GQ = HEADS // KV
HD = 64
CMP_LEN = 32
CMP_STRIDE = 16
NCP = SEQ // CMP_STRIDE - 1
NCS = PAST // CMP_STRIDE - 1
MEM = 256
MEM_HEADS = 4
D_FF = 2816
FC = D_FF // P
FCONV = 3
EPS = 1e-6
NEG = -1.0e30
FLOOR = -1.0e20
ROWS = DEC * HEADS
DIAG = P + HEADS

PROMPT = slice(0, SEQ)
SAMPLE = slice(SEQ, COLS)


class Order:

    def __init__(self, eng, sem):
        self.eng, self.sem, self.base, self.n = eng, sem, 0, 0

    def __call__(self, instruction):
        instruction.then_inc(self.sem, 1)
        self.n += 1

    def settle(self):
        self.eng.wait_ge(self.sem, self.base + self.n)

    def enter(self, i, per, first=0):
        self.start, self.per = self.base + self.n - first * per, per
        self.base, self.n = self.start + i * per, 0

    def leave(self, turns):
        assert self.n == self.per, (self.n, self.per)
        self.base, self.n = self.start + turns * self.per, 0


class Stage:

    taken = []

    def __init__(self, nc, ctx):
        self.nc, self.ctx = nc, ctx

    def sb(self, name, shape, dt=F32):
        return self.ctx.enter_context(self.nc.sbuf_tensor(name, shape, dt))

    def ps(self, name, shape):
        return self.ctx.enter_context(self.nc.psum_tensor(name, shape, F32))

    def sem(self, name):
        sem = self.nc.alloc_semaphore(name)
        Stage.taken.append(sem)
        return sem

    @staticmethod
    def retire_semaphores(nc):
        nc.clear_and_free_semaphores(Stage.taken)
        Stage.taken.clear()
        nc.all_engine_barrier()


def at(t, k):
    if len(t.shape) == 2:
        return t[:, bass.ds(k, 1)]
    if len(t.shape) == 3:
        return t[:, bass.ds(k, 1), :].rearrange("p a n -> p (a n)")
    return t[:, bass.ds(k, 1), :, :].rearrange("p a m n -> p (a m) n")


def halves(t):
    return t.rearrange("p (a n) -> p a n", a=2)


class SplitWeights:

    def __init__(self, s, name, w_dram, raw=None, rings_of=None):
        self.w, self.kin, self.tiles = w_dram, w_dram.shape[2], w_dram.shape[0]
        self.per = -(-self.kin // KC)
        self.total = self.tiles * self.per
        if rings_of is not None:
            self.raw, self.ring = rings_of.raw, rings_of.ring
        else:
            self.raw = raw if raw is not None else s.sb(name + "_raw", [P, 2, KC, P])
            self.ring = s.sb(name + "_ring", [P, 2, 2, KC, P], F32R)
        self.landed = [s.sem(f"{name}_landed{u}") for u in range(2)]
        self.high, self.low, self.used = s.sem(name + "_high"), s.sem(name + "_low"), s.sem(name + "_used")
        self.begun = False

    def begin(self, block, rings_from=None):
        @block.sync
        def _(sp):
            if rings_from is not None:
                sp.wait_ge(rings_from.low, rings_from.total)
            for b in range(2):
                self.load_piece(sp, 0, b)

        @block.gpsimd
        def _(pool):
            for b in range(2):
                self.write_low_of(pool, 0, b)

        self.begun = True

    def write_first_ahead(self, act, rings_from=None):
        if rings_from is not None:
            act.wait_ge(rings_from.used, rings_from.total)
        for b in range(2):
            self.write_high(act, 0, b)

    def load_piece(self, sp, i, b):
        t, j = b // self.per, b % self.per
        n = self.chunks(j)
        src = self.w[bass.ds(i * 2 + t, 1), :, j * KC:j * KC + n].rearrange("a p k m -> (a p) k m")
        sp.dma_start(self.raw[:, b % 2, 0:n], src).then_inc(self.landed[b % 2], 16)

    def chunks(self, j):
        return min(KC, self.kin - j * KC)

    def load(self, sp):
        for b in range(2 if self.begun else 0, 2 * self.per):
            if b >= 2:
                sp.wait_ge(self.low, b - 1)
            self.load_piece(sp, 0, b)
        with sp.Fori(1, self.tiles // 2) as i:
            for b in range(2 * self.per):
                sp.wait_ge(self.low, i * (2 * self.per) + (b - 1))
                self.load_piece(sp, i, b)

    def write_high(self, act, i, b):
        q = i * (2 * self.per) + b
        act.wait_ge(self.landed[b % 2], 16 * (i * self.per + (b // 2 + 1)))
        if isinstance(q, int) and q < 2:
            act.copy(self.ring[:, b % 2, 0], self.raw[:, b % 2]).then_inc(self.high, 1)
            return
        act.wait_ge(self.used, q - 1)
        act.copy(self.ring[:, b % 2, 0], self.raw[:, b % 2]).then_inc(self.high, 1)

    def write_first(self, act):
        if self.begun:
            return
        for b in range(2):
            self.write_high(act, 0, b)

    def write_ahead(self, act, i, u, last):
        for b in range(u * self.per, (u + 1) * self.per):
            if not last or b + 2 < 2 * self.per:
                self.write_high(act, i, b + 2)

    def write_low(self, pool):
        with pool.Fori(1 if self.begun else 0, self.total // 2) as i:
            for u in range(2):
                self.write_low_of(pool, i, u)

    def write_low_of(self, pool, i, u):
        pool.wait_ge(self.high, i * 2 + (u + 1))
        pool.tensor_tensor(self.ring[:, u, 1], self.raw[:, u], self.ring[:, u, 0].bitcast(F32),
                           ALU.subtract).then_inc(self.low, 1)

    def multiply(self, pe, i, b, out, x, chunk, parts, start=True, stop=True):
        pe.wait_ge(self.low, i * (2 * self.per) + (b + 1))
        size = self.chunks(b % self.per)
        for k in range(size):
            for wn, xn in ((0, 0), (0, 1), (1, 0)):
                for n, part in enumerate(parts):
                    last = pe.matmul(out(n), self.ring[:, b % 2, wn, k], x[:, xn, chunk + k, part],
                                     start=start and k == 0 and wn + xn == 0, stop=stop and k == size - 1 and wn == 1)
        last.then_inc(self.used, 1)

    def finished(self, eng, i, u):
        eng.wait_ge(self.used, i * (2 * self.per) + (u + 1) * self.per)


def raw_slots(scratch):
    return scratch[:].rearrange("p a b -> p (a b)")[:, 0:2 * KC * P].rearrange("p (u k m) -> p u k m", u=2, k=KC)


def tile_loop(eng, first, turns, turn):
    with eng.Fori(first, turns - 1) as i:
        turn(i, False)
    turn(turns - 1, True)


HALF = COLS // 2
HALF_PARTS = (slice(0, HALF), slice(HALF, COLS))


def high_of(act, src, dst, chunks, high):
    for k in range(chunks):
        act.copy(dst[:, 0, k, :], src[:, k, :]).then_inc(high, 1)


def low_of(dve, src, dst, chunks, high, low):
    for k in range(chunks):
        dve.wait_ge(high, k + 1)
        dve.tensor_tensor(dst[:, 1, k, :], src[:, k, :], dst[:, 0, k, :].bitcast(F32), ALU.subtract).then_inc(low, 1)


def load_constants(nc, d, c):
    with ExitStack() as ctx:
        s = Stage(nc, ctx)
        loaded = s.sem("consts_loaded")
        block = ctx.enter_context(nc.Block())
        names = [n for n in c if n in d]

        @block.sync
        def _(sp):
            for n in names:
                sp.dma_start(c[n][:], d[n]).then_inc(loaded, 16)
            sp.wait_ge(loaded, 16 * len(names))


def norm_columns(nc, name, src, dst, gain, ones, eps, chunks, parts, width, following):
    with ExitStack() as ctx:
        s = Stage(nc, ctx)
        sq = s.sb(name + "_sq", [P, 2, width])
        r = s.sb(name + "_r", [P, width])
        n2 = s.sb(name + "_normed", [P, 2, width])
        total = s.ps(name + "_total", [P, 2, 512])
        squared, summed, scaled = s.sem(name + "_squared"), s.sem(name + "_summed"), s.sem(name + "_scaled")
        act_order, normed, high, low = (s.sem(name + x) for x in ("_act", "_normed_k", "_high", "_low"))
        block = ctx.enter_context(nc.Block())

        @block.scalar
        def _(act):
            act.preload_act_table_set("natural_log_exp_and_others")
            for k in range(chunks):
                if k >= 2:
                    act.wait_ge(summed, k - 1)
                act.activation(sq[:, k % 2, :], src[:, k, :], ACT.Square).then_inc(squared, 1)
            following.write_first_ahead(act)
            act.wait_ge(summed, chunks)
            o = Order(act, act_order)
            for n, part in enumerate(parts):
                w = part.stop - part.start
                o(act.activation(r[:, part], total[:, n, 0:w], ACT.Ln, scale=1.0 / (chunks * P), bias=eps[:, 0:1]))
            o.settle()
            act.activation(r[:, :], r[:, :], ACT.Exp, scale=-0.5).then_inc(scaled, 1)
            for k in range(chunks):
                act.wait_ge(normed, k + 1)
                act.copy(dst[:, 0, k, :], n2[:, k % 2, :]).then_inc(high, 1)

        @block.tensor
        def _(pe):
            for k in range(chunks):
                pe.wait_ge(squared, k + 1)
                for n, part in enumerate(parts):
                    w = part.stop - part.start
                    mm = pe.matmul(total[:, n, 0:w], ones[:, :], sq[:, k % 2, part], start=k == 0,
                                   stop=k == chunks - 1)
                mm.then_inc(summed, 1)

        @block.vector
        def _(dve):
            dve.wait_ge(scaled, 1)
            def split(k):
                dve.wait_ge(high, k + 1)
                dve.tensor_tensor(dst[:, 1, k, :], n2[:, k % 2, :], dst[:, 0, k, :].bitcast(F32),
                                  ALU.subtract).then_inc(low, 1)

            for k in range(chunks):
                if k >= 2:
                    dve.wait_ge(low, k - 1)
                dve.scalar_tensor_tensor(out=n2[:, k % 2, :], in0=src[:, k, :], scalar=gain[:, k:k + 1], in1=r[:, :],
                                         op0=ALU.mult, op1=ALU.mult).then_inc(normed, 1)
                if k:
                    split(k - 1)
            split(chunks - 1)

        following.begin(block)


def project_ssd(nc, d, c, h, zt, xbct, dt_raw, gates_raw, w):
    nz, nx = DI // 2, XBC // 2
    first_x = 1 + nz
    turns = first_x + nx
    with ExitStack() as ctx:
        s = Stage(nc, ctx)
        pad = s.sb("ssd_pad", [P, 2, CONV - 1 + COLS])
        acc = s.sb("ssd_acc", [P, 2, COLS])
        prod = s.sb("ssd_prod", [P, 2, DEC, CONV])
        tails = s.sb("ssd_tails", [P, XBC, CONV - 1])
        conv_s = s.sb("ssd_conv_s", [P, XBC, DEC, CONV])
        pp = s.ps("ssd_pp", [P, 2, 2, 512])
        state_landed, evacuated, convolved = s.sem("ssd_state_landed"), s.sem("ssd_evacuated"), s.sem("ssd_convolved")
        dve_order, stored, silu_done = s.sem("ssd_dve"), s.sem("ssd_stored"), s.sem("ssd_silu_done")
        block = ctx.enter_context(nc.Block())

        @block.sync
        def _(sp):
            sp.dma_start(conv_s[:], d["ssd_state_conv"]).then_inc(state_landed, 16)
            w.load(sp)
            sp.wait_ge(silu_done, XBC)
            sp.dma_start(d["out_p_conv"], tails[:]).then_inc(stored, 16)
            sp.dma_start(d["out_s_conv"], conv_s[:]).then_inc(stored, 16)
            sp.wait_ge(stored, 32)

        @block.gpsimd
        def _(pool):
            w.write_low(pool)

        @block.tensor
        def _(pe):
            with pe.Fori(0, turns) as i:
                for u in range(2):
                    pe.wait_ge(evacuated, i * 2 + (u + 1))
                    w.multiply(pe, i, u, lambda n: pp[:, u, n, 0:HALF], h, 0, HALF_PARTS)

        @block.scalar
        def _(act):
            act.preload_act_table(ACT.Silu)
            w.write_first(act)
            for u, (dst, rows) in enumerate(((dt_raw, SSD_HEADS), (gates_raw, 3 * HEADS))):
                w.write_ahead(act, 0, u, False)
                w.finished(act, 0, u)
                act.copy(halves(dst[:]), pp[0:rows, u, :, 0:HALF]).then_inc(evacuated, 1)
            with act.Fori(1, first_x) as i:
                for u in range(2):
                    w.write_ahead(act, i, u, False)
                    w.finished(act, i, u)
                    act.activation(halves(at(zt, (i - 1) * 2 + u)), pp[:, u, :, 0:HALF], ACT.Silu).then_inc(evacuated, 1)
            act.wait_ge(state_landed, 16)

            def silu(t, u):
                act.wait_ge(convolved, t + 3)
                act.activation(at(xbct, t), acc[:, u, :], ACT.Silu).then_inc(silu_done, 1)

            def turn(i, last, first=False):
                for u in range(2):
                    t = (i - first_x) * 2 + u
                    w.write_ahead(act, i, u, last)
                    w.finished(act, i, u)
                    act.wait_ge(convolved, t + 1)
                    act.copy(halves(pad[:, u, CONV - 1:]), pp[:, u, :, 0:HALF])
                    act.copy(conv_s[:, bass.ds(t, 1), :, CONV - 1:CONV].rearrange("p a s k -> p (a s k)"),
                             pp[:, u, 1, HALF - DEC:HALF]).then_inc(evacuated, 1)
                    if not (first and u == 0):
                        silu(t - 1, 1 - u)

            turn(first_x, False, first=True)
            tile_loop(act, first_x + 1, turns, turn)
            silu(XBC - 1, 1)

        @block.vector
        def _(dve):
            o = Order(dve, dve_order)
            dve.memset(pad[:, :, 0:CONV - 1], 0.0).then_inc(evacuated, 2)
            dve.memset(acc[:], 0.0).then_inc(convolved, 2)
            dve.wait_ge(convolved, 2)
            cw, cb = c["ssd_conv_w"], c["ssd_conv_b"]
            with dve.Fori(0, nx) as i:
                o.enter(i, 2 * (CONV + 3))
                for u in range(2):
                    t = i * 2 + u
                    wt = at(cw, t)
                    dve.wait_ge(evacuated, t + (2 * first_x + 3))
                    o(dve.tensor_scalar(acc[:, u, PROMPT], pad[:, u, 0:SEQ], wt[:, 0:1], at(cb, t), ALU.mult, ALU.add))
                    o(dve.tensor_tensor(prod[:, u], at(conv_s, t), wt.unsqueeze(1).broadcast_to([P, DEC, CONV]),
                                        ALU.mult))
                    for k in range(1, CONV):
                        o.settle()
                        o(dve.scalar_tensor_tensor(out=acc[:, u, PROMPT], in0=pad[:, u, k:k + SEQ],
                                                   scalar=wt[:, k:k + 1], in1=acc[:, u, PROMPT], op0=ALU.mult,
                                                   op1=ALU.add))
                    o(dve.tensor_reduce(acc[:, u, SAMPLE], prod[:, u], AX_X, ALU.add))
                    o.settle()
                    o(dve.tensor_scalar(acc[:, u, SAMPLE], acc[:, u, SAMPLE], at(cb, t), None, ALU.add))
                    o.settle()
                    dve.tensor_copy(at(tails, t), pad[:, u, SEQ:SEQ + CONV - 1]).then_inc(convolved, 1)
                o.leave(nx)




LOG1P_TERMS = 7


def step_sizes(nc, d, c, dt_raw, ec, wend, cdec, negcum, dtr, cumt, dxs):
    H = SSD_HEADS
    with ExitStack() as ctx:
        s = Stage(nc, ctx)
        t, ab, e, sq, p, dts, dta = (s.sb("dt_" + n, [H, COLS]) for n in ("t", "ab", "e", "sq", "p", "dts", "dta"))
        a = s.sb("dt_a", [H, 2])
        both = s.sb("dt_both", [H, 2, DEC])
        dtar = s.sb("dt_dtar", [P, TT, 2, H])
        low_high = s.sb("dt_low_high", [2 * H, SEQ], F32R)
        cum = s.sb("dt_cum", [P, TT, H])
        dend = s.sb("dt_dend", [P, TT, H])
        ptr = s.ps("dt_ptr", [P, 2, TT, P])
        psum = s.ps("dt_psum", [P, 2, 512])
        pct = s.ps("dt_pct", [2 * H, 512])
        pex = s.ps("dt_pex", [P, 512])
        dve_order, act_order, pe_order = s.sem("dt_dve"), s.sem("dt_act"), s.sem("dt_pe")
        ready, exped = s.sem("dt_ready"), s.sem("dt_exped")
        expand, expand_landed = s.sb("dt_expand", [H, D_INNER]), s.sem("dt_expand_landed")
        block = ctx.enter_context(nc.Block())

        @block.sync
        def _(sp):
            sp.dma_start(expand[:], d["expand"]).then_inc(expand_landed, 16)

        @block.vector
        def _(dve):
            o = Order(dve, dve_order)

            def do(ins):
                o(ins)
                o.settle()

            do(dve.tensor_scalar(t[:], dt_raw[:], c["ssd_dt_bias"][:, 0:1], None, ALU.add))
            o(dve.scalar_tensor_tensor(out=ab[:], in0=t[:], scalar=-1.0, in1=t[:], op0=ALU.mult, op1=ALU.max))
            dve.wait_ge(act_order, 1)
            o(dve.tensor_scalar(a[:, 1:2], a[:, 0:1], -1.0, None, ALU.mult))
            dve.wait_ge(act_order, 2)
            do(dve.tensor_scalar(p[:], e[:], 2.0, None, ALU.add))
            do(dve.reciprocal(p[:], p[:]))
            do(dve.tensor_tensor(e[:], e[:], p[:], ALU.mult))
            do(dve.tensor_tensor(sq[:], e[:], e[:], ALU.mult))
            do(dve.tensor_scalar(p[:], sq[:], 1.0 / (2 * LOG1P_TERMS + 1), None, ALU.mult))
            for k in range(LOG1P_TERMS - 1, 0, -1):
                do(dve.scalar_tensor_tensor(out=p[:], in0=p[:], scalar=1.0 / (2 * k + 1), in1=sq[:], op0=ALU.add,
                                            op1=ALU.mult))
            do(dve.scalar_tensor_tensor(out=p[:], in0=p[:], scalar=1.0, in1=e[:], op0=ALU.add, op1=ALU.mult))
            do(dve.tensor_scalar(t[:], t[:], 0.0, None, ALU.max))
            do(dve.scalar_tensor_tensor(out=dts[:], in0=p[:], scalar=2.0, in1=t[:], op0=ALU.mult, op1=ALU.add))
            do(dve.tensor_scalar(dta[:], dts[:], a[:, 1:2], None, ALU.mult))
            dve.tensor_copy(both[:, 0, :], dts[:, SAMPLE]).then_inc(ready, 1)
            dve.wait_ge(pe_order, 1)
            do(dve.tensor_copy(dtr[:], ptr[:, 0, :, 0:H]))
            do(dve.tensor_copy(dtar[:, :, 0, :], ptr[:, 1, :, 0:H]))
            dve.tensor_copy(dtar[:, :, 1, :], ptr[:, 1, :, 0:H]).then_inc(ready, 1)
            dve.wait_ge(pe_order, 2)
            do(dve.tensor_copy(cum[:].rearrange("p a b -> p (a b)"), psum[:, 0, 0:TT * H]))
            do(dve.tensor_tensor(dend[:].rearrange("p a b -> p (a b)"), psum[:, 1, 0:TT * H],
                                 cum[:].rearrange("p a b -> p (a b)"), ALU.subtract))
            do(dve.tensor_scalar(negcum[:], cum[:], -1.0, None, ALU.mult))
            do(dve.tensor_copy(low_high[H:, :], pct[H:, :]))
            dve.tensor_copy(cumt[0:H, :], pct[0:H, :])
            dve.tensor_tensor(cumt[H:, :], pct[H:, :], low_high[H:, :].bitcast(F32), ALU.subtract).then_inc(ready, 1)
            dve.wait_ge(exped, 1)
            do(dve.tensor_tensor(wend[:], dend[:], dtr[:], ALU.mult))
            dve.wait_ge(pe_order, 3)
            dve.tensor_copy(dxs[:].rearrange("p a b c -> p (a b c)"), pex[:, 0:DI * 2 * DEC])

        @block.scalar
        def _(act):
            act.preload_act_table(ACT.Exp)
            act.activation(a[:, 0:1], c["ssd_a_log"][:, 0:1], ACT.Exp).then_inc(act_order, 1)
            act.wait_ge(dve_order, 2)
            act.activation(e[:], ab[:], ACT.Exp, scale=-1.0).then_inc(act_order, 1)
            act.wait_ge(ready, 1)
            act.activation(both[:, 1, :], dta[:, SAMPLE], ACT.Exp).then_inc(act_order, 1)
            act.wait_ge(ready, 3)
            act.activation(ec[:], cum[:], ACT.Exp)
            act.activation(cdec[:].rearrange("p a b -> p (a b)"), psum[:, 1, 0:TT * H], ACT.Exp)
            act.activation(dend[:], dend[:], ACT.Exp).then_inc(exped, 1)

        @block.tensor
        def _(pe):
            ident, tri, ones = c["ident"], c["tri"], c["ones"]
            pe.wait_ge(ready, 1)
            for n, src in enumerate((dts, dta)):
                for k in range(TT):
                    mm = pe.transpose(ptr[:, n, k, 0:H], src[:, k * P:(k + 1) * P], ident[0:H, 0:H])
            mm.then_inc(pe_order, 1)
            pe.wait_ge(ready, 2)
            rows = dtar[:, :, 0, :]
            pe.matmul(psum[:, 0, 0:TT * H], tri[:], rows, start=True, stop=True)
            pe.matmul(psum[:, 1, 0:TT * H], ones[:], rows, start=True, stop=True)
            for k in range(TT):
                mm = pe.matmul(pct[:, k * P:(k + 1) * P], dtar[:, k].rearrange("p a b -> p (a b)"), tri[:], start=True,
                               stop=True)
            mm.then_inc(pe_order, 1)
            pe.wait_ge(act_order, 3)
            pe.wait_ge(expand_landed, 16)
            for k in range(DI):
                mm = pe.matmul(pex[:, k * 2 * DEC:(k + 1) * 2 * DEC], expand[:, k * P:(k + 1) * P],
                               both[:].rearrange("p a b -> p (a b)"), start=True, stop=True)
            mm.then_inc(pe_order, 1)


def scan(nc, d, c, xbct, zt, dxs, dtr, ec, wend, cdec, negcum, cumt, scratch):
    W = HPG * HEAD_P
    XC = W // P
    HC = DI // 2
    G2 = GROUPS // 2
    R = 2 * SSD_HEADS
    with ExitStack() as ctx:
        s = Stage(nc, ctx)
        bc = s.sb("sc_bc", [P, 2, 2, P])
        xs = s.sb("sc_xs", [P, 2, XC, P])
        sel = s.sb("sc_sel", [R, HPG, P], F32R)
        br = s.sb("sc_br", [P, 2, P])
        seg = s.sb("sc_seg", [P, HPG, P])
        m = s.sb("sc_m", [P, 2, HPG, P])
        xdt = s.sb("sc_xdt", [P, 2, HPG, HEAD_P])
        xend = s.sb("sc_xend", [P, 2, HPG, HEAD_P])
        y = s.sb("sc_y", [P, HPG, HEAD_P])
        yx = s.sb("sc_yx", [P, 2, XC, P])
        state = s.sb("sc_state", [P, GROUPS, W])
        mask = s.sb("sc_mask", [P, HPG // 2, P], F32R)
        eye = s.sb("sc_eye", [P, P], F32R)
        diag = s.sb("sc_diag", [P, 2, 2, G2, STATE])
        xb = s.sb("sc_xb", [P, HC, STATE])
        hc = s.sb("sc_hc", [P, HC, STATE])
        xdt_s = s.sb("sc_xdt_s", [P, DI, DEC])
        y_s = s.sb("sc_y_s", [P, DEC, DI])
        ring = scratch[:].rearrange("p a b -> p (a b)")[:, 0:TT * HC * STATE].rearrange(
            "p (u k n) -> p u k n", u=TT, k=HC)
        pcb = s.ps("sc_pcb", [P, 4, P])
        px = s.ps("sc_px", [P, HPG, HEAD_P])
        pbc = s.ps("sc_pbc", [P, HPG, P])
        pyd = s.ps("sc_pyd", [P, HPG, HEAD_P])
        pyo = s.ps("sc_pyo", [P, HPG, HEAD_P])
        pst = s.ps("sc_pst", [P, HPG, HEAD_P])
        pbs = s.ps("sc_pbs", [P, 2, G2, STATE])
        pt = pyd[:].rearrange("p a b -> p (a b)").rearrange("p (j n) -> p j n", j=XC)
        copied, selected, fronted, exped, ready = (s.sem("sc_" + x) for x in (
            "copied", "selected", "fronted", "exped", "ready"))
        carried, multiplied, scaled, y_done, state_done = (s.sem("sc_" + x) for x in (
            "carried", "multiplied", "scaled", "y_done", "state_done"))
        turned, gained, gated, dve_order, made_r = (s.sem("sc_" + x) for x in (
            "turned", "gained", "gated", "dve", "made_r"))
        diag_ready, on_rows, outer, stepped, read_out = (s.sem("sc_" + x) for x in (
            "diag_ready", "on_rows", "outer", "stepped", "read_out"))
        landed, stored = [s.sem(f"sc_landed{u}") for u in range(TT)], [s.sem(f"sc_stored{u}") for u in range(TT)]
        sample_x, prompt_stored = s.sem("sc_sample_x"), s.sem("sc_prompt_stored")
        block = ctx.enter_context(nc.Block())

        def on(g, k, by):
            return (g, k + by) if k + by < TT else (g + 1, k + by - TT)

        def groups(eng, turn):
            turn(0, True, False)
            with eng.Fori(1, GROUPS - 1) as g:
                turn(g, False, False)
            turn(GROUPS - 1, False, True)

        @block.gpsimd
        def _(pool):
            def copy(g, k):
                pos = slice(k * P, (k + 1) * P)
                pool.tensor_copy(bc[:, k % 2, 0, :], at(xbct, g + DI)[:, pos])
                pool.tensor_copy(bc[:, k % 2, 1, :], at(xbct, g + (DI + GROUPS))[:, pos])
                pool.tensor_copy(xs[:, k % 2], xbct[:, bass.ds(g * XC, XC), pos]).then_inc(copied, 1)

            def select(g):
                pool.tensor_tensor(sel[:], c["ones"][0:R, :].unsqueeze(1).broadcast_to([R, HPG, P]),
                                   c["ident2"][:, bass.ds(g * HPG, HPG)].unsqueeze(2).broadcast_to([R, HPG, P]),
                                   ALU.mult).then_inc(selected, 1)

            def diagonals(g, k):
                col = bass.ds(g * 2 + (k // 2 + SEQ), 1)
                for n in range(2):
                    first = DI + n * GROUPS + (k % 2) * G2
                    ins = pool.tensor_tensor(diag[:, k % 2, n], c["ident"][:].unsqueeze(1).broadcast_to([P, G2, P]),
                                             xbct[:, first:first + G2, col].broadcast_to([P, G2, P]), ALU.mult)
                ins.then_inc(diag_ready, 1)

            select(0)
            copy(0, 0)
            diagonals(0, 0)
            copy(0, 1)
            diagonals(0, 1)

            def turn(g, first, last):
                for k in range(TT):
                    v = g * TT + k
                    pool.wait_ge(carried, v + 1)
                    if k:
                        pool.wait_ge(state_done, v)
                        st = at(state, g).rearrange("p (a b) -> p a b", a=HPG)
                        pool.tensor_tensor(st, st, cdec[:, k, bass.ds(g * HPG, HPG)].unsqueeze(2).broadcast_to(
                            [P, HPG, HEAD_P]), ALU.mult).then_inc(scaled, 1)
                    if k == 2 and not last:
                        pool.wait_ge(fronted, v + 2)
                        select(g + 1)
                    if not (last and k >= 2):
                        copy(*on(g, k, 2))
                        pool.wait_ge(on_rows, v + 1)
                        diagonals(*on(g, k, 2))
                    if not (first and k == 0):
                        gate(*on(g, k, -1) if k else (g - 1, TT - 1))
                if last:
                    gate(g, TT - 1)

            def gate(g, k):
                pool.wait_ge(gained, g * TT + (k + 1))
                zk = zt[:, bass.ds(g * XC, XC), k * P:(k + 1) * P]
                pool.tensor_tensor(zk, zk, yx[:, k % 2], ALU.mult).then_inc(gated, 1)

            groups(pool, turn)

        @block.tensor
        def _(pe):
            def front(g, k):
                v = g * TT + k
                pe.wait_ge(copied, v + 1)
                pe.wait_ge(selected, g + 1)
                pe.matmul(pcb[:, 0, :], bc[:, k % 2, 0, :], bc[:, k % 2, 1, :], start=True, stop=True)
                pe.transpose(pcb[:, 1, :], bc[:, k % 2, 0, :], c["ident"][:])
                for e in range(HPG):
                    if e % (HPG // 2) == 0:
                        pe.matmul(pbc[:, e:e + HPG // 2, :], eye[:], mask[:], start=True, stop=False,
                                  skip_group_check=True)
                    pe.matmul(pbc[:, e, :], sel[:, e, :], cumt[:, k * P:(k + 1) * P], start=False, stop=True,
                              skip_group_check=True)
                for j in range(XC):
                    mm = pe.transpose(px[:, 2 * j:2 * j + 2, :].rearrange("p a b -> p (a b)"), xs[:, k % 2, j, :],
                                      c["ident"][:])
                mm.then_inc(fronted, 1)

            def rows_of_sample(g, k):
                pe.wait_ge(diag_ready, g * TT + (k + 1))
                pe.matmul(pbs[:].rearrange("p a b n -> p (a b n)"), c["ones"][:],
                          diag[:, k % 2].rearrange("p a b n -> p (a b n)"), start=True, stop=True).then_inc(on_rows, 1)

            def turn_y(v):
                pe.wait_ge(y_done, v + 1)
                for j in range(XC):
                    mm = pe.transpose(pt[:, j, :], y[:, 2 * j:2 * j + 2, :].rearrange("p a b -> p (a b)"),
                                      c["ident"][:])
                mm.then_inc(turned, 1)

            def turn(g, first, last):
                for k in range(TT):
                    v = g * TT + k
                    pe.wait_ge(ready, v + 1)
                    if not (last and k == TT - 1):
                        front(*on(g, k, 1))
                    if not (first and k == 0):
                        turn_y(v - 1)
                        pe.wait_ge(state_done, v)
                    mm = pe.matmul(pst[:].rearrange("p a b -> p (a b)"), br[:, k % 2, :],
                                   xend[:, k % 2].rearrange("p a b -> p (a b)"), start=True, stop=True)
                    if k:
                        mm = pe.matmul(pyo[:].rearrange("p a b -> p (a b)"), bc[:, k % 2, 1, :], at(state, g),
                                       start=True, stop=True)
                    mm.then_inc(carried, 1)
                    if not (first and k == 0):
                        pe.wait_ge(gained, v)
                    for e in range(HPG):
                        mm = pe.matmul(pyd[:, e, :], m[:, k % 2, e, :], xdt[:, k % 2, e, :], start=True, stop=True)
                    mm.then_inc(multiplied, 1)
                    if not (last and k == TT - 1):
                        pe.wait_ge(read_out, v + 1)
                        rows_of_sample(*on(g, k, 1))

            pe.wait_ge(made_r, 2)
            front(0, 0)
            rows_of_sample(0, 0)
            groups(pe, turn)
            turn_y(GROUPS * TT - 1)

        @block.scalar
        def _(act):
            act.preload_act_table(ACT.Exp)
            act.copy(eye[:], c["ident"][:]).then_inc(made_r, 1)
            act.copy(mask[:], c["ssd_mask"][:].unsqueeze(1).broadcast_to([P, HPG // 2, P])).then_inc(made_r, 1)

            def decays(g, k):
                v = g * TT + k
                act.wait_ge(fronted, v + 1)
                act.copy(br[:, k % 2, :], pcb[:, 1, :])
                for e in range(HPG):
                    ins = act.activation(seg[:, e, :], pbc[:, e, :], ACT.Exp, bias=negcum[:, k, bass.ds(g * HPG + e, 1)])
                ins.then_inc(exped, 1)

            def outers(g, k, first=False):
                v = g * TT + k
                act.wait_ge(on_rows, v + 1)
                if not first:
                    act.wait_ge(stepped, v)
                for n in range(HC):
                    ins = act.activation(xb[:, n, :], pbs[:, 0, n // (HC // G2)], ACT.Copy,
                                         scale=xdt_s[:, (k % 2) * HC + n, bass.ds(g * 2 + k // 2, 1)])
                ins.then_inc(outer, 1)

            decays(0, 0)
            act.wait_ge(sample_x, 1)
            outers(0, 0, True)

            def turn(g, first, last):
                for k in range(TT):
                    if not (last and k == TT - 1):
                        decays(*on(g, k, 1))
                        outers(*on(g, k, 1))

            groups(act, turn)

        @block.vector
        def _(dve):
            o = Order(dve, dve_order)
            heads = [P, HPG, HEAD_P]

            def of_heads(t, g, k):
                return t[:, k, bass.ds(g * HPG, HPG)].unsqueeze(2).broadcast_to(heads)

            def weigh(g, k, first=False):
                v = g * TT + k
                dve.wait_ge(fronted, v + 1)
                if not first:
                    dve.wait_ge(multiplied, v - 1)
                dve.tensor_tensor(xdt[:, k % 2], px[:], of_heads(dtr, g, k), ALU.mult)
                dve.tensor_tensor(xend[:, k % 2], px[:], of_heads(wend, g, k), ALU.mult)
                dve.wait_ge(exped, v + 1)
                dve.tensor_tensor(m[:, k % 2], seg[:], pcb[:, 0, :].unsqueeze(1).broadcast_to([P, HPG, P]),
                                  ALU.mult).then_inc(ready, 1)

            def step(g, k):
                v = g * TT + k
                dve.wait_ge(outer, v + 1)
                dve.wait_ge(landed[k], 16 * (g + 1))
                for n in range(HC):
                    ins = dve.scalar_tensor_tensor(out=ring[:, k, n, :], in0=ring[:, k, n, :],
                                                   scalar=dxs[:, (k % 2) * HC + n, 1, bass.ds(g * 2 + k // 2, 1)],
                                                   in1=xb[:, n, :], op0=ALU.mult, op1=ALU.add)
                ins.then_inc(stepped, 1)

            def read_state(g, k):
                v = g * TT + k
                dve.wait_ge(stepped, v + 1)
                per = HC // G2
                for n in range(G2):
                    ins = dve.tensor_tensor(hc[:, n * per:(n + 1) * per], ring[:, k, n * per:(n + 1) * per],
                                            pbs[:, 1, n].unsqueeze(1).broadcast_to([P, per, STATE]), ALU.mult)
                ins.then_inc(read_out, 1)
                dve.wait_ge(read_out, v + 1)
                o(dve.tensor_reduce(at(y_s, g * 2 + k // 2)[:, (k % 2) * HC:(k % 2 + 1) * HC], hc[:], AX_X, ALU.add))
                o.settle()

            def add_dx(g, k, late):
                v = g * TT + k
                dve.wait_ge(turned, v + 1)
                if late:
                    dve.wait_ge(gated, v - 1)
                for j in range(XC):
                    ins = dve.scalar_tensor_tensor(out=yx[:, k % 2, j, :],
                                                   in0=at(xbct, g * XC + j)[:, k * P:(k + 1) * P],
                                                   scalar=at(c["ssd_d"], g * XC + j), in1=pt[:, j, :],
                                                   op0=ALU.mult, op1=ALU.add)
                ins.then_inc(gained, 1)

            def take_in(g, k):
                v = g * TT + k
                dve.wait_ge(multiplied, v + 1)
                st = at(state, g).rearrange("p (a b) -> p a b", a=HPG)
                if k:
                    o(dve.tensor_tensor(y[:], pyo[:], of_heads(ec, g, k), ALU.mult))
                    o.settle()
                    dve.tensor_tensor(y[:], y[:], pyd[:], ALU.add).then_inc(y_done, 1)
                    dve.wait_ge(scaled, g * (TT - 1) + k)
                    dve.tensor_tensor(st, st, pst[:], ALU.add).then_inc(state_done, 1)
                else:
                    dve.tensor_copy(y[:], pyd[:]).then_inc(y_done, 1)
                    dve.tensor_copy(st, pst[:]).then_inc(state_done, 1)

            dve.tensor_tensor(xdt_s[:], xbct[:, 0:DI, SAMPLE], dxs[:, :, 0, :], ALU.mult).then_inc(sample_x, 1)
            weigh(0, 0, True)

            def turn(g, first, last):
                for k in range(TT):
                    step(g, k)
                    if not (first and k == 0):
                        add_dx(*((g, k - 1) if k else (g - 1, TT - 1)), late=not (first and k < 3))
                    read_state(g, k)
                    if not (last and k == TT - 1):
                        weigh(*on(g, k, 1), first=first and k == 0)
                    take_in(g, k)

            turn(0, True, False)
            with dve.Fori(1, GROUPS - 1) as g:
                o.enter(g, TT + (TT - 1), 1)
                turn(g, False, False)
                o.leave(GROUPS - 1)
            turn(GROUPS - 1, False, True)
            add_dx(GROUPS - 1, TT - 1, late=True)
            dve.tensor_tensor(xdt_s[:], xbct[:, 0:DI, SAMPLE],
                              c["ssd_d"][:].unsqueeze(2).broadcast_to([P, DI, DEC]), ALU.mult).then_inc(sample_x, 1)
            dve.wait_ge(sample_x, 2)
            dve.tensor_tensor(xdt_s[:], xdt_s[:], y_s[:].rearrange("p s k -> p k s"), ALU.add).then_inc(sample_x, 1)
            dve.wait_ge(sample_x, 3)
            dve.tensor_tensor(zt[:, :, SAMPLE], zt[:, :, SAMPLE], xdt_s[:], ALU.mult)

        @block.sync
        def _(sp):
            def of_state(name, g, k):
                h0 = (k % 2) * HC
                return d[name][bass.ds(g * 2 + k // 2, 1), :, h0:h0 + HC, :].rearrange("a p k n -> (a p) k n")

            for k in range(TT):
                sp.dma_start(ring[:, k], of_state("ssd_state", 0, k)).then_inc(landed[k], 16)

            def store(g, k):
                sp.wait_ge(read_out, g * TT + (k + 1))
                sp.dma_start(of_state("out_s_ssd", g, k), ring[:, k]).then_inc(stored[k], 16)

            with sp.Fori(0, GROUPS - 1) as g:
                for k in range(TT):
                    store(g, k)
                    sp.wait_ge(stored[k], 16 * (g + 1))
                    sp.dma_start(ring[:, k], of_state("ssd_state", g + 1, k)).then_inc(landed[k], 16)
            for k in range(TT):
                store(GROUPS - 1, k)
            sp.wait_ge(state_done, GROUPS * TT)
            sp.dma_start(d["out_p_ssd"], state[:]).then_inc(prompt_stored, 16)
            for k in range(TT):
                sp.wait_ge(stored[k], 16 * GROUPS)
            sp.wait_ge(prompt_stored, 16)


def gain_and_square(nc, c, zt, split, r, following):
    with ExitStack() as ctx:
        s = Stage(nc, ctx)
        sq = s.sb("gn_sq", [P, 2, COLS])
        total = s.ps("gn_total", [P, 2, 512])
        squared, summed, act_order, gained, high, low = (s.sem("gn_" + x) for x in (
            "squared", "summed", "act", "gained", "high", "low"))
        block = ctx.enter_context(nc.Block())

        @block.scalar
        def _(act):
            act.preload_act_table_set("natural_log_exp_and_others")
            for k in range(DI):
                if k >= 2:
                    act.wait_ge(summed, k - 1)
                act.activation(sq[:, k % 2, :], zt[:, k, :], ACT.Square).then_inc(squared, 1)
                if k:
                    act.wait_ge(gained, k)
                    act.copy(split[:, 0, k - 1, :], zt[:, k - 1, :]).then_inc(high, 1)
            act.wait_ge(gained, DI)
            act.copy(split[:, 0, DI - 1, :], zt[:, DI - 1, :]).then_inc(high, 1)
            following.write_first_ahead(act)
            act.wait_ge(summed, DI)
            act.activation(halves(r[:]), total[:, :, 0:HALF], ACT.Ln, scale=1.0 / D_INNER,
                           bias=c["eps"][:, 0:1]).then_inc(act_order, 1)
            act.wait_ge(act_order, 1)
            act.activation(r[:, :], r[:, :], ACT.Exp, scale=-0.5)

        @block.tensor
        def _(pe):
            for k in range(DI):
                pe.wait_ge(squared, k + 1)
                for m, part in enumerate(HALF_PARTS):
                    mm = pe.matmul(total[:, m, 0:HALF], c["ones"][:], sq[:, k % 2, part], start=k == 0,
                                   stop=k == DI - 1)
                mm.then_inc(summed, 1)

        @block.vector
        def _(dve):
            def split_chunk(k):
                dve.wait_ge(high, k + 1)
                dve.tensor_tensor(split[:, 1, k, :], zt[:, k, :], split[:, 0, k, :].bitcast(F32),
                                  ALU.subtract).then_inc(low, 1)

            for k in range(DI):
                dve.wait_ge(squared, k + 1)
                dve.tensor_scalar(zt[:, k, :], zt[:, k, :], c["ssd_norm"][:, k:k + 1], None,
                                  ALU.mult).then_inc(gained, 1)
                if k >= 2:
                    split_chunk(k - 2)
            split_chunk(DI - 2)
            split_chunk(DI - 1)

        following.begin(block)


def merge_branch(nc, d, c, name, n, w, src, kin, h, mixed, r, following=None):
    with ExitStack() as ctx:
        s = Stage(nc, ctx)
        whole = len(src.shape) == 3
        split = s.sb(name + "_split", [P, 2, kin, COLS], F32R) if whole else src
        gate = s.sb(name + "_gate", [P, 2, COLS])
        pg = s.ps(name + "_pg", [P, 2, 2, 512])
        po = s.ps(name + "_po", [P, 2, 2, 512])
        gated, evacuated, dve_order, high, low = (s.sem(name + x) for x in (
            "_gated", "_evacuated", "_dve", "_src_high", "_src_low"))
        block = ctx.enter_context(nc.Block())

        @block.sync
        def _(sp):
            w.load(sp)

        @block.gpsimd
        def _(pool):
            w.write_low(pool)

        @block.tensor
        def _(pe):
            with pe.Fori(0, KC // 2) as i:
                for u in range(2):
                    pe.wait_ge(evacuated, i * 2 + (u + 1))
                    b = u * w.per
                    w.multiply(pe, i, b, lambda m: pg[:, u, m, 0:HALF], h, 0, HALF_PARTS)
                    if whole:
                        pe.wait_ge(low, kin)
                    for j in range(1, w.per):
                        w.multiply(pe, i, b + j, lambda m: po[:, u, m, 0:HALF], split, (j - 1) * KC, HALF_PARTS,
                                   start=j == 1, stop=j == w.per - 1)

        @block.scalar
        def _(act):
            act.preload_act_table(ACT.Sigmoid)
            bias = c["b_merge"][:, n * KC:(n + 1) * KC]
            w.write_first(act)
            if whole:
                high_of(act, src, split, kin, high)

            def turn(i, last):
                for u in range(2):
                    t = i * 2 + u
                    w.write_ahead(act, i, u, last)
                    w.finished(act, i, u)
                    act.wait_ge(evacuated, t + 1)
                    act.activation(halves(gate[:, u, :]), pg[:, u, :, 0:HALF], ACT.Sigmoid,
                                   bias=bias[:, bass.ds(t, 1)]).then_inc(gated, 1)

            tile_loop(act, 0, KC // 2, turn)
            if following is not None:
                following.write_first_ahead(act)

        @block.vector
        def _(dve):
            o = Order(dve, dve_order)
            dve.memset(gate[0:1, 0, 0:1], 0.0).then_inc(evacuated, 2)
            if whole:
                low_of(dve, src, split, kin, high, low)
            with dve.Fori(0, KC // 2) as i:
                o.enter(i, 2)
                for u in range(2):
                    t = i * 2 + u
                    dve.wait_ge(gated, t + 1)
                    o(dve.tensor_tensor(halves(gate[:, u, :]), po[:, u, :, 0:HALF], halves(gate[:, u, :]), ALU.mult))
                    o.settle()
                    if r is not None:
                        ins = dve.tensor_tensor(at(mixed, t), gate[:, u, :], r[:], ALU.mult)
                    else:
                        ins = dve.tensor_tensor(at(mixed, t), at(mixed, t), gate[:, u, :], ALU.add)
                    ins.then_inc(evacuated, 1)
                o.leave(KC // 2)

        if following is not None:
            following.begin(block)


NQ = HEADS // 2
NR = NQ + KV
CK, CV, SV = NR, NR + 2, NR + 4
CMP_P = KV * NCP
CMP_S = KV * DEC * NCS
QK_SCALE = HD ** -0.5


def project_nsa(nc, d, c, h, qk, vt):
    with ExitStack() as ctx:
        s = Stage(nc, ctx)
        w = SplitWeights(s, "nq", d["w_qk"])
        sq = s.sb("nq_sq", [P, COLS])
        r = s.sb("nq_r", [P, COLS])
        n = s.sb("nq_n", [P, 2, COLS])
        t2 = s.sb("nq_t2", [P, COLS])
        pp = s.ps("nq_pp", [P, 2, 2, 512])
        pss = s.ps("nq_pss", [P, 2, 512])
        prt = s.ps("nq_prt", [P, 2, 512])
        evacuated, stored, squared, summed, logged, scaled, normed, turned = (s.sem("nq_" + x) for x in (
            "evacuated", "stored", "squared", "summed", "logged", "scaled", "normed", "turned"))
        times_cos, times_sin, rotated = (s.sem("nq_" + x) for x in ("times_cos", "times_sin", "rotated"))
        block = ctx.enter_context(nc.Block())

        def turns(eng, turn):
            turn(0, (1,), (), False)
            with eng.Fori(1, NR // 2) as i:
                turn(i, (0, 1), (0, 1), False)
            turn(NR // 2, (0,), (0, 1), False)
            with eng.Fori(NR // 2 + 1, w.tiles // 2 - 1) as i:
                turn(i, (), (), False)
            turn(w.tiles // 2 - 1, (), (), True)

        @block.sync
        def _(sp):
            w.load(sp)
            sp.wait_ge(rotated, NR)
            sp.dma_start(d["out_k"], qk[:, NQ:NR, :]).then_inc(stored, 16)
            sp.wait_ge(evacuated, 2 + w.tiles)
            sp.dma_start(d["out_cmp"], qk[:, CK:CK + 4, :]).then_inc(stored, 16)
            sp.dma_start(d["out_v"], vt[:]).then_inc(stored, 16)
            sp.wait_ge(stored, 48)

        @block.gpsimd
        def _(pool):
            w.write_low(pool)

        @block.tensor
        def _(pe):
            def turn(i, norm, rotate, last):
                for u in range(2):
                    t = i * 2 + u
                    pe.wait_ge(evacuated, t + 1)
                    w.multiply(pe, i, u, lambda m: pp[:, u, m, 0:HALF], h, 0, HALF_PARTS)
                    if u in norm:
                        pe.wait_ge(squared, t)
                        for m, part in enumerate(HALF_PARTS):
                            mm = pe.matmul(pss[:, m, 0:HALF], c["head_ones"][:], sq[:, part], start=True, stop=True)
                        mm.then_inc(summed, 1)
                    if u in rotate:
                        pe.wait_ge(normed, t - 1)
                        for m, part in enumerate(HALF_PARTS):
                            mm = pe.matmul(prt[:, m, 0:HALF], c["rotate"][:], n[:, u, part], start=True, stop=True)
                        mm.then_inc(turned, 1)

            turns(pe, turn)

        @block.scalar
        def _(act):
            act.preload_act_table_set("natural_log_exp_and_others")
            w.write_first(act)

            def turn(i, norm, rotate, last):
                for u in range(2):
                    t = i * 2 + u
                    if u in norm:
                        act.wait_ge(evacuated, t + 2)
                        act.activation(sq[:], at(qk, t - 1), ACT.Square).then_inc(squared, 1)
                    w.write_ahead(act, i, u, last)
                    if u in norm:
                        act.wait_ge(summed, t)
                        if rotate:
                            act.wait_ge(normed, t - 1)
                        act.activation(halves(r[:]), pss[:, :, 0:HALF], ACT.Ln, scale=1.0 / HD,
                                       bias=c["eps"][:, 0:1]).then_inc(logged, 1)
                        act.wait_ge(logged, t)
                        act.activation(r[:], r[:], ACT.Exp, scale=-0.5).then_inc(scaled, 1)

            turns(act, turn)

        @block.vector
        def _(dve):
            dve.memset(t2[:], 0.0).then_inc(evacuated, 2)

            def evacuate(i, u, dst, k):
                w.finished(dve, i, u)
                dve.tensor_copy(halves(at(dst, k)), pp[:, u, :, 0:HALF]).then_inc(evacuated, 1)

            def norm_tile(t, u):
                dve.wait_ge(scaled, t + 1)
                dve.scalar_tensor_tensor(out=n[:, u, :], in0=at(qk, t), scalar=at(c["head_gain"], t), in1=r[:],
                                         op0=ALU.mult, op1=ALU.mult).then_inc(normed, 1)

            def rotate_tile(t, u):
                dve.wait_ge(normed, t + 1)
                dve.tensor_tensor(at(qk, t), n[:, u, :], c["cos"][:], ALU.mult).then_inc(times_cos, 1)
                dve.wait_ge(turned, t + 1)
                dve.tensor_tensor(halves(t2[:]), prt[:, :, 0:HALF], halves(c["sin"][:]), ALU.mult).then_inc(times_sin, 1)
                dve.wait_ge(times_sin, t + 1)
                dve.tensor_tensor(at(qk, t), at(qk, t), t2[:], ALU.add).then_inc(rotated, 1)

            def turn(i, norm, rotate, last):
                for u in range(2):
                    t = i * 2 + u
                    if u in rotate:
                        rotate_tile(t - 2, u)
                    evacuate(i, u, qk, t)
                    if u in norm:
                        norm_tile(t - 1, 1 - u)

            turn(0, (1,), (), False)
            with dve.Fori(1, NR // 2) as i:
                turn(i, (0, 1), (0, 1), False)
            turn(NR // 2, (0,), (0, 1), False)
            for dst, first, stop in ((qk, NR // 2 + 1, SV // 2), (vt, SV // 2, w.tiles // 2)):
                with dve.Fori(first, stop) as i:
                    for u in range(2):
                        evacuate(i, u, dst, (i - (first if dst is vt else 0)) * 2 + u)


def turn_rows(nc, d, c, vt, gates_raw, vr, gates, gates_s):
    G = 3 * HEADS
    with ExitStack() as ctx:
        s = Stage(nc, ctx)
        gs = s.sb("tr_gs", [DEC, G])
        pv = s.ps("tr_pv", [P, 2, 512])
        pg = s.ps("tr_pg", [P, TT + 1, G])
        rows_done, rows_out, gates_done, gates_out, stored = (s.sem("tr_" + x) for x in (
            "rows_done", "rows_out", "gates_done", "gates_out", "stored"))
        block = ctx.enter_context(nc.Block())
        parts = [(slice(i * P, (i + 1) * P), P) for i in range(TT)] + [(SAMPLE, DEC)]

        @block.tensor
        def _(pe):
            for i, (part, m) in enumerate(parts):
                mm = pe.transpose(pg[0:m, i, :], gates_raw[:, part], c["ident"][0:G, 0:G])
            mm.then_inc(gates_done, 1)
            for i, (part, m) in enumerate(parts):
                if i >= 2:
                    pe.wait_ge(rows_out, i)
                for k in range(4):
                    mm = pe.transpose(pv[0:m, i % 2, k * P:(k + 1) * P], vt[:, k, part], c["ident"][:])
                mm.then_inc(rows_done, 1)

        @block.scalar
        def _(act):
            act.preload_act_table(ACT.Sigmoid)
            act.wait_ge(gates_done, 1)
            act.activation(gs[:], pg[0:DEC, TT, :], ACT.Sigmoid).then_inc(gates_out, 1)
            act.activation(gates[:], pg[:, 0:TT, :], ACT.Sigmoid)

        @block.vector
        def _(dve):
            dve.memset(vr[:, TT, :], 0.0).then_inc(rows_out, 1)
            dve.wait_ge(rows_out, 1)
            for i, (part, m) in enumerate(parts):
                dve.wait_ge(rows_done, i + 1)
                dve.tensor_copy(vr[0:m, i, :], pv[0:m, i % 2, :]).then_inc(rows_out, 1)

        @block.sync
        def _(sp):
            sp.wait_ge(gates_out, 1)
            sp.dma_start(d["gates_turn"], gs[:]).then_inc(stored, 16)
            sp.wait_ge(stored, 16)
            sp.dma_start(gates_s[:], d["gates_turn"].rearrange("s (h b) -> (s h) b", b=3)).then_inc(stored, 16)
            sp.wait_ge(stored, 32)


def compress_rows(nc, d, c, qk, kct, vcp, vcs):
    PAIRS = CMP_LEN // 2
    NP_ALL = CMP_P + CMP_S
    with ExitStack() as ctx:
        s = Stage(nc, ctx)
        tp = s.sb("cm_tp", [P, KV, SEQ])
        ts = s.sb("cm_ts", [P, 2, KV, DEC // 2, PAST])
        w1 = s.sb("cm_w1", [P, 2, PAIRS, P])
        w2 = s.sb("cm_w2", [P, 2, 2 * HD])
        pos = s.sb("cm_pos", [P, 2, PAIRS])
        pb = s.sb("cm_pb", [P, 2])
        hid = s.sb("cm_hid", [P, NP_ALL])
        r = s.sb("cm_r", [P, NP_ALL])
        n = s.sb("cm_n", [P, NP_ALL])
        t2 = s.sb("cm_t2", [P, NP_ALL])
        table = s.sb("cm_table", [1, DEC * PAGES], I32)
        php = s.ps("cm_php", [P, 512])
        phs = s.ps("cm_phs", [P, 512])
        ppe = s.ps("cm_ppe", [P, 2])
        pa = s.ps("cm_pa", [P, 2, 512])
        pv = s.ps("cm_pv", [P, 2, KV, HD])
        w_landed, table_landed, half_used = s.sem("cm_w_landed"), s.sem("cm_table"), s.sem("cm_half_used")
        pages_landed = [s.sem(f"cm_pages{u}") for u in range(2)]
        products, act_order, dve_order = s.sem("cm_products"), s.sem("cm_act"), s.sem("cm_dve")
        turned = [s.sem(f"cm_turned{u}") for u in range(2)]
        shifted = s.sem("cm_shifted")
        block = ctx.enter_context(nc.Block())
        parts = ((0, CMP_P), (CMP_P, NP_ALL))

        @block.sync
        def _(sp):
            sp.dma_start(table[:], d["page_table"]).then_inc(table_landed, 16)
            sp.dma_start(w1[:], d["cmp_w1"]).then_inc(w_landed, 16)
            sp.dma_start(w2[:], d["cmp_w2"]).then_inc(w_landed, 16)
            sp.dma_start(pos[:], d["cmp_pe"]).then_inc(w_landed, 16)
            sp.wait_ge(table_landed, 16)
            for kind, name in enumerate(("pool_cmp_k", "pool_cmp_v")):
                for q in range(DEC):
                    part, qq = q // (DEC // 2), q % (DEC // 2)
                    if kind and qq == 0:
                        sp.wait_ge(half_used, part + 1)
                    for g in range(PAGES):
                        page = sp.value_load(table[0:1, q * PAGES + g:q * PAGES + g + 1], min_val=0,
                                             max_val=d[name].shape[0] - 1)
                        src = d[name][bass.ds(page, 1)].rearrange("a p k n -> (a p) k n")
                        lo = g * PAGE
                        sp.dma_start(ts[0:HD, part, :, qq, lo:lo + PAGE], src).then_inc(pages_landed[part], 16)
                        skip = 1 if g == 0 else 0
                        sp.dma_start(ts[HD:P, part, :, qq, lo - 1 + skip:lo - 1 + PAGE],
                                     src[:, :, skip:PAGE]).then_inc(pages_landed[part], 16)

        def turn_rows_under(eng, kind, half):
            for kv in range(KV):
                rows = slice((kv % 2) * HD, (kv % 2 + 1) * HD)
                last = eng.tensor_copy(tp[half * HD:(half + 1) * HD, kv, 0:SEQ - half],
                                       qk[rows, CK + 2 * kind + kv // 2, half:SEQ])
            last.then_inc(turned[half], 1)

        @block.gpsimd
        def _(pool):
            for kind in range(2):
                if kind:
                    pool.wait_ge(half_used, 1)
                turn_rows_under(pool, kind, 0)

        @block.tensor
        def _(pe):
            pe.wait_ge(w_landed, 48)
            for kind in range(2):
                pe.wait_ge(turned[0], kind + 1)
                pe.wait_ge(turned[1], kind + 1)
                for l in range(PAIRS):
                    pe.matmul(php[:, 0:CMP_P], w1[:, kind, l, :],
                              tp[:, :, 2 * l:2 * l + CMP_STRIDE * (NCP - 1) + 1:CMP_STRIDE],
                              start=l == 0, stop=l == PAIRS - 1)
                for part in range(2):
                    pe.wait_ge(pages_landed[part], 16 * DEC * PAGES * (kind + 1))
                    out = phs[:, 0:CMP_S].rearrange("p (k s) -> p k s", k=KV)[
                        :, :, part * (DEC // 2) * NCS:(part + 1) * (DEC // 2) * NCS]
                    for l in range(PAIRS):
                        mm = pe.matmul(out, w1[:, kind, l, :],
                                       ts[:, part, :, :, 2 * l:2 * l + CMP_STRIDE * (NCS - 1) + 1:CMP_STRIDE].rearrange(
                                           "p k s n -> p (k s) n"),
                                       start=l == 0, stop=l == PAIRS - 1)
                    mm.then_inc(half_used, 1)
                for l in range(PAIRS):
                    mm = pe.matmul(ppe[:, kind:kind + 1], w1[:, kind, l, :], pos[:, kind, l:l + 1], start=l == 0,
                                   stop=l == PAIRS - 1)
                mm.then_inc(products, 1)
                pe.wait_ge(act_order, 3 * (kind + 1) if kind == 0 else 3 + 3 + 3)
                if kind == 0:
                    for m, (a, b) in enumerate(parts):
                        mm = pe.matmul(pa[:, m, 0:b - a], w2[:, 0, :], hid[:, a:b], start=True, stop=True)
                    mm.then_inc(products, 1)
                    pe.wait_ge(act_order, 4)
                    pe.wait_ge(dve_order, 1)
                    for m, (a, b) in enumerate(parts):
                        mm = pe.matmul(pa[:, m, 0:b - a], c["head_ones"][:], r[:, a:b], start=True, stop=True)
                    mm.then_inc(products, 1)
                    pe.wait_ge(dve_order, 2)
                    for m, (a, b) in enumerate(parts):
                        mm = pe.matmul(pa[:, m, 0:b - a], c["rotate"][:], n[:, a:b], start=True, stop=True)
                    mm.then_inc(products, 1)
                else:
                    for kv in range(KV):
                        pe.matmul(pv[0:NCP, 0, kv, :], hid[:, kv * NCP:(kv + 1) * NCP], w2[:, 1, 0:HD], start=True,
                                  stop=True)
                    for kv in range(KV):
                        a = CMP_P + kv * DEC * NCS
                        mm = pe.matmul(pv[0:DEC * NCS, 1, kv, :], hid[:, a:a + DEC * NCS], w2[:, 1, 0:HD],
                                       start=True, stop=True)
                    mm.then_inc(products, 1)

        @block.scalar
        def _(act):
            o = Order(act, act_order)
            act.preload_act_table(ACT.Silu)
            for kind in range(2):
                act.wait_ge(products, 1 if kind == 0 else 5)
                o(act.activation(pb[:, kind:kind + 1], ppe[:, kind:kind + 1], ACT.Copy))
                o.settle()
                o(act.activation(hid[:, 0:CMP_P], php[:, 0:CMP_P], ACT.Silu, bias=pb[:, kind:kind + 1]))
                o(act.activation(hid[:, CMP_P:], phs[:, 0:CMP_S], ACT.Silu, bias=pb[:, kind:kind + 1]))
                if kind == 0:
                    act.wait_ge(products, 2)
                    act.activation(r[:, 0:CMP_P], pa[:, 0, 0:CMP_P], ACT.Square)
                    o(act.activation(r[:, CMP_P:], pa[:, 1, 0:CMP_S], ACT.Square))
                    act.wait_ge(products, 3)
                    act.activation(r[:, 0:CMP_P], pa[:, 0, 0:CMP_P], ACT.Ln, scale=1.0 / HD, bias=c["eps"][:, 0:1])
                    o(act.activation(r[:, CMP_P:], pa[:, 1, 0:CMP_S], ACT.Ln, scale=1.0 / HD, bias=c["eps"][:, 0:1]))
                    o.settle()
                    o(act.activation(r[:], r[:], ACT.Exp, scale=-0.5))

        @block.vector
        def _(dve):
            o = Order(dve, dve_order)
            gain = c["cmp_gain"][:, 0:1]
            turn_rows_under(dve, 0, 1)
            dve.wait_ge(half_used, 1)
            turn_rows_under(dve, 1, 1)
            dve.wait_ge(products, 2)
            dve.wait_ge(act_order, 4)
            dve.tensor_copy(n[:, 0:CMP_P], pa[:, 0, 0:CMP_P])
            o(dve.tensor_copy(n[:, CMP_P:], pa[:, 1, 0:CMP_S]))
            dve.wait_ge(act_order, 6)
            dve.wait_ge(dve_order, 1)
            o(dve.scalar_tensor_tensor(out=n[:], in0=n[:], scalar=gain, in1=r[:], op0=ALU.mult, op1=ALU.mult))
            o.settle()
            dve.wait_ge(products, 4)
            o(dve.tensor_tensor(t2[:, 0:CMP_P], pa[:, 0, 0:CMP_P], c["cmp_sin"][:, 0:CMP_P], ALU.mult))
            o(dve.tensor_tensor(t2[:, CMP_P:], pa[:, 1, 0:CMP_S], c["cmp_sin"][:, CMP_P:], ALU.mult))
            o(dve.tensor_tensor(n[:], n[:], c["cmp_cos"][:], ALU.mult))
            o.settle()
            dve.tensor_tensor(kct[:], n[:], t2[:], ALU.add)
            dve.wait_ge(products, 6)
            dve.tensor_copy(vcp[0:NCP], pv[0:NCP, 0])
            dve.tensor_copy(vcs[0:DEC * NCS], pv[0:DEC * NCS, 1])


def attend_prompt(nc, d, c, qk, vr, gates, kct, vcp, ot):
    UNITS = KV
    BLOCKS = [(kb, i) for kb in range(TT) for i in range(kb, TT)]
    GROUPS_T = [[0], [1], [2, 3]]
    EV = 1 + 2 * len(GROUPS_T)
    PARTS = 1 + TT
    with ExitStack() as ctx:
        s = Stage(nc, ctx)
        qs = s.sb("ap_qs", [P, 2, SEQ])
        pr = s.sb("ap_pr", [P, 2, TT, 2, SEQ])
        pc = s.sb("ap_pc", [P, 2, TT, NCP])
        pt = s.sb("ap_pt", [P, EV, SEQ])
        mx = s.sb("ap_mx", [P, TT, 2])
        mc = s.sb("ap_mc", [P, TT])
        nb = s.sb("ap_nb", [P, 2, TT, 2])
        den = s.sb("ap_den", [P, 2, TT, 3])
        pss = s.ps("ap_pss", [P, 2, 2, 512])
        psc = s.ps("ap_psc", [P, TT, 32])
        pst = s.ps("ap_pst", [P, 2, 512])
        pso = s.ps("ap_pso", [P, 512])
        copied, scored, shifted, exped = (s.sem("ap_" + x) for x in ("copied", "scored", "shifted", "exped"))
        scaled, scaled_w, turned, evacuated = (s.sem("ap_" + x) for x in ("scaled", "scaled_w", "turned", "evac"))
        summed, written, dve_order, pool_ready = (s.sem("ap_" + x) for x in ("summed", "written", "dve", "pool_ready"))
        block = ctx.enter_context(nc.Block())

        def on(g, u):
            return (g, u + 1) if u + 1 < UNITS else (g + 1, 0)

        def turns(eng, turn):
            turn(0, True, False)
            with eng.Fori(1, GQ - 1) as g:
                turn(g, False, False)
            turn(GQ - 1, False, True)

        @block.gpsimd
        def _(pool):
            def copy(g, ch):
                pool.tensor_copy(qs[:, ch, :], at(qk, g + ch * GQ)[:, PROMPT]).then_inc(copied, 1)

            def scale(g, u):
                v = g * UNITS + u
                pool.wait_ge(pool_ready, v + 1)
                for i in range(TT):
                    w = (i + 1) * P
                    ins = pool.tensor_tensor(pr[:, u % 2, i, 1, 0:w], pr[:, u % 2, i, 1, 0:w],
                                             den[:, u % 2, i, 2:3].broadcast_to([P, w]), ALU.mult)
                ins.then_inc(scaled_w, 1)

            def turn(g, first, last):
                for u in range(UNITS):
                    if not last and u % 2:
                        pool.wait_ge(scored, (g * UNITS + (u + 1)) * 5)
                        copy(g + 1, u // 2)
                    if not (last and u == UNITS - 1):
                        scale(*on(g, u))

            copy(0, 0)
            copy(0, 1)
            scale(0, 0)
            turns(pool, turn)

        @block.tensor
        def _(pe):
            ident = c["ident"]

            def score(g, u, part, first=False):
                v = g * UNITS + u
                ch, half = u // 2, slice((u % 2) * HD, (u % 2 + 1) * HD)
                if part == 0:
                    if u % 2 == 0:
                        pe.wait_ge(copied, g * 2 + (ch + 1))
                    if not first:
                        pe.wait_ge(shifted, v * 5 - 4)
                    for i in range(TT):
                        mm = pe.matmul(psc[:, i, 0:NCP], qs[half, ch, i * P:(i + 1) * P],
                                       kct[half, u * NCP:(u + 1) * NCP], start=True, stop=True)
                else:
                    i = TT - part
                    if part > 2 or not first:
                        pe.wait_ge(exped, v * 5 + (part - 1 if part > 2 else part - 2))
                    for b in range(2):
                        mm = pe.matmul(pss[:, part % 2, b, 0:(i + 1) * P], qs[half, ch, i * P:(i + 1) * P],
                                       qk[half, NQ + 2 * b + ch, 0:(i + 1) * P], start=True, stop=True)
                mm.then_inc(scored, 1)

            def turn_weights(g, u, k):
                v = g * UNITS + u
                if k < 2:
                    pe.wait_ge(scaled, v * 2 + (k + 1))
                if k >= 2:
                    pe.wait_ge(evacuated, v * EV + (k - 1))
                if k == 1 + len(GROUPS_T):
                    pe.wait_ge(scaled_w, v + 1)
                if k == 0:
                    for i in range(TT):
                        mm = pe.transpose(pst[0:NCP, k % 2, i * P:(i + 1) * P], pc[:, u % 2, i, :], ident[:])
                else:
                    b, gr = (k - 1) // len(GROUPS_T), GROUPS_T[(k - 1) % len(GROUPS_T)]
                    for n, (kb, i) in enumerate([x for x in BLOCKS if x[0] in gr]):
                        mm = pe.transpose(pst[:, k % 2, n * P:(n + 1) * P],
                                          pr[:, u % 2, i, b, kb * P:(kb + 1) * P], ident[:])
                mm.then_inc(turned, 1)

            def values(g, u, k):
                v = g * UNITS + u
                half = slice((u % 2) * HD, (u % 2 + 1) * HD)
                pe.wait_ge(evacuated, v * EV + (k + 1))
                if k == 0:
                    pe.matmul(pso[half, :], vcp[0:NCP, u, :], pt[0:NCP, 0, :], start=True, stop=False,
                              skip_group_check=True)
                    return
                b, gr = (k - 1) // len(GROUPS_T), GROUPS_T[(k - 1) % len(GROUPS_T)]
                n = 0
                for kb in gr:
                    w = (TT - kb) * P
                    mm = pe.matmul(pso[half, kb * P:SEQ], vr[:, kb, (b * KV + u) * HD:(b * KV + u + 1) * HD],
                                   pt[:, k, n * P:n * P + w], start=False, stop=k == EV - 1 and kb == gr[-1],
                                   skip_group_check=True)
                    n += TT - kb
                if k == EV - 1:
                    mm.then_inc(summed, 1)

            for part in range(PARTS):
                score(0, 0, part, first=True)

            def turn(g, first, last):
                for u in range(UNITS):
                    v = g * UNITS + u
                    turn_weights(g, u, 0)
                    if not (first and u < 2):
                        pe.wait_ge(written, v - 1)
                    for k in range(EV):
                        if k < PARTS - 1 and not (last and u == UNITS - 1):
                            for part in (0, 1) if k == 0 else (k + 1,):
                                score(*on(g, u), part)
                        if k + 1 < EV:
                            turn_weights(g, u, k + 1)
                        values(g, u, k)

            turns(pe, turn)

        @block.vector
        def _(dve):
            o = Order(dve, dve_order)

            def weigh(g, u, first=False):
                v = g * UNITS + u
                head = (u // 2) * 2 * GQ + (u % 2) * GQ
                pcu = pc[:, u % 2]
                if not first:
                    dve.wait_ge(turned, (v - 1) * EV)
                dve.wait_ge(scored, v * 5 + 1)
                o(dve.tensor_tensor(pcu, psc[:, :, 0:NCP], c["cmp_mask"][:], ALU.add))
                o.settle()
                o(dve.tensor_reduce(mc[:], pcu, AX_X, ALU.max))
                o.settle()
                o(dve.tensor_scalar(mc[:], mc[:], FLOOR, None, ALU.max))
                o.settle()
                dve.tensor_tensor(pcu, pcu, mc[:].unsqueeze(2).broadcast_to([P, TT, NCP]),
                                  ALU.subtract).then_inc(shifted, 1)
                for part in range(1, PARTS):
                    i = TT - part
                    dve.wait_ge(scored, v * 5 + (part + 1))
                    blk = pss[:, part % 2, :, i * P:(i + 1) * P]
                    o(dve.tensor_tensor(blk, blk, c["causal"][:].unsqueeze(1).broadcast_to([P, 2, P]), ALU.add))
                    o.settle()
                    o(dve.tensor_reduce(mx[:, i, :], pss[:, part % 2, :, 0:(i + 1) * P], AX_X, ALU.max))
                    o.settle()
                    dve.tensor_scalar(nb[:, u % 2, i, :], mx[:, i, :], -QK_SCALE, None, ALU.mult).then_inc(shifted, 1)
                dn = den[:, u % 2]
                dve.wait_ge(exped, v * 5 + 5)
                o(dve.tensor_reduce(dn[:, :, 0], pcu, AX_X, ALU.add))
                o.settle()
                o(dve.tensor_scalar(dn, dn, 1e-30, None, ALU.max))
                o.settle()
                o(dve.reciprocal(dn, dn))
                o.settle()
                dve.tensor_tensor(dn, dn, gates[:, :, bass.ds(g * 3 + head * 3, 3)], ALU.mult).then_inc(pool_ready, 1)
                dve.wait_ge(pool_ready, v + 1)
                dve.tensor_tensor(pcu, pcu, dn[:, :, 0:1].broadcast_to([P, TT, NCP]), ALU.mult).then_inc(scaled, 1)
                for i in range(TT):
                    w = (i + 1) * P
                    ins = dve.tensor_scalar(pr[:, u % 2, i, 0, 0:w], pr[:, u % 2, i, 0, 0:w], dn[:, i, 1:2], None,
                                            ALU.mult)
                ins.then_inc(scaled, 1)

            def turn(g, first, last):
                for u in range(UNITS):
                    if not (last and u == UNITS - 1):
                        weigh(*on(g, u), first=first and u == 0)

            weigh(0, 0, first=True)
            turn(0, True, False)
            with dve.Fori(1, GQ - 1) as g:
                o.enter(g, UNITS * (3 + 2 * TT + 3), 1)
                turn(g, False, False)
                o.leave(GQ - 1)
            turn(GQ - 1, False, True)

        @block.scalar
        def _(act):
            act.preload_act_table(ACT.Exp)

            def weights(g, u, part, first=False):
                v = g * UNITS + u
                if part == 0 and not first:
                    act.wait_ge(turned, (v - 1) * EV)
                act.wait_ge(shifted, v * 5 + (part + 1))
                if part == 0:
                    act.activation(pc[:, u % 2], pc[:, u % 2], ACT.Exp, scale=QK_SCALE).then_inc(exped, 1)
                    return
                i = TT - part
                w = (i + 1) * P
                for b in range(2):
                    ins = act.activation(pr[:, u % 2, i, b, 0:w], pss[:, part % 2, b, 0:w], ACT.Exp, scale=QK_SCALE,
                                         bias=nb[:, u % 2, i, b:b + 1], accum_out=den[:, u % 2, i, 1 + b:2 + b])
                ins.then_inc(exped, 1)

            def evacuate(g, u, k, first=False):
                v = g * UNITS + u
                act.wait_ge(turned, v * EV + (k + 1))
                if k == 0 and not first:
                    act.wait_ge(summed, v)
                w = {0: SEQ, 1: SEQ, 2: SEQ - P, 3: 3 * P}[(k - 1) % 3 + 1 if k else 0]
                rows = slice(0, P) if k else slice(0, NCP)
                act.copy(pt[rows, k, 0:w], pst[rows, k % 2, 0:w]).then_inc(evacuated, 1)

            for part in range(PARTS):
                weights(0, 0, part, first=True)

            def turn(g, first, last):
                for u in range(UNITS):
                    v = g * UNITS + u
                    for k in range(EV):
                        evacuate(g, u, k, first=first and u == 0)
                        if k < PARTS and not (last and u == UNITS - 1):
                            weights(*on(g, u), k, first=first and u == 0)
                    half = slice((u % 2) * HD, (u % 2 + 1) * HD)
                    act.wait_ge(summed, v + 1)
                    act.copy(at(ot, g + (u // 2) * GQ)[half, PROMPT], pso[half, :]).then_inc(written, 1)

            turns(act, turn)


def attend_sample_nsa(nc, d, c, qk, vr, gates_s, kct, vcs, ot):
    with ExitStack() as ctx:
        s = Stage(nc, ctx)
        qd = s.sb("as_qd", [P, 2, DEC * DIAG])
        q64 = s.sb("as_q64", [HD, ROWS])
        kt = s.sb("as_kt", [P, 2, 2, DEC, PAST + 1])
        vt = s.sb("as_vt", [P, DEC, PAGES, KV * HD])
        pd = s.sb("as_pd", [P, PAGES, DEC * DIAG])
        w = s.sb("as_w", [P, PAST + 1])
        wc = s.sb("as_wc", [P, KV, DEC * NCS])
        wct = s.sb("as_wct", [P, KV, P])
        wn = s.sb("as_wn", [P, DEC])
        wnt = s.sb("as_wnt", [DEC, P])
        st = s.sb("as_st", [P, 4])
        osum = s.sb("as_o", [P, HD])
        table = s.sb("as_table", [1, DEC * PAGES], I32)
        psc = s.ps("as_psc", [P, 512])
        ptr = s.ps("as_ptr", [P, PAGES, P])
        pn = s.ps("as_pn", [DEC, P])
        pcs = s.ps("as_pcs", [P, 512])
        pct = s.ps("as_pct", [P, KV, P])
        po = s.ps("as_po", [P, KV * HD])
        poc = s.ps("as_poc", [P, HD])
        pot = s.ps("as_pot", [HD, P])
        table_landed, k_landed = s.sem("as_table_landed"), s.sem("as_k_landed")
        v_landed, vw_landed = s.sem("as_v_landed"), s.sem("as_vw_landed")
        pe_order, act_order, dve_order, pool_order = (s.sem("as_" + x) for x in ("pe", "act", "dve", "pool"))
        dve_steps, shift_ready = s.sem("as_dve_steps"), s.sem("as_shift_ready")
        PE_SEL_VALUES = 6
        block = ctx.enter_context(nc.Block())

        @block.sync
        def _(sp):
            sp.dma_start(table[:], d["page_table"]).then_inc(table_landed, 16)
            sp.dma_start(kt[:, 1, :, :, 0:PAST], d["win_k"]).then_inc(k_landed, 16)
            sp.wait_ge(table_landed, 16)
            for q in range(DEC):
                for g in range(PAGES):
                    page = sp.value_load(table[0:1, q * PAGES + g:q * PAGES + g + 1], min_val=0,
                                         max_val=d["pool_sel_k"].shape[0] - 1)
                    sp.dma_start(kt[:, 0, :, q, g * PAGE:(g + 1) * PAGE],
                                 d["pool_sel_k"][bass.ds(page, 1)].rearrange("a p k n -> (a p) k n")
                                 ).then_inc(k_landed, 16)
                    sp.dma_start(vt[:, q, g, :], d["pool_sel_v"][bass.ds(page, 1)].rearrange("a p n -> (a p) n")
                                 ).then_inc(v_landed, 16)
            sp.wait_ge(pe_order, PE_SEL_VALUES)
            sp.dma_start(vt[:], d["win_v"]).then_inc(vw_landed, 16)

        @block.gpsimd
        def _(pool):
            pool.memset(qd[:], 0.0).then_inc(pool_order, 1)
            pool.memset(pd[:], 0.0).then_inc(pool_order, 1)

        @block.tensor
        def _(pe):
            ident = c["ident"]
            o = Order(pe, pe_order)
            pe.wait_ge(dve_order, 1)
            o(pe.matmul(pcs[:, 0:CMP_S], q64[:], kct[0:HD, CMP_P:], start=True, stop=True))
            pe.wait_ge(dve_order, 2)
            for kv in range(KV):
                mm = pe.transpose(pct[0:DEC * NCS, kv, :], wc[:, kv, :], ident[:])
            o(mm)
            pe.wait_ge(k_landed, 16 * (1 + DEC * PAGES))
            pe.wait_ge(pool_order, 3)
            for b in range(2):
                n = 0
                if b:
                    pe.wait_ge(act_order, 2)
                for q in range(DEC):
                    for ch in range(2):
                        mm = pe.matmul(psc[:, 0:PAST + 1], qd[:, ch, 0:DEC * P].rearrange("p (s r) -> p s r", s=DEC)[
                            :, q, :], kt[:, b, ch, q, :], start=n == 0, stop=n == 2 * DEC - 1)
                        n += 1
                o(mm)
                pe.wait_ge(dve_order, 3 + 2 * b)
                for g in range(PAGES):
                    mm = pe.transpose(ptr[:, g, :], w[:, g * PAGE:(g + 1) * PAGE], ident[:])
                o(mm)
                o(pe.transpose(pn[:], wn[:], ident[:]))
                pe.wait_ge(dve_order, 4 + 2 * b)
                if b:
                    pe.wait_ge(vw_landed, 16)
                else:
                    pe.wait_ge(v_landed, 16 * DEC * PAGES)
                for q in range(DEC):
                    for g in range(PAGES):
                        pe.matmul(po[:], pd[:, g, 0:DEC * P].rearrange("p (s r) -> p s r", s=DEC)[:, q, :],
                                  vt[:, q, g, :], start=b == 0 and q == 0 and g == 0, stop=False,
                                  skip_group_check=True)
                o(pe.matmul(po[:], wnt[:], vr[0:DEC, TT, b * KV * HD:(b + 1) * KV * HD], start=False, stop=b == 1,
                            skip_group_check=True))
            for kv in range(KV):
                mm = pe.matmul(poc[:], wct[0:DEC * NCS, kv, :], vcs[0:DEC * NCS, kv, :], start=kv == 0,
                               stop=kv == KV - 1)
            o(mm)
            pe.wait_ge(dve_order, 7)
            o(pe.transpose(pot[:], osum[:], ident[:]))

        @block.scalar
        def _(act):
            act.preload_act_table(ACT.Exp)
            o = Order(act, act_order)
            act.wait_ge(pool_order, 2)
            for ch in range(2):
                for par in range(2):
                    half = slice(par * HD, (par + 1) * HD)
                    first = ch * 2 * GQ + par * GQ
                    dst = qd[half, ch, :].rearrange("p (s x) -> p s x", x=DIAG)[:, :, first:first + GQ]
                    act.copy(dst, qk[half, ch * GQ:(ch + 1) * GQ, SAMPLE].rearrange("p g s -> p s g"))
            for b in range(2):
                for ch in range(2):
                    ins = act.copy(kt[:, b, ch, :, PAST], qk[:, NQ + 2 * b + ch, SAMPLE])
            ins.then_inc(pool_order, 1)
            act.wait_ge(shift_ready, 1)
            o(act.activation(wc[:], wc[:], ACT.Exp, scale=QK_SCALE, accum_out=st[:, 2:3]))
            for b in range(2):
                act.wait_ge(shift_ready, 2 + b)
                o(act.activation(w[:], psc[:, 0:PAST + 1], ACT.Exp, scale=QK_SCALE, bias=st[:, 1:2],
                                 accum_out=st[:, 2:3]))

        @block.vector
        def _(dve):
            sh, o = Order(dve, dve_steps), Order(dve, dve_order)

            def do(ins):
                sh(ins)
                sh.settle()

            for ch in range(2):
                for par in range(2):
                    half = slice(par * HD, (par + 1) * HD)
                    first = ch * 2 * GQ + par * GQ
                    ins = dve.tensor_copy(q64[:].rearrange("p (s h) -> p s h", s=DEC)[:, :, first:first + GQ],
                                          qk[half, ch * GQ:(ch + 1) * GQ, SAMPLE].rearrange("p g s -> p s g"))
            o(ins)
            dve.wait_ge(pe_order, 1)
            wcf = wc[:].rearrange("p a b -> p (a b)")
            do(dve.tensor_tensor(wcf, pcs[:, 0:CMP_S], c["own_mask"][:], ALU.add))
            do(dve.tensor_reduce(st[:, 0:1], wcf, AX_X, ALU.max))
            dve.tensor_scalar(wcf, wcf, st[:, 0:1], None, ALU.subtract).then_inc(shift_ready, 1)
            dve.wait_ge(act_order, 1)
            do(dve.reciprocal(st[:, 3:4], st[:, 2:3]))
            do(dve.tensor_tensor(st[:, 3:4], st[:, 3:4], gates_s[:, 0:1], ALU.mult))
            o(dve.tensor_scalar(wcf, wcf, st[:, 3:4], None, ALU.mult))
            dve.wait_ge(pe_order, 2)
            do(dve.tensor_copy(wct[0:DEC * NCS], pct[0:DEC * NCS]))
            for b in range(2):
                dve.wait_ge(pe_order, 3 + 4 * b)
                do(dve.tensor_reduce(st[:, 0:1], psc[:, 0:PAST + 1], AX_X, ALU.max))
                dve.tensor_scalar(st[:, 1:2], st[:, 0:1], -QK_SCALE, None, ALU.mult).then_inc(shift_ready, 1)
                dve.wait_ge(act_order, 2 + b)
                do(dve.reciprocal(st[:, 3:4], st[:, 2:3]))
                do(dve.tensor_tensor(st[:, 3:4], st[:, 3:4], gates_s[:, 1 + b:2 + b], ALU.mult))
                do(dve.tensor_scalar(w[:], w[:], st[:, 3:4], None, ALU.mult))
                o(dve.tensor_scalar(wn[:], c["own_seq"][:], w[:, PAST:PAST + 1], None, ALU.mult))
                dve.wait_ge(pe_order, 3 + 4 * b + 2)
                for g in range(PAGES):
                    dve.tensor_copy(pd[:, g, :].rearrange("p (s x) -> p s x", x=DIAG)[:, :, 0:HEADS],
                                    ptr[:, g, :].rearrange("p (s h) -> p s h", s=DEC))
                o(dve.tensor_copy(wnt[:], pn[:]))
            dve.wait_ge(pe_order, 11)
            do(dve.tensor_copy(osum[:], poc[:]))
            for kv in range(KV):
                ins = dve.scalar_tensor_tensor(out=osum[:], in0=po[:, kv * HD:(kv + 1) * HD],
                                               scalar=c["own_kv"][:, kv:kv + 1], in1=osum[:], op0=ALU.mult,
                                               op1=ALU.add)
                if kv < KV - 1:
                    do(ins)
            o(ins)
            dve.wait_ge(pe_order, 12)
            for ch in range(2):
                for par in range(2):
                    half = slice(par * HD, (par + 1) * HD)
                    first = ch * 2 * GQ + par * GQ
                    dve.tensor_copy(ot[half, ch * GQ:(ch + 1) * GQ, SAMPLE],
                                    pot[:].rearrange("p (s h) -> p h s", s=DEC)[:, first:first + GQ, :])


MC = D_MODEL // P
MD = D_MODEL // MEM_HEADS
HALVES = MD // P
MEM_SCALE = MD ** -0.5
MROWS = DEC * MEM_HEADS
MDIAG = MROWS + 1


def project_mem(nc, d, c, h, mem, mkv, qm, w):
    turns = 3 * MC // 2
    with ExitStack() as ctx:
        s = Stage(nc, ctx)
        pp = s.ps("mp_pp", [P, 2, 2, 512])
        evacuated, stored = s.sem("mp_evacuated"), s.sem("mp_stored")
        block = ctx.enter_context(nc.Block())

        @block.sync
        def _(sp):
            w.load(sp)
            sp.wait_ge(evacuated, 2 + 2 * MC)
            sp.dma_start(d["out_mem_v"], mkv[:, MC:2 * MC, :]).then_inc(stored, 16)
            sp.wait_ge(stored, 16)

        @block.gpsimd
        def _(pool):
            w.write_low(pool)

        @block.tensor
        def _(pe):
            for first, stop, x, parts in ((0, MC, mem, (slice(0, MEM),)), (MC, turns, h, HALF_PARTS)):
                with pe.Fori(first, stop) as i:
                    for u in range(2):
                        pe.wait_ge(evacuated, i * 2 + (u + 1))
                        w.multiply(pe, i, u, lambda n: pp[:, u, n, 0:parts[n].stop - parts[n].start], x, 0, parts)

        @block.scalar
        def _(act):
            w.write_first(act)

            def turn(i, last):
                for u in range(2):
                    w.write_ahead(act, i, u, last)

            tile_loop(act, 0, turns, turn)

        @block.vector
        def _(dve):
            dve.memset(qm[0:1, 0, 0:1], 0.0).then_inc(evacuated, 2)
            dve.wait_ge(evacuated, 2)
            with dve.Fori(0, MC) as i:
                for u in range(2):
                    w.finished(dve, i, u)
                    dve.tensor_copy(at(mkv, i * 2 + u), pp[:, u, 0, 0:MEM]).then_inc(evacuated, 1)
            with dve.Fori(MC, turns) as i:
                for u in range(2):
                    w.finished(dve, i, u)
                    dve.tensor_copy(halves(at(qm, (i - MC) * 2 + u)), pp[:, u, :, 0:HALF]).then_inc(evacuated, 1)


def norm_heads(nc, d, c, mkv, mv, qm):
    mk = mkv[:, 0:MC, :]
    with ExitStack() as ctx:
        s = Stage(nc, ctx)
        sq = s.sb("mn_sq", [P, 2, HALVES, COLS])
        r = s.sb("mn_r", [P, 2, COLS])
        pss = s.ps("mn_pss", [P, 2, 2, 512])
        pv = s.ps("mn_pv", [P, 2, 512])
        squared, summed, logged, scaled, normed = (s.sem("mn_" + x) for x in (
            "squared", "summed", "logged", "scaled", "normed"))
        stored, rows_done, rows_out = s.sem("mn_stored"), s.sem("mn_rows"), s.sem("mn_rows_out")
        block = ctx.enter_context(nc.Block())
        jobs = [(t, w, parts, hd * HALVES, gain) for t, w, parts, gain in (
            (mk, MEM, (slice(0, MEM),), c["mem_k_gain"]), (qm, COLS, HALF_PARTS, c["mem_q_gain"]))
            for hd in range(MEM_HEADS)]

        @block.scalar
        def _(act):
            act.preload_act_table_set("natural_log_exp_and_others")

            def square(j):
                t, w, parts, ch, gain = jobs[j]
                act.activation(sq[:, j % 2, :, 0:w], t[:, ch:ch + HALVES, :], ACT.Square).then_inc(squared, 1)

            square(0)
            for j, (t, w, parts, ch, gain) in enumerate(jobs):
                if j + 1 < len(jobs):
                    square(j + 1)
                act.wait_ge(summed, j + 1)
                if j >= 2:
                    act.wait_ge(normed, j - 1)
                n, m = len(parts), w // len(parts)
                act.activation(r[:, j % 2, 0:w].rearrange("p (a n) -> p a n", a=n), pss[:, j % 2, 0:n, 0:m], ACT.Ln,
                               scale=1.0 / MD, bias=c["eps"][:, 0:1]).then_inc(logged, 1)
                act.wait_ge(logged, j + 1)
                act.activation(r[:, j % 2, 0:w], r[:, j % 2, 0:w], ACT.Exp, scale=-0.5).then_inc(scaled, 1)

        @block.tensor
        def _(pe):
            for j, (t, w, parts, ch, gain) in enumerate(jobs):
                pe.wait_ge(squared, j + 1)
                if j >= 2:
                    pe.wait_ge(logged, j - 1)
                for n, part in enumerate(parts):
                    for k in range(HALVES):
                        mm = pe.matmul(pss[:, j % 2, n, 0:part.stop - part.start], c["ones"][:], sq[:, j % 2, k, part],
                                       start=k == 0, stop=k == HALVES - 1)
                mm.then_inc(summed, 1)
                if j < 2 * (MEM // P):
                    i, half = j // 2, j % 2
                    if j >= 2:
                        pe.wait_ge(rows_out, j - 1)
                    for k in range(4):
                        mm = pe.transpose(pv[:, j % 2, k * P:(k + 1) * P],
                                          mkv[:, MC + 4 * half + k, i * P:(i + 1) * P], c["ident"][:])
                    mm.then_inc(rows_done, 1)

        @block.vector
        def _(dve):
            for j, (t, w, parts, ch, gain) in enumerate(jobs):
                if j < 2 * (MEM // P):
                    dve.wait_ge(rows_done, j + 1)
                    dve.tensor_copy(mv[:, j // 2, (j % 2) * 512:(j % 2 + 1) * 512], pv[:, j % 2, :]).then_inc(rows_out, 1)
                dve.wait_ge(scaled, j + 1)
                for k in range(HALVES):
                    ins = dve.scalar_tensor_tensor(out=t[:, ch + k, :], in0=t[:, ch + k, :], scalar=gain[:, k:k + 1],
                                                   in1=r[:, j % 2, 0:w], op0=ALU.mult, op1=ALU.mult)
                ins.then_inc(normed, 1)

        @block.sync
        def _(sp):
            sp.wait_ge(normed, MEM_HEADS)
            sp.dma_start(d["out_mem_k"], mk).then_inc(stored, 16)
            sp.wait_ge(stored, 16)


def attend_prompt_mem(nc, d, c, qm, mk, mv, om):
    KB = MEM // P
    with ExitStack() as ctx:
        s = Stage(nc, ctx)
        w = s.sb("am_w", [P, 2, TT, MEM])
        wt = s.sb("am_wt", [P, KB, SEQ])
        mx, nb, den = (s.sb("am_" + x, [P, 2, TT]) for x in ("mx", "nb", "den"))
        psc = s.ps("am_psc", [P, 2, TT, MEM])
        pt = s.ps("am_pt", [P, KB, SEQ])
        po = s.ps("am_po", [P, HALVES, SEQ])
        scored, shifted, exped, weighted, turned, evacuated, summed, written, dve_order = (s.sem("am_" + x) for x in (
            "scored", "shifted", "exped", "weighted", "turned", "evacuated", "summed", "written", "dve"))
        block = ctx.enter_context(nc.Block())

        @block.tensor
        def _(pe):
            def scores(hd):
                ch = hd * HALVES
                if hd >= 2:
                    pe.wait_ge(exped, hd - 1)
                for i in range(TT):
                    for k in range(HALVES):
                        mm = pe.matmul(psc[:, hd % 2, i, :], qm[:, ch + k, i * P:(i + 1) * P], mk[:, ch + k, :],
                                       start=k == 0, stop=k == HALVES - 1)
                mm.then_inc(scored, 1)

            scores(0)
            for hd in range(MEM_HEADS):
                if hd + 1 < MEM_HEADS:
                    scores(hd + 1)
                pe.wait_ge(weighted, hd + 1)
                if hd:
                    pe.wait_ge(evacuated, hd)
                for kb in range(KB):
                    for i in range(TT):
                        mm = pe.transpose(pt[:, kb, i * P:(i + 1) * P], w[:, hd % 2, i, kb * P:(kb + 1) * P],
                                          c["ident"][:])
                mm.then_inc(turned, 1)
                pe.wait_ge(evacuated, hd + 1)
                if hd:
                    pe.wait_ge(written, hd)
                for k in range(HALVES):
                    for kb in range(KB):
                        mm = pe.matmul(po[:, k, :], mv[:, kb, hd * MD + k * P:hd * MD + (k + 1) * P], wt[:, kb, :],
                                       start=kb == 0, stop=kb == KB - 1)
                mm.then_inc(summed, 1)

        @block.vector
        def _(dve):
            o = Order(dve, dve_order)
            for hd in range(MEM_HEADS):
                u = hd % 2
                dve.wait_ge(scored, hd + 1)
                o(dve.tensor_reduce(mx[:, u], psc[:, u], AX_X, ALU.max))
                o.settle()
                dve.tensor_scalar(nb[:, u], mx[:, u], -MEM_SCALE, None, ALU.mult).then_inc(shifted, 1)
                dve.wait_ge(exped, hd + 1)
                o(dve.reciprocal(den[:, u], den[:, u]))
                o.settle()
                dve.tensor_tensor(w[:, u], w[:, u], den[:, u].unsqueeze(2).broadcast_to([P, TT, MEM]),
                                  ALU.mult).then_inc(weighted, 1)

        @block.scalar
        def _(act):
            act.preload_act_table(ACT.Exp)

            def exps(hd):
                u = hd % 2
                act.wait_ge(shifted, hd + 1)
                if hd >= 2:
                    act.wait_ge(turned, hd - 1)
                for i in range(TT):
                    ins = act.activation(w[:, u, i, :], psc[:, u, i, :], ACT.Exp, scale=MEM_SCALE,
                                         bias=nb[:, u, i:i + 1], accum_out=den[:, u, i:i + 1])
                ins.then_inc(exped, 1)

            exps(0)
            for hd in range(MEM_HEADS):
                if hd + 1 < MEM_HEADS:
                    exps(hd + 1)
                act.wait_ge(turned, hd + 1)
                if hd:
                    act.wait_ge(summed, hd)
                for kb in range(KB):
                    ins = act.copy(wt[:, kb, :], pt[:, kb, :])
                ins.then_inc(evacuated, 1)
                act.wait_ge(summed, hd + 1)
                for k in range(HALVES):
                    ins = act.copy(om[:, hd * HALVES + k, PROMPT], po[:, k, :])
                ins.then_inc(written, 1)


def attend_sample_mem(nc, d, c, qm, om, following):
    slots = 2
    with ExitStack() as ctx:
        s = Stage(nc, ctx)
        qd = s.sb("sm_qd", [P, HALVES, MROWS * MDIAG])
        wd = s.sb("sm_wd", [P, MEM // P, MROWS * MDIAG])
        ring = s.sb("sm_ring", [P, slots, MC, MEM])
        w = s.sb("sm_w", [MROWS, MEM])
        st = s.sb("sm_st", [MROWS, 4])
        orow = s.sb("sm_orow", [MROWS, MD])
        psc = s.ps("sm_psc", [MROWS, MEM])
        pt = s.ps("sm_pt", [P, MEM // P, MROWS])
        po = s.ps("sm_po", [MROWS, MD])
        pot = s.ps("sm_pot", [P, HALVES, MROWS])
        landed = [s.sem(f"sm_landed{u}") for u in range(slots)]
        used, pe_order, act_order, dve_order, zeroed = (s.sem("sm_" + x) for x in ("used", "pe", "act", "dve", "zeroed"))
        dve_steps, shift_ready = s.sem("sm_dve_steps"), s.sem("sm_shift_ready")
        block = ctx.enter_context(nc.Block())

        @block.gpsimd
        def _(pool):
            pool.memset(qd[:], 0.0).then_inc(zeroed, 1)
            pool.memset(wd[:], 0.0).then_inc(zeroed, 1)

        @block.sync
        def _(sp):
            for u in range(slots):
                sp.dma_start(ring[:, u], d["mem_kv"][u]).then_inc(landed[u], 16)
            with sp.Fori(0, 2 * DEC // slots - 1) as i:
                for u in range(slots):
                    sp.wait_ge(used, i * slots + (u + 1))
                    sp.dma_start(ring[:, u], d["mem_kv"][bass.ds(i * slots + (u + slots), 1)].rearrange(
                        "a p k n -> (a p) k n")).then_inc(landed[u], 16)

        @block.tensor
        def _(pe):
            ident = c["ident"]

            def rows(t, n, r):
                return t[:, n, 0:MROWS * MROWS].rearrange("p (a b) -> p a b", a=MROWS)[:, r, :]

            pe.wait_ge(act_order, 1)
            for q in range(DEC):
                pe.wait_ge(landed[q % slots], 16 * (q // slots + 1))
                for hd in range(MEM_HEADS):
                    for k in range(HALVES):
                        mm = pe.matmul(psc[:], rows(qd, k, q * MEM_HEADS + hd), ring[:, q % slots, hd * HALVES + k, :],
                                       start=q == 0 and hd == 0 and k == 0,
                                       stop=q == DEC - 1 and hd == MEM_HEADS - 1 and k == HALVES - 1)
                mm.then_inc(used, 1)
            pe.wait_ge(dve_order, 1)
            for g in range(MEM // P):
                mm = pe.transpose(pt[:, g, :], w[:, g * P:(g + 1) * P], ident[0:MROWS, 0:MROWS])
            mm.then_inc(pe_order, 1)
            pe.wait_ge(act_order, 3)
            for q in range(DEC):
                pe.wait_ge(landed[q % slots], 16 * (DEC // slots + q // slots + 1))
                vq = ring[:, q % slots].rearrange("p (g h) n -> p g h n", g=MEM // P)
                for hd in range(MEM_HEADS):
                    for g in range(MEM // P):
                        mm = pe.matmul(po[:], rows(wd, g, q * MEM_HEADS + hd), vq[:, g, hd, :],
                                       start=q == 0 and hd == 0 and g == 0,
                                       stop=q == DEC - 1 and hd == MEM_HEADS - 1 and g == MEM // P - 1)
                mm.then_inc(used, 1)
            pe.wait_ge(dve_order, 2)
            for k in range(HALVES):
                mm = pe.transpose(pot[:, k, :], orow[:, k * P:(k + 1) * P], ident[0:MROWS, 0:MROWS])
            mm.then_inc(pe_order, 1)

        @block.scalar
        def _(act):
            act.preload_act_table(ACT.Exp)
            act.wait_ge(zeroed, 2)
            for k in range(HALVES):
                dst = qd[:, k, :].rearrange("p (s h x) -> p s h x", s=DEC, h=MEM_HEADS)[:, :, :, 0]
                src = qm[:].rearrange("p (h k) n -> p k h n", k=HALVES)[:, k, :, SAMPLE].rearrange("p h s -> p s h")
                ins = act.copy(dst, src)
            ins.then_inc(act_order, 1)
            act.wait_ge(shift_ready, 1)
            act.activation(w[:], psc[:], ACT.Exp, scale=MEM_SCALE, bias=st[:, 1:2],
                           accum_out=st[:, 2:3]).then_inc(act_order, 1)
            act.wait_ge(pe_order, 1)
            for g in range(MEM // P):
                ins = act.copy(wd[:, g, :].rearrange("p (r x) -> p r x", x=MDIAG)[:, :, 0], pt[:, g, :])
            ins.then_inc(act_order, 1)
            following.write_first_ahead(act)

        @block.vector
        def _(dve):
            o = Order(dve, dve_steps)

            def do(ins):
                o(ins)
                o.settle()

            dve.wait_ge(used, DEC)
            do(dve.tensor_reduce(st[:, 0:1], psc[:], AX_X, ALU.max))
            dve.tensor_scalar(st[:, 1:2], st[:, 0:1], -MEM_SCALE, None, ALU.mult).then_inc(shift_ready, 1)
            dve.wait_ge(act_order, 2)
            do(dve.reciprocal(st[:, 3:4], st[:, 2:3]))
            dve.tensor_scalar(w[:], w[:], st[:, 3:4], None, ALU.mult).then_inc(dve_order, 1)
            dve.wait_ge(used, 2 * DEC)
            dve.tensor_copy(orow[:], po[:]).then_inc(dve_order, 1)
            dve.wait_ge(pe_order, 2)
            for k in range(HALVES):
                dve.tensor_copy(om[:].rearrange("p (h k) n -> p k h n", k=HALVES)[:, k, :, SAMPLE],
                                pot[:, k, :].rearrange("p (s h) -> p h s", s=DEC))

        following.begin(block)


def project_add(nc, d, c, name, w, kin, src, dst, again, out):
    with ExitStack() as ctx:
        s = Stage(nc, ctx)
        whole = len(src.shape) == 3
        x = s.sb(name + "_split", [P, 2, kin, COLS], F32R) if whole else src
        credit = s.sb(name + "_credit", [1, 1])
        pp = s.ps(name + "_pp", [P, 2, 2, 512])
        evacuated, stored, high, low, loaded = (s.sem(name + v) for v in (
            "_evacuated", "_stored", "_src_high", "_src_low", "_loaded"))
        block = ctx.enter_context(nc.Block())

        @block.sync
        def _(sp):
            if whole:
                sp.wait_ge(low, kin)
                sp.dma_start(dst[:], again).then_inc(loaded, 16)
            w.load(sp)
            if out is not None:
                sp.wait_ge(evacuated, 2 + KC)
                sp.dma_start(out, dst[:]).then_inc(stored, 16)
                sp.wait_ge(stored, 16)

        @block.gpsimd
        def _(pool):
            w.write_low(pool)

        @block.tensor
        def _(pe):
            if whole:
                pe.wait_ge(low, kin)
            with pe.Fori(0, KC // 2) as i:
                for u in range(2):
                    pe.wait_ge(evacuated, i * 2 + (u + 1))
                    for j in range(w.per):
                        w.multiply(pe, i, u * w.per + j, lambda n: pp[:, u, n, 0:HALF], x, j * KC, HALF_PARTS,
                                   start=j == 0, stop=j == w.per - 1)

        @block.scalar
        def _(act):
            w.write_first(act)
            if whole:
                high_of(act, src, x, kin, high)

            def turn(i, last):
                for u in range(2):
                    w.write_ahead(act, i, u, last)

            tile_loop(act, 0, KC // 2, turn)

        @block.vector
        def _(dve):
            dve.memset(credit[:], 0.0).then_inc(evacuated, 2)
            dve.wait_ge(evacuated, 2)
            if whole:
                low_of(dve, src, x, kin, high, low)
                dve.wait_ge(loaded, 16)
            with dve.Fori(0, KC // 2) as i:
                for u in range(2):
                    t = i * 2 + u
                    w.finished(dve, i, u)
                    dve.tensor_tensor(halves(at(dst, t)), pp[:, u, :, 0:HALF], halves(at(dst, t)),
                                      ALU.add).then_inc(evacuated, 1)


def expand_ffn(nc, d, c, h, act_t, w, following):
    with ExitStack() as ctx:
        s = Stage(nc, ctx)
        pad = s.sb("up_pad", [P, 2, 2, FCONV - 1 + COLS])
        acc = s.sb("up_acc", [P, 2, 2, COLS])
        prod = s.sb("up_prod", [P, 2, 2, DEC, FCONV])
        sil = s.sb("up_sil", [P, 2, COLS])
        tails = s.sb("up_tails", [P, FC, 2, FCONV - 1])
        conv_s = s.sb("up_conv_s", [P, FC, 2, DEC * FCONV])
        pp = s.ps("up_pp", [P, 2, 2, 2, 512])
        evacuated, convolved, silued, dve_order, state_landed, stored, made, high, low = (s.sem("up_" + x) for x in (
            "evacuated", "convolved", "silued", "dve", "state_landed", "stored", "made", "out_high", "out_low"))
        PER_HALF = 1 + 1 + (FCONV - 1) + 1 + 1 + 1
        TILE = 2 * PER_HALF - 1
        block = ctx.enter_context(nc.Block())

        @block.sync
        def _(sp):
            sp.dma_start(conv_s[:], d["ffn_state"]).then_inc(state_landed, 16)
            w.load(sp)

        @block.gpsimd
        def _(pool):
            w.write_low(pool)

        @block.tensor
        def _(pe):
            with pe.Fori(0, FC // 2) as i:
                for u in range(2):
                    pe.wait_ge(evacuated, i * 2 + (u + 1))
                    for m in range(2):
                        w.multiply(pe, i, 2 * u + m, lambda n: pp[:, u, m, n, 0:HALF], h, 0, HALF_PARTS)

        @block.scalar
        def _(act):
            act.preload_act_table(ACT.Silu)
            w.write_first(act)
            act.wait_ge(state_landed, 16)

            def join(t, u):
                act.wait_ge(convolved, t + 3)
                act.activation(sil[:, u, :], acc[:, u, 0, :], ACT.Silu).then_inc(silued, 1)
                act.wait_ge(made, t + 1)
                act.copy(act_t[:, 0, bass.ds(t, 1), :].rearrange("p a n -> p (a n)"), sil[:, u, :]).then_inc(high, 1)

            def turn(i, last, first=False):
                for u in range(2):
                    t = i * 2 + u
                    w.write_ahead(act, i, u, last)
                    w.finished(act, i, u)
                    act.wait_ge(convolved, t + 1)
                    for m in range(2):
                        act.copy(halves(pad[:, u, m, FCONV - 1:]), pp[:, u, m, :, 0:HALF])
                    act.copy(conv_s[:, bass.ds(t, 1), :, :].rearrange("p a m (s k) -> p (a m) s k", k=FCONV)[
                        :, :, :, FCONV - 1], pp[:, u, :, 1, HALF - DEC:HALF]).then_inc(evacuated, 1)
                    if not (first and u == 0):
                        join(t - 1, 1 - u)

            turn(0, False, first=True)
            tile_loop(act, 1, FC // 2, turn)
            following.write_first_ahead(act, w)
            join(FC - 1, 1)

        @block.vector
        def _(dve):
            o = Order(dve, dve_order)
            dve.memset(pad[:, :, :, 0:FCONV - 1], 0.0).then_inc(evacuated, 2)
            dve.memset(acc[:], 0.0).then_inc(convolved, 2)
            dve.wait_ge(convolved, 2)
            def product(t, u):
                dve.wait_ge(silued, t + 1)
                dve.tensor_tensor(sil[:, u, :], sil[:, u, :], acc[:, u, 1, :], ALU.mult).then_inc(made, 1)

            def write_lo(t, u):
                dve.wait_ge(high, t + 1)
                hi, lo = (act_t[:, n, bass.ds(t, 1), :].rearrange("p a n -> p (a n)") for n in range(2))
                dve.tensor_tensor(lo, sil[:, u, :], hi.bitcast(F32), ALU.subtract).then_inc(low, 1)

            def convolve(t, u):
                dve.wait_ge(evacuated, t + 3)
                wt = at(c["ffn_conv_w"], t)
                cs = conv_s[:, bass.ds(t, 1), :, :].rearrange("p a m (s k) -> p (a m) s k", k=FCONV)
                for m in range(2):
                    tap = lambda k: wt[:, m * (FCONV + 1) + k:m * (FCONV + 1) + k + 1]
                    taps = wt[:, m * (FCONV + 1):m * (FCONV + 1) + FCONV]
                    o(dve.tensor_scalar(acc[:, u, m, PROMPT], pad[:, u, m, 0:SEQ], tap(0), tap(FCONV), ALU.mult,
                                        ALU.add))
                    o(dve.tensor_tensor(prod[:, u, m], cs[:, m], taps.unsqueeze(1).broadcast_to([P, DEC, FCONV]),
                                        ALU.mult))
                    for k in range(1, FCONV):
                        o.settle()
                        o(dve.scalar_tensor_tensor(out=acc[:, u, m, PROMPT], in0=pad[:, u, m, k:k + SEQ],
                                                   scalar=tap(k), in1=acc[:, u, m, PROMPT], op0=ALU.mult,
                                                   op1=ALU.add))
                    o(dve.tensor_reduce(acc[:, u, m, SAMPLE], prod[:, u, m], AX_X, ALU.add))
                    o(dve.tensor_copy(tails[:, bass.ds(t, 1), m, :].rearrange("p a k -> p (a k)"),
                                      pad[:, u, m, SEQ:SEQ + FCONV - 1]))
                    o.settle()
                    ins = dve.tensor_scalar(acc[:, u, m, SAMPLE], acc[:, u, m, SAMPLE], tap(FCONV), None, ALU.add)
                    if m == 0:
                        o(ins)
                    else:
                        ins.then_inc(convolved, 1)

            convolve(0, 0)
            product(0, 0)
            convolve(1, 1)
            write_lo(0, 0)
            with dve.Fori(1, FC // 2) as i:
                o.enter(i, 2 * TILE, 1)
                for u in range(2):
                    product(i * 2 + u - 1, 1 - u)
                    convolve(i * 2 + u, u)
                    write_lo(i * 2 + u - 1, 1 - u)
                o.leave(FC // 2)
            product(FC - 1, 1)
            write_lo(FC - 1, 1)

        following.begin(block, w)

        @block.sync
        def _(sp):
            sp.wait_ge(low, FC)
            sp.dma_start(d["out_p_ffn"], tails[:]).then_inc(stored, 16)
            sp.dma_start(d["out_s_ffn"], conv_s[:]).then_inc(stored, 16)
            sp.wait_ge(stored, 32)


def copy_windows(nc, d):
    with ExitStack() as ctx:
        s = Stage(nc, ctx)
        stored = s.sem("cw_stored")
        block = ctx.enter_context(nc.Block())

        @block.sync
        def _(sp):
            sp.dma_start(d["out_win_k"], d["win_k_rows"]).then_inc(stored, 16)
            sp.dma_start(d["out_win_v"], d["win_v_rows"]).then_inc(stored, 16)
            sp.wait_ge(stored, 32)


CONSTANTS = {
    "ident": [P, P], "ones": [P, P], "head_ones": [P, P], "rotate": [P, P], "tri": [P, P], "ssd_mask": [P, P],
    "causal": [P, P], "ident2": [2 * SSD_HEADS, SSD_HEADS], "own_seq": [P, DEC], "own_kv": [P, KV], "eps": [P, 1],
    "norm_mix": [P, KC], "norm_ffn": [P, KC], "mem_norm": [P, KC], "b_merge": [P, 3 * KC],
    "ssd_conv_w": [P, XBC, CONV], "ssd_conv_b": [P, XBC], "ssd_dt_bias": [SSD_HEADS, 1], "ssd_a_log": [SSD_HEADS, 1],
    "ssd_d": [P, DI], "ssd_norm": [P, DI], "head_gain": [P, NR], "cmp_gain": [P, 1],
    "mem_k_gain": [P, HALVES], "mem_q_gain": [P, HALVES], "ffn_conv_w": [P, FC, 2 * (FCONV + 1)],
}

NSA_CONSTANTS = {
    "cmp_mask": [P, TT, NCP], "cos": [P, COLS], "sin": [P, COLS], "own_mask": [P, CMP_S],
    "cmp_cos": [P, CMP_P + CMP_S], "cmp_sin": [P, CMP_P + CMP_S],
}

OUTPUTS = {
    "out_y": [P, KC, COLS], "out_cmp": [P, 4, COLS], "out_v": [P, 4, COLS],
    "out_k": [P, KV, COLS], "out_p_conv": [P, XBC, CONV - 1], "out_s_conv": [P, XBC, DEC, CONV],
    "out_p_ssd": [P, GROUPS, HPG * HEAD_P], "out_s_ssd": [DEC, P, DI, STATE],
    "out_p_ffn": [P, FC, 2, FCONV - 1], "out_s_ffn": [P, FC, 2, DEC * FCONV],
    "out_mem_k": [P, MC, MEM], "out_mem_v": [P, MC, MEM],
    "out_win_k": [DEC, PAST * KV * HD], "out_win_v": [DEC, PAST * KV * HD],
}


def load_columns(nc, name, pairs):
    with ExitStack() as ctx:
        s = Stage(nc, ctx)
        landed = s.sem(name + "_landed")
        block = ctx.enter_context(nc.Block())

        @block.sync
        def _(sp):
            for dst, src in pairs:
                sp.dma_start(dst[:], src).then_inc(landed, 16)
            sp.wait_ge(landed, 16 * len(pairs))


def build_layer(nc, d):
    both = (PROMPT, SAMPLE)
    Stage.taken.clear()
    with ExitStack() as whole:
        top = Stage(nc, whole)
        c = {n: top.sb("c_" + n, shape) for n, shape in CONSTANTS.items()}
        h = top.sb("h", [P, 2, KC, COLS], F32R)
        mixed, gates_raw = top.sb("mixed", [P, KC, COLS]), top.sb("gates_raw", [3 * HEADS, COLS])
        load_constants(nc, d, c)
        with ExitStack() as ctx:
            s = Stage(nc, ctx)
            zt, r = s.sb("zt", [P, DI, COLS]), s.sb("zr", [P, COLS])
            with ExitStack() as inner:
                s = Stage(nc, inner)
                xbct = s.sb("xbct", [P, XBC, COLS])
                dt_raw = s.sb("dt_raw", [SSD_HEADS, COLS])
                ec, wend, cdec, negcum, dtr = (s.sb("t_" + n, [P, TT, SSD_HEADS]) for n in (
                    "ec", "wend", "cdec", "negcum", "dtr"))
                cumt = s.sb("cumt", [2 * SSD_HEADS, SEQ], F32R)
                dxs = s.sb("dxs", [P, DI, 2, DEC])
                with ExitStack() as rings:
                    w = SplitWeights(Stage(nc, rings), "ssd", d["w_ssd"], raw=raw_slots(mixed))
                    with ExitStack() as first:
                        x = Stage(nc, first).sb("x", [P, KC, COLS])
                        load_columns(nc, "x", [(x, d["x"])])
                        norm_columns(nc, "nx", x, h, c["norm_mix"], c["ones"], c["eps"], KC, both, COLS, w)
                    project_ssd(nc, d, c, h, zt, xbct, dt_raw, gates_raw, w)
                step_sizes(nc, d, c, dt_raw, ec, wend, cdec, negcum, dtr, cumt, dxs)
                scan(nc, d, c, xbct, zt, dxs, dtr, ec, wend, cdec, negcum, cumt, mixed)
            w = SplitWeights(Stage(nc, ctx), "ms", d["w_ssd_merge"])
            split = Stage(nc, ctx).sb("z_split", [P, 2, DI, COLS], F32R)
            gain_and_square(nc, c, zt, split, r, w)
            merge_branch(nc, d, c, "ms", 0, w, split, DI, h, mixed, r)

        with ExitStack() as ctx:
            s = Stage(nc, ctx)
            ot = s.sb("ot", [P, KC, COLS])
            with ExitStack() as inner:
                s = Stage(nc, inner)
                nsa = {n: s.sb("c_" + n, shape) for n, shape in NSA_CONSTANTS.items()}
                qk = s.sb("qk", [P, SV, COLS])
                vr = s.sb("vr", [P, TT + 1, 2 * KV * HD])
                gates, gates_s = s.sb("gates", [P, TT, 3 * HEADS]), s.sb("gates_s", [ROWS, 3])
                kct, vcp, vcs = s.sb("kct", [P, CMP_P + CMP_S]), s.sb("vcp", [P, KV, HD]), s.sb("vcs", [P, KV, HD])
                load_columns(nc, "nsa_consts", [(t, d[n]) for n, t in nsa.items()])
                c.update(nsa)
                with ExitStack() as rows:
                    vt = Stage(nc, rows).sb("vt", [P, 4, COLS])
                    project_nsa(nc, d, c, h, qk, vt)
                    turn_rows(nc, d, c, vt, gates_raw, vr, gates, gates_s)
                compress_rows(nc, d, c, qk, kct, vcp, vcs)
                attend_prompt(nc, d, c, qk, vr, gates, kct, vcp, ot)
                attend_sample_nsa(nc, d, c, qk, vr, gates_s, kct, vcs, ot)
            Stage.retire_semaphores(nc)
            w = SplitWeights(Stage(nc, ctx), "mn", d["w_nsa_merge"])
            merge_branch(nc, d, c, "mn", 1, w, ot, KC, h, mixed, None)

        with ExitStack() as late:
            w_out = SplitWeights(Stage(nc, late), "po", d["w_out"])
            with ExitStack() as ctx:
                s = Stage(nc, ctx)
                om = s.sb("om", [P, KC, COLS])
                w_merge = SplitWeights(s, "mm", d["w_mem_merge"])
                with ExitStack() as inner:
                    s = Stage(nc, inner)
                    mkv, mv = s.sb("mkv", [P, 2 * MC, MEM]), s.sb("mv", [P, MEM // P, D_MODEL])
                    qm = s.sb("qm", [P, MC, COLS])
                    with ExitStack() as first:
                        s = Stage(nc, first)
                        mem, mem_split = s.sb("mem", [P, KC, MEM]), s.sb("mem_split", [P, 2, KC, MEM], F32R)
                        w = SplitWeights(s, "mp", d["w_mkv_qm"], rings_of=w_merge)
                        load_columns(nc, "mem", [(mem, d["mem"])])
                        norm_columns(nc, "nm", mem, mem_split, c["mem_norm"], c["ones"], c["eps"], KC,
                                     (slice(0, MEM),), MEM, w)
                        project_mem(nc, d, c, h, mem_split, mkv, qm, w)
                    norm_heads(nc, d, c, mkv, mv, qm)
                    attend_prompt_mem(nc, d, c, qm, mkv, mv, om)
                    attend_sample_mem(nc, d, c, qm, om, w_merge)
                merge_branch(nc, d, c, "mm", 2, w_merge, om, KC, h, mixed, None, w_out)

            x = mixed
            project_add(nc, d, c, "po", w_out, KC, mixed, x, d["x"], None)
            Stage.retire_semaphores(nc)
            act_t = Stage(nc, late).sb("act_t", [P, 2, FC, COLS], F32R)
            w_up = SplitWeights(Stage(nc, late), "up", d["w_up"], rings_of=w_out)
            norm_columns(nc, "nf", x, h, c["norm_ffn"], c["ones"], c["eps"], KC, both, COLS, w_up)
            w_down = SplitWeights(Stage(nc, late), "pd", d["w_down"], rings_of=w_out)
            expand_ffn(nc, d, c, h, act_t, w_up, w_down)
            project_add(nc, d, c, "pd", w_down, FC, act_t, x, None, d["out_y"])
        copy_windows(nc, d)


def tiles(w):
    k, m = w.shape
    return w.reshape(k // P, P, m // P, P).transpose(2, 1, 0, 3)


def columns(v):
    return v.reshape(-1, P).T


def constants():
    f = np.float32
    i = np.arange(P)
    pos = np.concatenate([np.arange(SEQ), np.full(DEC, PAST)]).astype(f)
    inv = (f(10000.0) ** (-np.arange(HD // 2, dtype=f) / f(HD // 2))).astype(f)
    of_row = inv[i % (HD // 2)][:, None]
    cmp_pos = np.concatenate([np.tile(np.arange(NCP), KV), np.tile(np.arange(NCS), KV * DEC)]) * CMP_STRIDE + CMP_LEN - 1
    ang, cang = of_row * pos[None, :], of_row * cmp_pos.astype(f)[None, :]
    rotate = np.zeros((P, P), f)
    for m in range(P):
        if m % HD < HD // 2:
            rotate[m + HD // 2, m] = -1
        else:
            rotate[m - HD // 2, m] = 1
    t = np.arange(SEQ).reshape(TT, P).T[:, :, None]
    end = np.arange(NCP) * CMP_STRIDE + CMP_LEN - 1
    sq, hd = np.divmod(np.arange(ROWS), HEADS)
    own = (sq[:, None, None] == np.arange(DEC)[None, None, :]) & (hd[:, None, None] // GQ == np.arange(KV)[None, :, None])
    return {
        "ident": np.eye(P, dtype=f), "ident2": np.tile(np.eye(SSD_HEADS, dtype=f), (2, 1)), "ones": np.ones((P, P), f),
        "head_ones": (i[:, None] // HD == i[None, :] // HD).astype(f), "rotate": rotate,
        "tri": (i[:, None] <= i[None, :]).astype(f),
        "ssd_mask": np.where(i[:, None] <= i[None, :], 0, NEG).astype(f),
        "causal": np.where(i[None, :] <= i[:, None], 0, NEG).astype(f),
        "cmp_mask": np.where(end[None, None, :] <= t, 0, NEG).astype(f),
        "cos": np.cos(ang).astype(f), "sin": np.sin(ang).astype(f),
        "cmp_cos": np.cos(cang).astype(f), "cmp_sin": np.sin(cang).astype(f),
        "expand": (np.arange(SSD_HEADS)[:, None] == np.arange(D_INNER)[None, :] // HEAD_P).astype(f),
        "own_mask": np.repeat(np.where(own, 0, NEG).astype(f).reshape(ROWS, -1), NCS, axis=1),
        "own_seq": (sq[:, None] == np.arange(DEC)[None, :]).astype(f),
        "own_kv": (hd[:, None] // GQ == np.arange(KV)[None, :]).astype(f),
        "eps": np.full((P, 1), EPS, f),
    }


def by_pair(pool):
    lead = pool.shape[:-3]
    n = len(lead)
    a = pool.reshape(lead + (pool.shape[-3], KV // 2, 2, HD))
    a = a.transpose(tuple(range(n)) + (n + 2, n + 3, n + 1, n))
    return a.reshape(lead + (P, KV // 2, pool.shape[-3]))


def lay_out(v):
    f = {n: np.asarray(a)[0] if np.asarray(a).ndim and n not in (
        "x_prompt", "x_sample", "page_table", "mem_prompt") else np.asarray(a) for n, a in v.items()}
    cut = np.cumsum([D_INNER, XBC * P, SSD_HEADS, HEADS * HD, 6 * KV * HD, 3 * HEADS, D_MODEL])
    wz, wxbc, wdt, wq, wkv, wg, wqm, wm = np.split(f["w_in"], cut, axis=1)
    order = [2 * GQ * ch + GQ * par + g for ch in range(2) for g in range(GQ) for par in range(2)]
    wq = wq.reshape(D_MODEL, HEADS, HD)[:, order].reshape(D_MODEL, HEADS * HD)
    w_nsa_o = f["w_nsa_o"].reshape(HEADS, HD, D_MODEL)[order].reshape(HEADS * HD, D_MODEL)
    ck, cv, sk, sv, wk, wv = np.split(wkv, 6, axis=1)
    first = np.zeros((D_MODEL, 2 * P), np.float32)
    first[:, :SSD_HEADS], first[:, P:P + 3 * HEADS] = wdt, wg
    merge = [wm[:, n * D_MODEL:(n + 1) * D_MODEL] for n in range(3)]
    mem_k = f["cache_mem_k"].reshape(DEC, MEM, MC, P).transpose(0, 3, 2, 1)
    mem_v = f["cache_mem_v"].reshape(DEC, MEM // P, P, MEM_HEADS, MD).transpose(0, 2, 1, 3, 4).reshape(DEC, P, MC, MEM)
    state = f["state_ssd"].reshape(DEC, DI, 2, HEAD_P, STATE).transpose(0, 2, 3, 1, 4).reshape(DEC, P, DI, STATE)
    conv = np.zeros((P, XBC, DEC, CONV), np.float32)
    conv[..., :CONV - 1] = f["state_ssd_conv"].reshape(DEC, CONV - 1, XBC, P).transpose(3, 2, 0, 1)
    ffn = np.zeros((P, FC, 2, DEC, FCONV), np.float32)
    ffn[..., :FCONV - 1] = f["state_ffn_conv"].reshape(DEC, FCONV - 1, 2, FC, P).transpose(4, 3, 2, 0, 1)
    taps = np.concatenate([f["ffn_conv_w"], f["ffn_conv_b"][None]]).reshape(FCONV + 1, 2, FC, P).transpose(3, 2, 1, 0)
    q_gain, k_gain = f["nsa_q_norm"], f["nsa_k_norm"]
    win_k, win_v = f["state_nsa_win_k"], f["state_nsa_win_v"]
    pe = [f["cmp_k_pe"], f["cmp_v_pe"]]
    a = {
        "x": np.concatenate([f["x_prompt"][0], f["x_sample"][:, 0]]).T.reshape(KC, P, COLS).transpose(1, 0, 2),
        "mem": f["mem_prompt"][0].T.reshape(KC, P, MEM).transpose(1, 0, 2),
        "w_ssd": tiles(np.concatenate([first, wz, wxbc], axis=1)),
        "w_ssd_merge": np.concatenate([tiles(merge[0]), tiles(f["w_ssd_o"])], axis=2),
        "w_qk": tiles(np.concatenate([wq, sk, wk, ck, cv, sv, wv], axis=1)),
        "w_nsa_merge": np.concatenate([tiles(merge[1]), tiles(w_nsa_o)], axis=2),
        "w_mkv_qm": tiles(np.concatenate([f["w_mem_kv"], wqm], axis=1)),
        "w_mem_merge": np.concatenate([tiles(merge[2]), tiles(f["w_mem_o"])], axis=2),
        "w_out": tiles(f["w_out"]),
        "w_up": np.concatenate([tiles(f["w_up"][:, :D_FF]), tiles(f["w_up"][:, D_FF:])], axis=2),
        "w_down": tiles(f["w_down"]),
        "ssd_state": state, "ssd_state_conv": conv, "ffn_state": ffn.reshape(P, FC, 2, DEC * FCONV),
        "pool_cmp_k": f["cache_nsa_cmp_k"].transpose(0, 3, 2, 1), "pool_cmp_v": f["cache_nsa_cmp_v"].transpose(0, 3, 2, 1),
        "pool_sel_k": by_pair(f["cache_nsa_sel_k"]),
        "pool_sel_v": f["cache_nsa_sel_v"].reshape(-1, PAGE, KV * HD),
        "win_k": by_pair(win_k).transpose(1, 2, 0, 3),
        "win_v": win_v.reshape(DEC, PAGES, P, KV * HD).transpose(2, 0, 1, 3),
        "win_k_rows": win_k.reshape(DEC, -1), "win_v_rows": win_v.reshape(DEC, -1),
        "cmp_w1": np.stack([f[n].reshape(CMP_LEN // 2, P, P).transpose(1, 0, 2) for n in ("cmp_k_w1", "cmp_v_w1")], 1),
        "cmp_w2": np.stack([np.tile(f[n], (1, 2)) for n in ("cmp_k_w2", "cmp_v_w2")], 1),
        "cmp_pe": np.stack([p.reshape(CMP_LEN // 2, P).T for p in pe], 1),
        "page_table": f["page_table"].reshape(1, -1).astype(np.int32),
        "mem_kv": np.concatenate([mem_k, mem_v]),
        "norm_mix": columns(f["norm_mix"]), "norm_ffn": columns(f["norm_ffn"]), "mem_norm": columns(f["mem_norm"]),
        "b_merge": columns(f["b_merge"].reshape(-1)),
        "ssd_conv_w": f["ssd_conv_w"].reshape(CONV, XBC, P).transpose(2, 1, 0), "ssd_conv_b": columns(f["ssd_conv_b"]),
        "ssd_dt_bias": f["ssd_dt_bias"][:, None], "ssd_a_log": f["ssd_a_log"][:, None],
        "ssd_d": columns(np.repeat(f["ssd_d"], HEAD_P)), "ssd_norm": columns(f["ssd_norm"]),
        "head_gain": np.stack([np.tile(g, 2) for g in [q_gain] * NQ + [k_gain[1]] * 2 + [k_gain[2]] * 2], 1),
        "cmp_gain": np.tile(k_gain[0], 2)[:, None],
        "mem_k_gain": columns(f["mem_k_norm"]), "mem_q_gain": columns(f["mem_q_norm"]),
        "ffn_conv_w": taps.reshape(P, FC, 2 * (FCONV + 1)),
    }
    a.update(constants())
    return {n: np.ascontiguousarray(x) for n, x in a.items()}


def channels(a):
    return a.transpose(2, 1, 0).reshape(a.shape[2], -1)


def rows_by_kv(a):
    return a.reshape(2, HD, KV // 2, -1).transpose(3, 2, 0, 1).reshape(-1, KV, HD)


def take_apart(o):
    y = channels(o["out_y"])
    cmp_k, cmp_v = rows_by_kv(o["out_cmp"][:, 0:2]), rows_by_kv(o["out_cmp"][:, 2:4])
    sel_k, win_k = rows_by_kv(o["out_k"][:, 0:2]), rows_by_kv(o["out_k"][:, 2:4])
    v = channels(o["out_v"]).reshape(COLS, 2, KV, HD)
    v, v_s = v[:SEQ], v[SEQ:]
    p_conv = channels(o["out_p_conv"])
    s_conv = o["out_s_conv"][..., 1:].transpose(2, 3, 1, 0).reshape(DEC, CONV - 1, XBC * P)
    p_ssd = o["out_p_ssd"].reshape(STATE, GROUPS * HPG, HEAD_P).transpose(1, 2, 0)
    s_ssd = o["out_s_ssd"].reshape(DEC, 2, HEAD_P, DI, STATE).transpose(0, 3, 1, 2, 4).reshape(
        DEC, SSD_HEADS, HEAD_P, STATE)
    p_ffn = o["out_p_ffn"].transpose(3, 2, 1, 0).reshape(FCONV - 1, 2 * D_FF)
    s_ffn = o["out_s_ffn"].reshape(P, FC, 2, DEC, FCONV)[..., 1:].transpose(3, 4, 2, 1, 0).reshape(
        DEC, FCONV - 1, 2 * D_FF)
    mem_k = channels(o["out_mem_k"]).reshape(MEM, MEM_HEADS, MD)
    mem_v = channels(o["out_mem_v"]).reshape(MEM, MEM_HEADS, MD)
    s_win = [np.concatenate([o[n].reshape(DEC, PAST, KV, HD), new[:, None]], axis=1)
             for n, new in (("out_win_k", win_k[SEQ:]), ("out_win_v", v_s[:, 1]))]
    p = [cmp_k[:SEQ], cmp_v[:SEQ], sel_k[:SEQ], v[:, 0], win_k[:SEQ], v[:, 1], p_conv, p_ssd, p_ffn, mem_k, mem_v]
    s = [cmp_k[SEQ:][:, None], cmp_v[SEQ:][:, None], sel_k[SEQ:][:, None], v_s[:, 0][:, None], s_win[0], s_win[1],
         s_conv, s_ssd, s_ffn]
    return tuple([y[None, :SEQ], y[SEQ:, None]] + [a[None, None] for a in p] + [a[None] for a in s])


def build_program(nc, arrays):
    d = {n: nc.dram_tensor("in_" + n, a.shape, mybir.dt.from_np(a.dtype), kind="ExternalInput").ap()
         for n, a in arrays.items()}
    for n, shape in OUTPUTS.items():
        d[n] = nc.dram_tensor(n, shape, F32, kind="ExternalOutput").ap()
    d["gates_turn"] = nc.dram_tensor("gates_turn", [DEC, 3 * HEADS], F32, kind="Internal").ap()
    build_layer(nc, d)


def kernel(**inputs):
    import concourse.bacc as bacc
    from concourse.bass_utils import run_bass_kernel_spmd

    nc = bacc.Bacc("TRN2", target_bir_lowering=False, num_devices=1)
    arrays = lay_out(inputs)
    build_program(nc, arrays)
    r = run_bass_kernel_spmd(nc, [{"in_" + n: a for n, a in arrays.items()}], core_ids=[0])
    return take_apart({n: r.results[0][n] for n in OUTPUTS})
```
